# Optimizing a Trainium2 kernel written in Bass

```python
import jax, jax.numpy as jnp
from jax import lax
import numpy as np

D_MODEL = 1024
BATCH = 1
SEQ = 512
DEPTH = 1
DEC_BATCH = 1
DEC_SEQ = 64
PAST_LEN = 256

CHUNK = 64
D_MIX = D_MODEL
D_CONV = 3 * D_MIX // 8
CONV_WIDTH = 3
D_POOL = D_MIX // 4
POOL_WINDOWS = (2, 4, 8, 16)
N_POOL_GROUPS = 4
POOL_GROUP = D_POOL // N_POOL_GROUPS
POOL_HIST = max(POOL_WINDOWS) - 1
D_SGU = D_MIX - D_CONV - D_POOL
SGU_HEADS = 4
SGU_HEAD_DIM = D_SGU // SGU_HEADS
SGU_LEN = 128
D_PROJ = 3 * D_CONV + D_POOL + 2 * D_SGU
SPLIT_POINTS = (D_CONV, 2 * D_CONV, 3 * D_CONV, 3 * D_CONV + D_POOL, 3 * D_CONV + D_POOL + D_SGU)
N_GROUPS = 4
EXPERTS_PER_GROUP = 8
N_EXPERTS = N_GROUPS * EXPERTS_PER_GROUP
TOP_K_FINE = 2
D_EXPERT = D_MODEL // 2
EPS = 1e-6

kernel_name = 'hybrid_conv_pool_sgu_hiermoe_stream_step'

def rmsnorm(x, g):
    xf = x.astype(jnp.float32)
    y = xf * lax.rsqrt(jnp.mean(xf * xf, axis=-1, keepdims=True) + EPS)
    return (y * g.astype(jnp.float32)).astype(x.dtype)

def short_conv(z, hist, w):
    L = z.shape[1]
    zc = jnp.concatenate([hist.astype(z.dtype), z], axis=1)
    y = w[0] * zc[:, 0:L]
    for k in range(1, CONV_WIDTH):
        y = y + w[k] * zc[:, k:k + L]
    return y, zc[:, -(CONV_WIDTH - 1):]

def multiscale_pool(z, hist, pos0, w, scale):
    B, L, _ = z.shape
    zp = jnp.concatenate([hist.astype(z.dtype), z], axis=1)
    cs = jnp.pad(jnp.cumsum(zp.astype(jnp.float32), axis=1), ((0, 0), (1, 0), (0, 0)))
    end = cs[:, POOL_HIST + 1:POOL_HIST + 1 + L]
    pos = pos0 + jnp.arange(L)
    means = []
    for g, win in enumerate(POOL_WINDOWS):
        sl = slice(g * POOL_GROUP, (g + 1) * POOL_GROUP)
        start = cs[:, POOL_HIST + 1 - win:POOL_HIST + 1 - win + L, sl]
        cnt = jnp.minimum(win, pos + 1).astype(jnp.float32)[None, :, None]
        means.append((end[..., sl] - start) / cnt)
    pooled = (jnp.concatenate(means, axis=-1) - z.astype(jnp.float32)).astype(z.dtype)
    pooled = pooled.reshape(B, L, N_POOL_GROUPS, POOL_GROUP)
    y = jnp.einsum('blgc,gcd->blgd', pooled, w).reshape(B, L, D_POOL) * scale
    return y, zp[:, -POOL_HIST:]

def spatial_gating(u, v, w_s, b_s):
    B, L, _ = v.shape
    pad = (-L) % SGU_LEN
    n = (L + pad) // SGU_LEN
    vp = jnp.pad(v, ((0, 0), (0, pad), (0, 0))).reshape(B, n, SGU_LEN, SGU_HEADS, SGU_HEAD_DIM)
    mask = jnp.tril(jnp.ones((SGU_LEN, SGU_LEN), dtype=bool))
    wm = jnp.where(mask[None], w_s, jnp.zeros_like(w_s))
    s = jnp.einsum('hij,bnjhc->bnihc', wm, vp) + b_s.T[None, None, :, :, None]
    s = s.reshape(B, n * SGU_LEN, D_SGU)[:, :L]
    return u * s

def hier_moe(x, rc_w, rc_b, rf_w, rf_b, w_gate, w_up, w_down):
    B, L, D = x.shape
    t = x.reshape(-1, D)
    lc = jnp.dot(t, rc_w).astype(jnp.float32) + rc_b.astype(jnp.float32)
    pc = jax.nn.softmax(lc, axis=-1)
    g_sel = jnp.argmax(lc, axis=-1)
    p_sel = jnp.take_along_axis(pc, g_sel[:, None], axis=-1)[:, 0]
    lf = (jnp.dot(t, rf_w).astype(jnp.float32) + rf_b.astype(jnp.float32)).reshape(-1, N_GROUPS, EXPERTS_PER_GROUP)
    lf_sel = jnp.take_along_axis(lf, g_sel[:, None, None], axis=1)[:, 0]
    top_v, top_i = lax.top_k(lf_sel, TOP_K_FINE)
    top_w = jax.nn.softmax(top_v, axis=-1)
    fine = jnp.einsum('tk,tke->te', top_w, jax.nn.one_hot(top_i, EXPERTS_PER_GROUP, dtype=jnp.float32))
    gates = (p_sel[:, None, None] * jax.nn.one_hot(g_sel, N_GROUPS, dtype=jnp.float32)[:, :, None]
             * fine[:, None, :]).astype(x.dtype)
    y = jnp.zeros_like(t)
    for g in range(N_GROUPS):
        e = slice(g * EXPERTS_PER_GROUP, (g + 1) * EXPERTS_PER_GROUP)
        hg = jnp.einsum('td,edf->tef', t, w_gate[e])
        hu = jnp.einsum('td,edf->tef', t, w_up[e])
        h = jax.nn.silu(hg) * hu * gates[:, g, :, None]
        y = y + jnp.einsum('tef,efd->td', h, w_down[e])
    return y.reshape(B, L, D)

def trunk_layer(x, conv_hist, pool_hist, pos0, g1, w_in, conv_w, pool_w, pool_scale, sgu_w, sgu_b,
                w_out, g2, rc_w, rc_b, rf_w, rf_b, w_gate, w_up, w_down):
    h = rmsnorm(x, g1)
    proj = jnp.einsum('bld,dp->blp', h, w_in)
    a_b, a_c, a_h, p_in, s_u, s_v = jnp.split(proj, SPLIT_POINTS, axis=-1)
    conv_y, conv_state = short_conv(a_c * a_h, conv_hist, conv_w)
    a_out = a_b * conv_y
    p_out, pool_state = multiscale_pool(p_in, pool_hist, pos0, pool_w, pool_scale)
    s_out = spatial_gating(s_u, s_v, sgu_w, sgu_b)
    mix = jnp.einsum('blm,md->bld', jnp.concatenate([a_out, p_out, s_out], axis=-1), w_out)
    x = x + mix
    x = x + hier_moe(rmsnorm(x, g2), rc_w, rc_b, rf_w, rf_b, w_gate, w_up, w_down)
    return x, conv_state, pool_state, s_v

def setup_inputs(seed: int = 0) -> dict:
    key = jax.random.key(seed)
    ks = jax.random.split(key, 24)
    f32 = jnp.float32
    nrm = lambda k, shape, s: (jax.random.normal(k, shape, f32) * s)
    return {
        'x_prompt': nrm(ks[0], (BATCH, SEQ, D_MODEL), 1.0),
        'x_sample': nrm(ks[1], (DEC_BATCH, DEC_SEQ, D_MODEL), 1.0),
        'state_conv': nrm(ks[2], (DEPTH, DEC_BATCH, CONV_WIDTH - 1, D_CONV), 1.0),
        'state_pool': nrm(ks[3], (DEPTH, DEC_BATCH, POOL_HIST, D_POOL), 1.0),
        'norm1_g': 1.0 + nrm(ks[4], (DEPTH, D_MODEL), 0.02),
        'w_in': nrm(ks[5], (DEPTH, D_MODEL, D_PROJ), D_MODEL ** -0.5),
        'conv_w': nrm(ks[6], (DEPTH, CONV_WIDTH, D_CONV), CONV_WIDTH ** -0.5),
        'pool_w': nrm(ks[7], (DEPTH, N_POOL_GROUPS, POOL_GROUP, POOL_GROUP), POOL_GROUP ** -0.5),
        'pool_scale': 1.0 + nrm(ks[8], (DEPTH, D_POOL), 0.02),
        'sgu_w': nrm(ks[9], (DEPTH, SGU_HEADS, SGU_LEN, SGU_LEN), SGU_LEN ** -0.5),
        'sgu_b': 1.0 + nrm(ks[10], (DEPTH, SGU_HEADS, SGU_LEN), 0.02),
        'w_out': nrm(ks[11], (DEPTH, D_MIX, D_MODEL), D_MIX ** -0.5),
        'norm2_g': 1.0 + nrm(ks[12], (DEPTH, D_MODEL), 0.02),
        'router_coarse_w': nrm(ks[13], (DEPTH, D_MODEL, N_GROUPS), D_MODEL ** -0.5),
        'router_coarse_b': nrm(ks[14], (DEPTH, N_GROUPS), 0.01),
        'router_fine_w': nrm(ks[15], (DEPTH, D_MODEL, N_EXPERTS), D_MODEL ** -0.5),
        'router_fine_b': nrm(ks[16], (DEPTH, N_EXPERTS), 0.01),
        'moe_w_gate': nrm(ks[17], (DEPTH, N_EXPERTS, D_MODEL, D_EXPERT), D_MODEL ** -0.5),
        'moe_w_up': nrm(ks[18], (DEPTH, N_EXPERTS, D_MODEL, D_EXPERT), D_MODEL ** -0.5),
        'moe_w_down': nrm(ks[19], (DEPTH, N_EXPERTS, D_EXPERT, D_MODEL), D_EXPERT ** -0.5),
        'final_norm_g': 1.0 + nrm(ks[20], (D_MODEL,), 0.02),
    }

def reference(x_prompt, x_sample, state_conv, state_pool, norm1_g, w_in, conv_w, pool_w, pool_scale,
              sgu_w, sgu_b, w_out, norm2_g, router_coarse_w, router_coarse_b, router_fine_w,
              router_fine_b, moe_w_gate, moe_w_up, moe_w_down, final_norm_g):
    def run_stack(x, conv_hist, pool_hist, pos0):
        conv_new, pool_new, v_new = [], [], []
        for l in range(DEPTH):
            x, c, p, v = trunk_layer(x, conv_hist[l], pool_hist[l], pos0, norm1_g[l], w_in[l], conv_w[l],
                                     pool_w[l], pool_scale[l], sgu_w[l], sgu_b[l], w_out[l], norm2_g[l],
                                     router_coarse_w[l], router_coarse_b[l], router_fine_w[l],
                                     router_fine_b[l], moe_w_gate[l], moe_w_up[l], moe_w_down[l])
            conv_new.append(c)
            pool_new.append(p)
            v_new.append(v)
        return rmsnorm(x, final_norm_g), jnp.stack(conv_new), jnp.stack(pool_new), jnp.stack(v_new)

    b_p = x_prompt.shape[0]
    zero_conv = jnp.zeros((DEPTH, b_p, CONV_WIDTH - 1, D_CONV), x_prompt.dtype)
    zero_pool = jnp.zeros((DEPTH, b_p, POOL_HIST, D_POOL), x_prompt.dtype)
    y_prompt, new_conv_prompt, new_pool_prompt, _ = run_stack(x_prompt, zero_conv, zero_pool, 0)
    y_sample, new_conv_sample, new_pool_sample, new_sgu_v_sample = run_stack(x_sample, state_conv, state_pool, PAST_LEN)
    return (y_prompt, y_sample, new_conv_prompt, new_pool_prompt, new_conv_sample, new_pool_sample, new_sgu_v_sample)


_drawn_inputs = setup_inputs


def setup_inputs(seed=0):
    import zlib

    import numpy as np

    out = dict(_drawn_inputs(seed))
    spreads = {}
    factors = {'pool_scale': 15.471,
     'sgu_b': 11.641,
     'router_coarse_b': 11.887,
     'router_fine_b': 14.236,
     'final_norm_g': 25.744,
     'norm2_g': 5.523,
     'state_conv': 4.623}
    for name, (base, spread) in spreads.items():
        noise = np.random.default_rng([zlib.crc32(name.encode()), seed]).standard_normal(out[name].shape)
        drawn = base * np.exp(spread * noise) if base else spread * noise
        out[name] = __import__('jax').numpy.asarray(drawn.astype(out[name].dtype))
    for name, factor in factors.items():
        out[name] = (out[name] * factor).astype(out[name].dtype)
    return out
```

```python
import concourse.bass as bass
from concourse import mybir
from concourse.alu_op_type import AluOpType as ALU

F32 = mybir.dt.float32
BF16 = mybir.dt.bfloat16
I32 = mybir.dt.int32
ACT = mybir.ActivationFunctionType
AX = mybir.AxisListType

P = 128
D = 1024
KD = D // P
SEQ, DEC = 512, 64
T = SEQ + DEC
NT = 5
TOK = [P, P, P, P, DEC]
D_CONV, D_POOL, D_SGU = 384, 256, 384
CONV_HIST, POOL_HIST = 2, 15
D_PROJ = 3 * D_CONV + D_POOL + 2 * D_SGU
COL_B, COL_C, COL_H = 0, D_CONV, 2 * D_CONV
COL_P = 3 * D_CONV
COL_U = COL_P + D_POOL
COL_V = COL_U + D_SGU
HEADS, HEAD_DIM = 4, D_SGU // 4
NG, EPG, NE = 4, 8, 32
F = 512
EPS = 1e-6
HT = T // 2

ZC = CONV_HIST + SEQ + CONV_HIST + DEC
ZC_S = CONV_HIST + SEQ + CONV_HIST
YC = ZC - CONV_HIST
YC_S = SEQ + CONV_HIST
ZP = POOL_HIST + SEQ + POOL_HIST + DEC
ZP_S = POOL_HIST + SEQ + POOL_HIST
PO = ZP - POOL_HIST
PO_S = SEQ + POOL_HIST
PO_A = 296

R_G1, R_CW, R_PS, R_SC, R_SP, R_ALL = 0, 8, 17, 19, 25, 55

BLK = 64
MAX_J = T // BLK - 1
NOV = 2 * T // BLK
NCOL = NE + NOV
NSLOT = 3
PRE = [(NE - s + NSLOT - 1) // NSLOT for s in range(NSLOT)]
ROUNDS = NE // NSLOT
PAD = 65536.0

CONSTS = {}
_at = 0
for _name, _n in (("ident", P), ("causal", P), ("strict", P), ("iota_col", NCOL), ("iota_pos", BLK),
                  ("w4", NG), ("w8", EPG), ("valid", NT), ("vals", 6 * NT), ("half", 1), ("invw", 2),
                  ("rc15", 2 * POOL_HIST), ("expert", NE), ("past", MAX_J), ("ovnum", NOV), ("eps", 1)):
    CONSTS[_name] = (_at, _at + _n)
    _at += _n
NCONST = _at


def constant_tile():
    import numpy as np
    c = np.zeros((P, NCONST), np.float32)
    p = np.arange(P)

    def put(name, value):
        a, b = CONSTS[name]
        c[:, a:b] = value

    put("ident", np.eye(P))
    put("causal", p[:, None] <= p[None, :])
    put("strict", p[:, None] < p[None, :])
    put("iota_col", np.arange(NCOL))
    put("iota_pos", np.arange(BLK))
    put("w4", np.arange(NG, 0, -1))
    put("w8", np.arange(EPG, 0, -1))
    valid = np.array([[float(i < TOK[t]) for t in range(NT)] for i in range(P)])
    put("valid", valid)
    vals = np.zeros((P, NT, 2, 3))
    for t in range(NT):
        number = t * P + p + 1
        for k in range(2):
            vals[:, t, k, 0] = number // 32
            vals[:, t, k, 1] = number % 32
            vals[:, t, k, 2] = k
    put("vals", (vals * valid[:, :, None, None]).reshape(P, -1))
    put("half", (p >= 64)[:, None])
    win = np.array([[2, 8], [4, 16]])[(p >= 64).astype(int)]
    put("invw", 1.0 / win)
    put("rc15", (1.0 / np.minimum(win[:, :, None], np.arange(1, POOL_HIST + 1))).reshape(P, -1))
    put("expert", np.arange(NE))
    put("past", BLK * np.arange(1, MAX_J + 1))
    put("ovnum", np.arange(NOV))
    put("eps", EPS)
    return c


def sgu_pieces():
    out = []
    for q in range(D_SGU // P):
        at = 0
        while at < P:
            ch = q * P + at
            head = ch // HEAD_DIM
            left = min((head + 1) * HEAD_DIM - ch, P - at)
            size = 64 if left >= 64 and at % 64 == 0 else 32
            out.append((q, at, size, head, ch))
            at += size
    return out


def build(nc, x_prompt, x_sample, state_conv, state_pool, norm1_g, w_in, conv_w, pool_w, pool_scale,
          sgu_w, sgu_b, w_out, norm2_g, rc_w, rc_b, rf_w, rf_b, w_gate, w_up, w_down, final_g, consts,
          y_prompt, y_sample, new_conv_prompt, new_pool_prompt, new_conv_sample, new_pool_sample,
          new_sgu_v):
    hn2_rows = nc.dram_tensor("hn2_rows", [2 * T, D // 2], F32, kind="Internal").ap()
    y_rows = nc.dram_tensor("y_rows", [4 * T, D // 2], F32, kind="Internal").ap()

    W1_BYTES, WD_BYTES = 2 * KD * F * 4, (F // P) * D * 4
    SLOT_BYTES = W1_BYTES + WD_BYTES
    first = (nc.sbuf_base + 31) // 32 * 32
    slot_at = [first + s * SLOT_BYTES for s in range(NSLOT + 1)]
    where = {}

    def region(start, end):
        at = [start]

        def place(name, shape, dt=F32):
            n = 2 if dt == BF16 else 4
            for x in shape[1:]:
                n *= x
            t = nc.alloc_sbuf_tensor_at(name, shape, dt, offset=at[0])
            where[name] = at[0]
            at[0] += (n + 31) // 32 * 32
            where["end"] = at[0]
            assert at[0] <= end, (name, at[0] - end)
            return t
        return place

    w1, wd = [], []
    for s in range(NSLOT):
        slot = region(slot_at[s], slot_at[s + 1])
        w1.append(slot(f"w1_{s}", [P, 2, KD, F]))
        wd.append(slot(f"wd_{s}", [P, F // P, D]))
    early = region(slot_at[0], slot_at[2])
    wi = early("wi", [P, KD, D_PROJ])
    hT = early("hT", [P, KD, T])
    cbuf = early("cbuf", [P, T])
    zc = early("zc", [P, 3, ZC])
    early2 = region(slot_at[2], slot_at[3])
    wo = early2("wo", [P, KD, D])
    v_sb = early2("v_sb", [P, NT, D_SGU])
    yconv = early2("yconv", [P, YC])
    gated = early2("gated", [P, T])
    pool_wbd = early2("pool_wbd", [P, 2, P])
    wmT = early2("wmT", [P, HEADS, P])
    convst = early2("convst", [P, 3, 4])
    poolst = early2("poolst", [P, 2, 2 * POOL_HIST])
    late2 = region(where["yconv"], slot_at[3])
    conv_rows = late2("conv_rows", [P, D_CONV])
    pool_rows = late2("pool_rows", [P, D_POOL])

    rest = region(slot_at[3], nc.sbuf_usable_end)
    x_sb = rest("x_sb", [P, NT, D])
    mixT = rest("mixT", [P, KD, T])
    zp = rest("zp", [P, 2, ZP])
    win_a = rest("win_a", [P, ZP])
    win_b = rest("win_b", [P, ZP])
    pooled = rest("pooled", [P, 2, PO])
    pool_end = where["end"]
    cst = rest("cst", [P, NCONST])
    g2b = rest("g2b", [P, D])
    gfb = g2b
    rw = rest("rw", [P, KD, NG + NE])
    rbias = rest("rbias", [P, NG + NE])
    bfull = rest("bfull", [P, 3, P])
    prmT = rest("prmT", [P, R_ALL])
    small = rest("small", [P, 24, NT])
    gates = rest("gates", [P, NT, 2])
    L = rest("L", [P, NT, NG + NE])
    idx_x = rest("idx_x", [P, NCOL], I32)
    idx_y = rest("idx_y", [P, NCOL], I32)
    ovexp = rest("ovexp", [P, NOV], I32)
    nov = rest("nov", [P, 1], I32)
    idc_x = rest("idc_x", [P, NSLOT], I32)
    idc_y = rest("idc_y", [P, NSLOT], I32)
    pre = region(where["mixT"], where["zp"])
    hstage = pre("hstage", [P, 2, D])
    sguw = pre("sguw", [P, HEADS, P])
    prm = pre("prm", [P, P])
    post = region(where["mixT"], where["zp"])
    xT = post("xT", [P, KD // 2, P])
    silu_g = post("silu_g", [P, F // 2])
    hexp = post("hexp", [P, F // 2])
    hexT = post("hexT", [P, 2, P])
    t_g = post("t_g", [P, NT, NG])
    e_g = post("e_g", [P, NT, NG])
    oh_g = post("oh_g", [P, NT, NG])
    t_ge = post("t_ge", [P, NT, NG, EPG])
    sel = post("sel", [P, NT, EPG])
    t_e = post("t_e", [P, NT, EPG])
    oh_k = post("oh_k", [P, NT, 2, EPG])
    memb = post("memb", [P, NT, 2, NE])
    Mb = post("Mb", [P, NT, NE], BF16)
    Mc = post("Mc", [P, NT + 1, NE], BF16)
    pos = post("pos", [P, NT + 1, NE])
    t_m = post("t_m", [P, NT, 2, NE])
    t_j = post("t_j", [P, NE, MAX_J])
    nblk = post("nblk", [P, 3, NE])
    t_o = post("t_o", [P, NOV, NE])
    at_k = post("at_k", [P, 6, NT * 2])
    t_k = post("t_k", [P, NT * 2, MAX_J])
    t_x = post("t_x", [P, 5, NCOL])
    p2 = region(where["zp"], pool_end)
    hn2p = p2("hn2p", [P, 2, D])
    hn2T = p2("hn2T", [P, KD, P])
    tri_b = p2("tri_b", [P, P], BF16)
    ones_b = p2("ones_b", [P, P], BF16)
    p3 = region(where["zp"], pool_end)
    xg = p3("xg", [P, NSLOT, D // 2])
    ybuf = p3("ybuf", [P, NSLOT, D // 2])
    p4 = region(where["ybuf"], pool_end)
    onehot_s = p4("onehot_s", [P, NT * 2, BLK], BF16)
    onehot_c = p4("onehot_c", [P, NT * 2, NCOL], BF16)
    onehot_v = p4("onehot_v", [P, NT * 2, 3, NCOL], BF16)
    p5 = region(slot_at[1], slot_at[2])
    yfin = [p5(f"yfin{i}", [P, 2 * D]) for i in range(NT)]

    ps = nc.alloc_psum_tensor("ps", [P, 8, 512], F32)

    def con(name):
        a, b = CONSTS[name]
        return cst[:, a:b]

    ident = con("ident")

    sem = nc.alloc_semaphore
    consts_in, params_in, sguw_in, sgub_in = sem("consts_in"), sem("params_in"), sem("sguw_in"), sem("sgub_in")
    x_in = [sem(f"x_in{j}") for j in range(NT)]
    wi_in = {g: sem(f"wi_in_{g}") for g in "vpuchb"}
    poolw_in, g2_in, router_in, wo_in, gf_in = (sem("poolw_in"), sem("g2_in"), sem("router_in"),
                                                sem("wo_in"), sem("gf_in"))
    zeroed, tri_ready = sem("zeroed"), sem("tri_ready")
    prm_ps, prm_ready, wm_ps, wm_ready = sem("prm_ps"), sem("prm_ready"), sem("wm_ps"), sem("wm_ready")
    hist_ready = sem("hist_ready")
    std1, rstd1, h_ready, hT_ps, hT_ready = (sem("std1"), sem("rstd1"), sem("h_ready"), sem("hT_ps"),
                                             sem("hT_ready"))
    v_ps, v_ready = sem("v_ps"), sem("v_ready")
    proj_ps, evac_act, evac_dve = sem("proj_ps"), sem("evac_act"), sem("evac_dve")
    sgu_ps, sgu_read, sgu_ready = sem("sgu_ps"), sem("sgu_read"), sem("sgu_ready")
    pooled_ready, pool_ps, pool_ready = sem("pooled_ready"), sem("pool_ps"), sem("pool_ready")
    st_ready, st_ps, st_rows, st_out = sem("st_ready"), sem("st_ps"), sem("st_rows"), sem("st_out")
    wo_ps, x2_ready, std2, hn2_ready = sem("wo_ps"), sem("x2_ready"), sem("std2"), sem("hn2_ready")
    hn2_out = [sem("hn2_out0"), sem("hn2_out1")]
    hn2T_ps, hn2T_ready, L_ps, L_ready = sem("hn2T_ps"), sem("hn2T_ready"), sem("L_ps"), sem("L_ready")
    gdiff_ready, gexp_ready, kdiff_ready, kexp_ready = (sem("gdiff_ready"), sem("gexp_ready"),
                                                        sem("kdiff_ready"), sem("kexp_ready"))
    memb_ready, pos_ps, onehot_ready, idx_ps, idx_ready, nov_ready = (
        sem("memb_ready"), sem("pos_ps"), sem("onehot_ready"), sem("idx_ps"), sem("idx_ready"),
        sem("nov_ready"))
    xg_zero = sem("xg_zero")
    w1_in = [sem(f"w1_in{s}") for s in range(NSLOT)]
    wd_in = [sem(f"wd_in{s}") for s in range(NSLOT)]
    xg_in = [sem(f"xg_in{s}") for s in range(NSLOT)]
    y_out = [sem(f"y_out{s}") for s in range(NSLOT)]
    idc_ready = sem("idc_ready")
    idc_seen = sem("idc_seen")
    xT_ps, xT_ready, gu_ps, silu_ready, h_exp = (sem("xT_ps"), sem("xT_ready"), sem("gu_ps"),
                                                 sem("silu_ready"), sem("h_exp"))
    hexT_ps, hexT_ready, dn_ps, y_ready = sem("hexT_ps"), sem("hexT_ready"), sem("dn_ps"), sem("y_ready")
    yfin_in = [sem(f"yfin_in{j}") for j in range(NT)]
    acc_ready, std3, out_ready, y_done = sem("acc_ready"), sem("std3"), sem("out_ready"), sem("y_done")
    dve_step, act_step = sem("dve_step"), sem("act_step")

    CHUNKS = [("p", 0), ("p", 1), ("u", 0), ("u", 1), ("u", 2)] + [(g, q) for q in range(3) for g in "chb"]
    COLS = {"p": COL_P, "u": COL_U, "c": COL_C, "h": COL_H, "b": COL_B}
    nth = {ch: n for n, ch in enumerate(CHUNKS)}
    ON_ACT = "puc"

    def evacuated(eng, n):
        mine = CHUNKS[n][0] in ON_ACT
        count = sum((g in ON_ACT) == mine for g, _ in CHUNKS[:n + 1])
        eng.wait_ge(evac_act if mine else evac_dve, count)

    def pair(n):
        return 2 * (n % 2)

    halves = ((0, 0, HT), (1, HT, T))
    segs = ((0, 0, HT, 0, 0), (1, 0, SEQ - HT, HT, 0), (1, SEQ - HT, HT, SEQ, 1))
    pieces = sgu_pieces()

    def experts(eng, body, last=ROUNDS):
        for s in range(NSLOT):
            body(0, s)
        with eng.Fori(1, last) as i:
            for s in range(NSLOT):
                body(i, s)
        for n in range(NSLOT * last, NE):
            body(n // NSLOT, n % NSLOT)

    def blocks_past(eng, body):
        eng.wait_ge(nov_ready, 1)
        count = eng.value_load(nov[0:1, 0:1], min_val=0, max_val=NOV)
        with eng.If(count > 0):
            with eng.Fori(0, count) as b:
                body(b)
        return count

    with nc.Block() as block:

        @block.sync
        def _(sp):
            x_rows = [x_prompt[0, j * P:(j + 1) * P, :] for j in range(4)] + [x_sample[0]]
            wi_v = w_in[0].rearrange("(k p) n -> p k n", p=P)

            def load_wi(g, a, n):
                sp.dma_start(wi[:, :, a:a + n], wi_v[:, :, a:a + n]).then_inc(wi_in[g], 16)

            sp.dma_start(x_sb[:, 0, :], x_rows[0]).then_inc(x_in[0], 16)
            sp.dma_start(cst[:], consts).then_inc(consts_in, 16)
            sp.dma_start(prm[R_G1:R_CW, :], norm1_g[0].rearrange("(q p) -> q p", p=P)).then_inc(params_in, 16)
            sp.dma_start(prm[R_CW:R_PS, :], conv_w[0].rearrange("k (q p) -> (k q) p", p=P)).then_inc(params_in, 16)
            sp.dma_start(prm[R_PS:R_SC, :], pool_scale[0].rearrange("(q p) -> q p", p=P)).then_inc(params_in, 16)
            sp.dma_start(prm[R_SC:R_SP, :], state_conv[0, 0].rearrange("r (q p) -> (r q) p", p=P)).then_inc(params_in, 16)
            sp.dma_start(prm[R_SP:R_ALL, :], state_pool[0, 0].rearrange("r (q p) -> (r q) p", p=P)).then_inc(params_in, 16)
            sp.dma_start(x_sb[:, 1, :], x_rows[1]).then_inc(x_in[1], 16)
            load_wi("v", COL_V, D_SGU)
            sp.dma_start(sguw[:], sgu_w[0].rearrange("h i j -> i h j")).then_inc(sguw_in, 16)
            for j in range(2, NT):
                sp.dma_start(x_sb[0:TOK[j], j, :], x_rows[j]).then_inc(x_in[j], 16)
            load_wi("p", COL_P, D_POOL)
            load_wi("u", COL_U, D_SGU)
            for head in range(HEADS):
                for q in range(3):
                    a, b = max(head * HEAD_DIM, q * P), min((head + 1) * HEAD_DIM, (q + 1) * P)
                    if a < b:
                        sp.dma_start(bfull[a - q * P:b - q * P, q, :],
                                     sgu_b[0, head:head + 1, :].broadcast_to([b - a, P])).then_inc(sgub_in, 16)
            sp.wait_ge(zeroed, 1)
            for g in range(4):
                r, a = g // 2, 64 * (g % 2)
                sp.dma_start(pool_wbd[a:a + 64, r, a:a + 64], pool_w[0, g]).then_inc(poolw_in, 16)
            load_wi("c", COL_C, D_CONV)
            load_wi("h", COL_H, D_CONV)
            load_wi("b", COL_B, D_CONV)
            sp.dma_start(wo[:], w_out[0].rearrange("(k p) n -> p k n", p=P)).then_inc(wo_in, 16)
            sp.dma_start(g2b[:], norm2_g[0:1, :].broadcast_to([P, D])).then_inc(g2_in, 16)
            sp.dma_start(rw[:, :, 0:NG], rc_w[0].rearrange("(p k) e -> p k e", p=P)).then_inc(router_in, 16)
            sp.dma_start(rw[:, :, NG:NG + NE], rf_w[0].rearrange("(p k) e -> p k e", p=P)).then_inc(router_in, 16)
            sp.dma_start(rbias[:, 0:NG], rc_b[0:1, :].broadcast_to([P, NG])).then_inc(router_in, 16)
            sp.dma_start(rbias[:, NG:NG + NE], rf_b[0:1, :].broadcast_to([P, NE])).then_inc(router_in, 16)
            sp.wait_ge(v_ready, NT)
            sp.dma_start(new_sgu_v[0, 0], v_sb[0:DEC, NT - 1, :]).then_inc(st_out, 16)

            gate_v = w_gate[0].rearrange("e (p k) f -> p e (k f)", p=P)
            up_v = w_up[0].rearrange("e (p k) f -> p e (k f)", p=P)
            down_v = w_down[0].rearrange("e (c p) d -> p e c d", p=P)

            def load_gate_up(e, s):
                for a, view in ((0, gate_v), (1, up_v)):
                    sp.dma_start(w1[s][:, a:a + 1, :, :].rearrange("p a k f -> p a (k f)"),
                                 view[:, bass.ds(e, 1), :]).then_inc(w1_in[s], 16)

            def load_down(e, s):
                sp.dma_start(wd[s][:].rearrange("p (o c) d -> p o c d", o=1),
                             down_v[:, bass.ds(e, 1), :, :]).then_inc(wd_in[s], 16)

            sp.wait_ge(proj_ps, len(CHUNKS))
            load_gate_up(0, 0)
            load_down(0, 0)
            sp.wait_ge(evac_dve, 6)
            sp.wait_ge(st_ready, 1)
            load_gate_up(1, 1)
            load_down(1, 1)
            sp.wait_ge(st_rows, 2)
            sp.dma_start(new_conv_prompt[0, 0], conv_rows[0:2, :]).then_inc(st_out, 16)
            sp.dma_start(new_conv_sample[0, 0], conv_rows[2:4, :]).then_inc(st_out, 16)
            sp.dma_start(new_pool_prompt[0, 0], pool_rows[0:POOL_HIST, :]).then_inc(st_out, 16)
            sp.dma_start(new_pool_sample[0, 0], pool_rows[POOL_HIST:2 * POOL_HIST, :]).then_inc(st_out, 16)
            hn2_v = hn2_rows.rearrange("(t h) d -> t (h d)", h=2)
            for j in range(NT):
                sp.wait_ge(hn2_ready, j + 1)
                sp.dma_start(hn2_v[j * P:j * P + TOK[j], :], hn2p[0:TOK[j], j % 2, :]).then_inc(hn2_out[j % 2], 16)
                if j == NT - 1:
                    sp.dma_start(gfb[:], final_g.rearrange("(o d) -> o d", o=1).broadcast_to([P, D])).then_inc(gf_in, 16)
                if j == NT - 2:
                    sp.wait_ge(wo_ps, NT)
                    sp.wait_ge(st_out, 80)
                    load_gate_up(2, 2)
                    load_down(2, 2)

            def refill(i, s):
                sp.wait_ge(gu_ps, NSLOT * (i - 1) + s + 1)
                load_gate_up(NSLOT * i + s, s)
                sp.wait_ge(dn_ps, NSLOT * (i - 1) + s + 1)
                load_down(NSLOT * i + s, s)

            with sp.Fori(1, ROUNDS) as i:
                for s in range(NSLOT):
                    refill(i, s)
            for n in range(NSLOT * ROUNDS, NE):
                refill(n // NSLOT, n % NSLOT)

            def block_past(b):
                sp.wait_ge(dn_ps, NE + b)
                e = sp.value_load(ovexp[0:1, bass.ds(b, 1)], min_val=0, max_val=NE - 1)
                load_gate_up(e, 0)
                load_down(e, 0)

            count = blocks_past(sp, block_past)
            sp.wait_ge(y_out[0], 16 * (PRE[0] + count))
            sp.wait_ge(y_out[1], 16 * PRE[1])
            sp.wait_ge(y_out[2], 16 * PRE[2])
            y_v = y_rows.rearrange("(t r) d -> t (r d)", r=4)
            for j in range(NT):
                sp.dma_start(yfin[j][0:TOK[j], :], y_v[j * P:j * P + TOK[j], :]).then_inc(yfin_in[j], 16)
            y_tiles = [y_prompt[0, j * P:(j + 1) * P, :] for j in range(4)] + [y_sample[0]]
            for j in range(NT):
                sp.wait_ge(out_ready, j + 1)
                sp.dma_start(y_tiles[j], yfin[j][0:TOK[j], 0:D]).then_inc(y_done, 16)
            sp.wait_ge(y_done, 16 * NT)

        @block.gpsimd
        def _(pool):
            nc.gpsimd.memset(pool_wbd[:], 0.0).then_inc(zeroed, 1)
            nc.gpsimd.memset(zc[:], 0.0).then_inc(zeroed, 1)
            nc.gpsimd.memset(zp[:], 0.0).then_inc(zeroed, 1)
            evacuated(pool, nth["p", 1])
            nc.gpsimd.tensor_copy(poolst[:, :, 0:POOL_HIST], zp[:, :, SEQ:SEQ + POOL_HIST])
            nc.gpsimd.tensor_copy(poolst[:, :, POOL_HIST:], zp[:, :, ZP - POOL_HIST:ZP])
            evacuated(pool, nth["h", 2])
            nc.gpsimd.tensor_copy(convst[:, :, 0:2], zc[:, :, SEQ:SEQ + CONV_HIST])
            nc.gpsimd.tensor_copy(convst[:, :, 2:4], zc[:, :, ZC - CONV_HIST:ZC]).then_inc(st_ready, 1)

            pool.wait_ge(hn2T_ps, 2 * NT)
            for par in range(2):
                pool.wait_ge(hn2_out[par], 16 * len(range(par, NT, 2)))
            pool.wait_ge(L_ps, NT)
            nc.gpsimd.memset(xg[:], 0.0).then_inc(xg_zero, 1)
            pool.wait_ge(xg_zero, 1)
            pool.wait_ge(idx_ready, 1)

            def gather(col, s, done):
                nc.gpsimd.tensor_copy(idc_x[:, s:s + 1], idx_x[:, bass.ds(col, 1)]).then_inc(idc_ready, 1)
                pool.wait_ge(idc_ready, done)
                pool.sem_inc(idc_seen, 1)
                nc.gpsimd.indirect_dma_start(
                    out=xg[:, s, :], out_offset=None, in_=hn2_rows,
                    in_offset=bass.IndirectOffsetOnAxis(ap=idc_x[:, s:s + 1], axis=0),
                    bounds_check=2 * T - 1, oob_is_err=False).then_inc(xg_in[s], 16)

            def scatter(col, s, n, done):
                nc.gpsimd.tensor_copy(idc_y[:, s:s + 1], idx_y[:, bass.ds(col, 1)]).then_inc(idc_ready, 1)
                pool.wait_ge(idc_ready, done)
                pool.sem_inc(idc_seen, 1)
                nc.gpsimd.indirect_dma_start(
                    out=y_rows, out_offset=bass.IndirectOffsetOnAxis(ap=idc_y[:, s:s + 1], axis=0),
                    in_=ybuf[:, s, :], in_offset=None,
                    bounds_check=4 * T - 1, oob_is_err=False).then_inc(y_out[s], 16)

            for s in range(NSLOT):
                gather(s, s, s + 1)

            def turn(i, s, more=True):
                n = NSLOT * i + s
                pool.wait_ge(y_ready, n + 1)
                scatter(n, s, n, NSLOT + 2 * n + 1)
                if more:
                    gather(n + NSLOT, s, NSLOT + 2 * n + 2)

            for s in range(NSLOT):
                turn(0, s)
            with pool.Fori(1, ROUNDS - 1) as i:
                for s in range(NSLOT):
                    turn(i, s)
            left = NSLOT * (ROUNDS - 1)
            for n in range(left, NE):
                if n + NSLOT < NE:
                    turn(n // NSLOT, n % NSLOT)
            copies = NSLOT + 2 * (NE - NSLOT)
            for n in range(NE - NSLOT, NE):
                pool.wait_ge(y_ready, n + 1)
                copies += 1
                scatter(n, n % NSLOT, n, copies)

            def block_past(b):
                pool.wait_ge(y_ready, NE + b)
                gather(NE + b, 0, copies + 2 * b + 1)
                pool.wait_ge(y_ready, NE + b + 1)
                scatter(NE + b, 0, NE + b, copies + 2 * b + 2)

            blocks_past(pool, block_past)

        @block.scalar
        def _(act):
            steps = [0]

            def link(ins):
                steps[0] += 1
                ins.then_inc(act_step, 1)
                act.wait_ge(act_step, steps[0])

            def std(j, col, src, junk, done):
                n = TOK[j]
                link(nc.scalar.activation(junk, src, ACT.Square, accum_out=small[0:n, col, j:j + 1]))
                nc.scalar.activation(small[0:n, col + 1, j:j + 1], small[0:n, col, j:j + 1], ACT.Sqrt,
                                     bias=con("eps")[0:n, :], scale=1.0 / D).then_inc(done, 1)

            def normalise(j):
                n = TOK[j]
                act.wait_ge(rstd1, j + 1)
                if j >= 2:
                    act.wait_ge(hT_ps, 2 * (j - 1))
                nc.scalar.activation(hstage[0:n, j % 2, :], x_sb[0:n, j, :], ACT.Copy,
                                     scale=small[0:n, 2, j:j + 1]).then_inc(h_ready, 1)

            act.wait_ge(consts_in, 16)
            for j in range(NT):
                act.wait_ge(x_in[j], 16)
                if j >= 2:
                    act.wait_ge(hT_ps, 2 * (j - 1))
                std(j, 0, x_sb[0:TOK[j], j, :], hstage[0:TOK[j], j % 2, :], std1)
                if j >= 1:
                    normalise(j - 1)
            normalise(NT - 1)

            def take(g, q):
                n = nth[g, q]
                act.wait_ge(proj_ps, n + 1)
                b0 = pair(n)
                if g == "p":
                    for bank, a, b, t0, smp in segs:
                        at = POOL_HIST + t0 + smp * POOL_HIST
                        last = nc.scalar.copy(zp[:, q, at:at + b - a], ps[:, b0 + bank, a:b])
                elif g == "u":
                    for bank, a, b in halves:
                        last = nc.scalar.copy(mixT[:, 5 + q, a:b], ps[:, b0 + bank, 0:b - a])
                else:
                    if q:
                        evacuated(act, nth["h", q - 1])
                    for bank, a, b in halves:
                        last = nc.scalar.copy(cbuf[:, a:b], ps[:, b0 + bank, 0:b - a])
                last.then_inc(evac_act, 1)

            def take_pool(r):
                act.wait_ge(pool_ps, r + 1)
                scale = prmT[:, R_PS + r:R_PS + r + 1]
                nc.scalar.activation(mixT[:, 3 + r, 0:PO_A], ps[:, 6, 0:PO_A], ACT.Copy, scale=scale)
                nc.scalar.activation(mixT[:, 3 + r, PO_A:SEQ], ps[:, 7, 0:SEQ - PO_A], ACT.Copy, scale=scale)
                nc.scalar.activation(mixT[:, 3 + r, SEQ:T], ps[:, 7, PO_S - PO_A:PO - PO_A], ACT.Copy,
                                     scale=scale).then_inc(pool_ready, 1)

            act.wait_ge(hT_ps, 2 * NT)
            act.wait_ge(wm_ps, 1)
            act.wait_ge(prm_ready, 1)
            act.wait_ge(hist_ready, 1)
            for g, q in CHUNKS[:nth["h", 0]]:
                take(g, q)
            take_pool(0)
            take_pool(1)
            take("c", 1)
            take("c", 2)
            act.wait_ge(st_ps, 1)
            act.wait_ge(evac_dve, 6)
            nc.scalar.copy(conv_rows[0:4, :], ps[0:4, 7, 0:D_CONV]).then_inc(st_rows, 1)
            nc.scalar.copy(pool_rows[0:2 * POOL_HIST, :], ps[0:2 * POOL_HIST, 6, 0:D_POOL]).then_inc(st_rows, 1)

            def take_hn2T(j):
                n = TOK[j]
                if j:
                    act.wait_ge(L_ps, j)
                for h in range(2):
                    act.wait_ge(hn2T_ps, 2 * j + h + 1)
                    nc.scalar.copy(hn2T[:, 4 * h:4 * h + 4, 0:n],
                                   ps[:, 4 + h, 0:4 * n].rearrange("p (k t) -> p k t", k=4)).then_inc(hn2T_ready, 1)

            junk = hn2T[:].rearrange("p k t -> p (k t)")
            for j in range(NT):
                act.wait_ge(x2_ready, j + 1)
                if j >= 2:
                    act.wait_ge(L_ps, j - 1)
                std(j, 3, x_sb[0:TOK[j], j, :], junk[0:TOK[j], :], std2)
                if j >= 1:
                    take_hn2T(j - 1)
            take_hn2T(NT - 1)

            act.wait_ge(gdiff_ready, 1)
            nc.scalar.activation(e_g[:], t_g[:], ACT.Exp).then_inc(gexp_ready, 1)
            act.wait_ge(kdiff_ready, 1)
            nc.scalar.activation(small[:, 15, :], small[:, 14, :], ACT.Exp).then_inc(kexp_ready, 1)

            def work(n, s, i):
                act.wait_ge(gu_ps, n + 1)
                nc.scalar.activation(silu_g[:], ps[:, 1, 0:F // 2], ACT.Silu).then_inc(silu_ready, 1)
                act.wait_ge(dn_ps, n + 1)
                if not (isinstance(i, int) and i == 0):
                    act.wait_ge(y_out[s], 16 * i)
                nc.scalar.copy(ybuf[:, s, :], ps[:, 3, :]).then_inc(y_ready, 1)

            experts(act, lambda i, s: work(NSLOT * i + s, s, i))
            blocks_past(act, lambda b: work(NE + b, 0, PRE[0] + b))
            for j in range(NT):
                act.wait_ge(acc_ready, j + 1)
                std(j, 6, x_sb[0:TOK[j], j, :], yfin[j][0:TOK[j], D:2 * D], std3)

        @block.vector
        def _(dve):
            steps = [0]

            def link(ins):
                steps[0] += 1
                ins.then_inc(dve_step, 1)
                dve.wait_ge(dve_step, steps[0])

            def tt(out, a, b, op):
                return nc.vector.tensor_tensor(out, a, b, op)

            def ts(out, a, s1, s2, op0, op1=ALU.bypass):
                return nc.vector.tensor_scalar(out, a, s1, s2, op0, op1)

            def stt(out, a, s, b, op0, op1):
                return nc.vector.scalar_tensor_tensor(out, a, s, b, op0, op1)

            def rstd(j):
                dve.wait_ge(std1, j + 1)
                nc.vector.reciprocal(small[0:TOK[j], 2, j:j + 1], small[0:TOK[j], 1, j:j + 1]).then_inc(rstd1, 1)

            def take_hT(j):
                n = TOK[j]
                for h in range(2):
                    dve.wait_ge(hT_ps, 2 * j + h + 1)
                    g1 = prmT[:, R_G1 + 4 * h:R_G1 + 4 * h + 4, None].broadcast_to([P, 4, n])
                    tt(hT[:, 4 * h:4 * h + 4, j * P:j * P + n],
                       ps[:, pair(j) + h, 0:4 * n].rearrange("p (k t) -> p k t", k=4), g1,
                       ALU.mult).then_inc(hT_ready, 1)

            def take_v(j):
                dve.wait_ge(v_ps, j + 1)
                nc.vector.tensor_copy(v_sb[0:TOK[j], j, :], ps[0:TOK[j], 4 + j % 2, 0:D_SGU]).then_inc(v_ready, 1)

            dve.wait_ge(consts_in, 16)
            rstd(0)
            dve.wait_ge(prm_ps, 1)
            nc.vector.tensor_copy(prmT[:], ps[:, 7, 0:R_ALL]).then_inc(prm_ready, 1)
            dve.wait_ge(prm_ready, 1)
            rstd(1)
            take_hT(0)
            rstd(2)
            take_hT(1)
            dve.wait_ge(wm_ps, 1)
            tt(wmT[:], ps[:, 6, :].rearrange("p (h i) -> p h i", h=HEADS),
               con("causal")[:, None, :].broadcast_to([P, HEADS, P]), ALU.mult).then_inc(wm_ready, 1)
            take_v(0)
            rstd(3)
            take_hT(2)
            take_v(1)
            rstd(4)
            take_hT(3)
            dve.wait_ge(zeroed, 3)
            nc.vector.tensor_copy(zc[:, :, ZC_S - CONV_HIST:ZC_S],
                                  prmT[:, R_SC:R_SP].rearrange("p (r q) -> p q r", q=3))
            nc.vector.tensor_copy(zp[:, :, ZP_S - POOL_HIST:ZP_S],
                                  prmT[:, R_SP:R_ALL].rearrange("p (r q) -> p q r", q=2)).then_inc(hist_ready, 1)
            take_v(2)
            take_hT(4)
            take_v(3)
            take_v(4)
            dve.wait_ge(hist_ready, 1)

            def pool(r):
                evacuated(dve, nth["p", r])
                z = zp[:, r, :]
                link(tt(win_a[:, 1:ZP], z[:, 1:ZP], z[:, 0:ZP - 1], ALU.add))
                low, up = slice(0, 64), slice(64, P)
                if r == 0:
                    link(tt(win_b[up, 3:ZP], win_a[up, 3:ZP], win_a[up, 1:ZP - 2], ALU.add))
                else:
                    link(tt(win_b[:, 3:ZP], win_a[:, 3:ZP], win_a[:, 1:ZP - 2], ALU.add))
                    link(tt(win_a[:, 7:ZP], win_b[:, 7:ZP], win_b[:, 3:ZP - 4], ALU.add))
                    link(tt(win_b[up, 15:ZP], win_a[up, 15:ZP], win_a[up, 7:ZP - 8], ALU.add))
                rc = con("rc15").rearrange("p (r i) -> p r i", r=2)
                for part, win in ((low, win_a), (up, win_b)):
                    link(stt(pooled[part, r, :], win[part, POOL_HIST:ZP], con("invw")[part, r:r + 1],
                             z[part, POOL_HIST:ZP], ALU.mult, ALU.subtract))
                    link(tt(win[part, POOL_HIST:2 * POOL_HIST], win[part, POOL_HIST:2 * POOL_HIST],
                            rc[part, r, :], ALU.mult))
                    last = tt(pooled[part, r, 0:POOL_HIST], win[part, POOL_HIST:2 * POOL_HIST],
                              z[part, POOL_HIST:2 * POOL_HIST], ALU.subtract)
                    if part == low:
                        link(last)
                last.then_inc(pooled_ready, 1)

            def sgu(q):
                dve.wait_ge(sgu_ps, q + 1)
                if q == 0:
                    dve.wait_ge(sgub_in, 96)
                tt(gated[:, 0:SEQ].rearrange("p (n i) -> p n i", n=4),
                   ps[:, 4 + q % 2, :].rearrange("p (n i) -> p n i", n=4),
                   bfull[:, q, None, :].broadcast_to([P, 4, P]), ALU.add)
                tt(gated[:, SEQ:T], ps[:, 6 + q % 2, 0:DEC], bfull[:, q, 0:DEC], ALU.add).then_inc(sgu_read, 1)
                dve.wait_ge(sgu_read, q + 1)
                evacuated(dve, nth["u", q])
                tt(mixT[:, 5 + q, :], mixT[:, 5 + q, :], gated[:], ALU.mult).then_inc(sgu_ready, 1)
                dve.wait_ge(sgu_ready, q + 1)

            def conv(q):
                n = nth["h", q]
                dve.wait_ge(proj_ps, n + 1)
                evacuated(dve, nth["c", q])
                for bank, a, b, t0, smp in segs:
                    at = CONV_HIST + t0 + smp * CONV_HIST
                    last = tt(zc[:, q, at:at + b - a], ps[:, pair(n) + bank, a:b], cbuf[:, t0:t0 + b - a], ALU.mult)
                last.then_inc(evac_dve, 1)
                dve.wait_ge(evac_dve, 2 * q + 1)
                z = zc[:, q, :]
                w = [prmT[:, R_CW + 3 * k + q:R_CW + 3 * k + q + 1] for k in range(3)]
                link(ts(yconv[:], z[:, 0:YC], w[0], None, ALU.mult))
                link(stt(yconv[:], z[:, 1:YC + 1], w[1], yconv[:], ALU.mult, ALU.add))
                link(stt(yconv[:], z[:, 2:YC + 2], w[2], yconv[:], ALU.mult, ALU.add))
                n = nth["b", q]
                dve.wait_ge(proj_ps, n + 1)
                for bank, a, b, t0, smp in segs:
                    at = t0 + smp * CONV_HIST
                    last = tt(mixT[:, q, t0:t0 + b - a], ps[:, pair(n) + bank, a:b], yconv[:, at:at + b - a], ALU.mult)
                last.then_inc(evac_dve, 1)

            pool(0)
            pool(1)
            for q in range(3):
                sgu(q)
            for q in range(3):
                conv(q)

            def take_L(j):
                n = TOK[j]
                dve.wait_ge(L_ps, j + 1)
                tt(L[0:n, j, :], ps[0:n, 6 + j % 2, 0:NG + NE], rbias[0:n, :], ALU.add).then_inc(L_ready, 1)

            link(nc.vector.memset(L[:], 0.0))
            dve.wait_ge(pool_ps, 2)
            nc.vector.memset(ones_b[:], 1.0)
            nc.vector.tensor_copy(tri_b[:], con("strict")).then_inc(tri_ready, 1)
            dve.wait_ge(g2_in, 16)
            dve.wait_ge(router_in, 64)
            for j in range(NT):
                n = TOK[j]
                dve.wait_ge(wo_ps, j + 1)
                tt(x_sb[0:n, j, :], ps[0:n, pair(j):pair(j) + 2, :].rearrange("p b n -> p (b n)"),
                   x_sb[0:n, j, :], ALU.add).then_inc(x2_ready, 1)
                dve.wait_ge(std2, j + 1)
                link(nc.vector.reciprocal(small[0:n, 5, j:j + 1], small[0:n, 4, j:j + 1]))
                if j >= 2:
                    dve.wait_ge(hn2_out[j % 2], 16 * (j // 2))
                    dve.wait_ge(hn2T_ps, 2 * (j - 1))
                stt(hn2p[0:n, j % 2, :].rearrange("t (k p) -> t k p", k=KD),
                    x_sb[0:n, j, :].rearrange("t (p k) -> t k p", k=KD), small[0:n, 5, j:j + 1],
                    g2b[0:n, :].rearrange("t (p k) -> t k p", k=KD), ALU.mult, ALU.mult).then_inc(hn2_ready, 1)
                if j >= 2:
                    take_L(j - 2)
            take_L(NT - 2)
            take_L(NT - 1)
            dve.wait_ge(L_ready, NT)

            mx, v1, v2, mark = (small[:, c, :] for c in (9, 10, 11, 12))
            psel, kdiff, kexp, w_hi = (small[:, c, :] for c in (13, 14, 15, 16))

            def over(x, shape):
                return x.broadcast_to(shape)

            def first_greatest(out, x, top, weights, tmp, n):
                link(tt(tmp, x, over(top[:, :, None], [P, NT, n]), ALU.is_equal))
                link(tt(tmp, tmp, over(weights[:, None, :], [P, NT, n]), ALU.mult))
                link(nc.vector.tensor_reduce(mark, tmp, AX.X, ALU.max))
                link(tt(out, tmp, over(mark[:, :, None], [P, NT, n]), ALU.is_equal))

            lc, lf = L[:, :, 0:NG], L[:, :, NG:].rearrange("p t (g e) -> p t g e", g=NG)
            link(nc.vector.tensor_reduce(mx, lc, AX.X, ALU.max))
            tt(t_g[:], lc, over(mx[:, :, None], [P, NT, NG]), ALU.subtract).then_inc(gdiff_ready, 1)
            first_greatest(oh_g[:], lc, mx, con("w4"), oh_g[:], NG)
            link(tt(t_ge[:], lf, over(oh_g[:, :, :, None], [P, NT, NG, EPG]), ALU.mult))
            link(nc.vector.tensor_reduce(sel[:], t_ge[:].rearrange("p t g e -> p t e g"), AX.X, ALU.add))
            link(nc.vector.tensor_reduce(v1, sel[:], AX.X, ALU.max))
            first_greatest(oh_k[:, :, 0, :], sel[:], v1, con("w8"), t_e[:], EPG)
            link(stt(sel[:], oh_k[:, :, 0, :], -3.0e38, sel[:], ALU.mult, ALU.add))
            link(nc.vector.tensor_reduce(v2, sel[:], AX.X, ALU.max))
            tt(kdiff, v2, v1, ALU.subtract).then_inc(kdiff_ready, 1)
            first_greatest(oh_k[:, :, 1, :], sel[:], v2, con("w8"), t_e[:], EPG)
            link(tt(oh_g[:], oh_g[:], over(con("valid")[:, :, None], [P, NT, NG]), ALU.mult))
            for k in range(2):
                link(tt(memb[:, :, k, :].rearrange("p t (g e) -> p t g e", g=NG),
                        over(oh_g[:, :, :, None], [P, NT, NG, EPG]),
                        over(oh_k[:, :, k, None, :], [P, NT, NG, EPG]), ALU.mult))
            link(tt(Mb[:], memb[:, :, 0, :], memb[:, :, 1, :], ALU.add))
            link(nc.vector.memset(Mc[:, 0, :], 0.0))
            for j in range(NT):
                last = tt(Mc[:, j + 1, :], Mc[:, j, :], Mb[:, j, :], ALU.add)
                if j < NT - 1:
                    link(last)
            last.then_inc(memb_ready, 1)
            dve.wait_ge(gexp_ready, 1)
            link(nc.vector.tensor_reduce(psel, e_g[:], AX.X, ALU.add))
            link(nc.vector.reciprocal(psel, psel))
            dve.wait_ge(kexp_ready, 1)
            link(ts(w_hi, kexp, 1.0, None, ALU.add))
            link(nc.vector.reciprocal(w_hi, w_hi))
            link(tt(gates[:, :, 0], psel, w_hi, ALU.mult))
            link(tt(gates[:, :, 1], gates[:, :, 0], kexp, ALU.mult))
            dve.wait_ge(pos_ps, 1)
            link(nc.vector.tensor_copy(pos[:].rearrange("p t e -> p (t e)"), ps[:, 7, 0:(NT + 1) * NE]))
            link(tt(t_j[:], over(pos[:, NT, :, None], [P, NE, MAX_J]), over(con("past")[:, None, :], [P, NE, MAX_J]),
                    ALU.is_gt))
            link(nc.vector.tensor_reduce(nblk[:, 0, :], t_j[:], AX.X, ALU.add))
            link(nc.vector.tensor_tensor_scan(nblk[:, 1, :], nblk[:, 0, :], nblk[:, 0, :], 0.0, ALU.add, ALU.bypass))
            link(tt(nblk[:, 2, :], nblk[:, 1, :], nblk[:, 0, :], ALU.subtract))
            link(ts(nblk[:, 2, :], nblk[:, 2, :], float(NE - 1), None, ALU.add))
            for c, x in ((0, over(pos[:, 0:NT, None, :], [P, NT, 2, NE])),
                         (1, over(con("expert")[:, None, None, :], [P, NT, 2, NE])),
                         (2, over(nblk[:, 2, None, None, :], [P, NT, 2, NE]))):
                link(tt(t_m[:], memb[:], x, ALU.mult))
                link(nc.vector.tensor_reduce(at_k[:, c, :], t_m[:].rearrange("p t k e -> p (t k) e"), AX.X, ALU.add))
            place, expert, past, j_k, d_k, s_k = (at_k[:, c, :] for c in range(6))
            link(tt(t_k[:], over(place[:, :, None], [P, NT * 2, MAX_J]),
                    over(con("past")[:, None, :], [P, NT * 2, MAX_J]), ALU.is_ge))
            link(nc.vector.tensor_reduce(j_k, t_k[:], AX.X, ALU.add))
            link(stt(s_k, j_k, -float(BLK), place, ALU.mult, ALU.add))
            link(tt(past, past, expert, ALU.subtract))
            link(stt(d_k, j_k, 1.0, past, ALU.min, ALU.mult))
            link(tt(d_k, d_k, expert, ALU.add))
            link(tt(d_k, d_k, j_k, ALU.add))
            dve.wait_ge(hn2_out[0], 48)
            dve.wait_ge(hn2_out[1], 32)
            dve.wait_ge(L_ps, NT)
            tt(onehot_s[:], over(con("iota_pos")[:, None, :], [P, NT * 2, BLK]),
               over(s_k[:, :, None], [P, NT * 2, BLK]), ALU.is_equal)
            link(tt(onehot_c[:], over(con("iota_col")[:, None, :], [P, NT * 2, NCOL]),
                    over(d_k[:, :, None], [P, NT * 2, NCOL]), ALU.is_equal))
            tt(onehot_v[:], over(onehot_c[:, :, None, :], [P, NT * 2, 3, NCOL]),
               over(con("vals").rearrange("p (t c) -> p t c", c=3)[:, :, :, None], [P, NT * 2, 3, NCOL]),
               ALU.mult).then_inc(onehot_ready, 1)
            link(tt(t_o[:], over(nblk[:, 1, None, :], [P, NOV, NE]), over(con("ovnum")[:, :, None], [P, NOV, NE]),
                    ALU.is_le))
            link(nc.vector.tensor_reduce(small[:, 17:21, :].rearrange("p a b -> p (a b)")[:, 0:NOV], t_o[:], AX.X,
                                         ALU.add))
            nc.vector.tensor_copy(ovexp[:], small[:, 17:21, :].rearrange("p a b -> p (a b)")[:, 0:NOV])
            nc.vector.tensor_copy(nov[:], nblk[:, 1, NE - 1:NE]).then_inc(nov_ready, 1)
            dve.wait_ge(idx_ps, 1)
            link(nc.vector.tensor_copy(t_x[:, 0:3, :], ps[:, 6, 0:3 * NCOL].rearrange("p (c n) -> p c n", c=3)))
            hi, lo, kk, a_x, a_p = (t_x[:, c, :] for c in range(5))
            link(stt(a_x, hi, 32.0, lo, ALU.mult, ALU.add))
            link(ts(a_p, a_x, 0.0, PAD - 2.0, ALU.is_equal, ALU.mult))
            link(ts(a_x, a_x, 2.0, con("half"), ALU.mult, ALU.add))
            link(tt(a_x, a_x, a_p, ALU.add))
            link(ts(a_x, a_x, -2.0, None, ALU.add))
            link(ts(kk, kk, 2.0, con("half"), ALU.mult, ALU.subtract))
            nc.vector.tensor_copy(idx_x[:], a_x)
            stt(idx_y[:], a_x, 2.0, kk, ALU.mult, ALU.add).then_inc(idx_ready, 1)

            def work(n):
                dve.wait_ge(xT_ps, n + 1)
                nc.vector.tensor_copy(xT[:].rearrange("p c s -> p (c s)"), ps[:, 0, :]).then_inc(xT_ready, 1)

            def work_h(n):
                dve.wait_ge(silu_ready, n + 1)
                tt(hexp[:], silu_g[:], ps[:, 1, F // 2:F], ALU.mult).then_inc(h_exp, 1)

            def work_hT(n):
                dve.wait_ge(hexT_ps, n + 1)
                nc.vector.tensor_copy(hexT[:].rearrange("p c s -> p (c s)"), ps[:, 2, 0:2 * P]).then_inc(hexT_ready, 1)

            work(0)

            def turn(i, s, more=True):
                n = NSLOT * i + s
                work_h(n)
                if more:
                    work(n + 1)
                work_hT(n)

            experts(dve, lambda i, s: turn(i, s, not (isinstance(i, int) and NSLOT * i + s == NE - 1)))

            def block_past(b):
                work(NE + b)
                work_h(NE + b)
                work_hT(NE + b)

            blocks_past(dve, block_past)

            dve.wait_ge(gf_in, 16)

            def finish(j):
                n = TOK[j]
                dve.wait_ge(std3, j + 1)
                link(nc.vector.reciprocal(small[0:n, 8, j:j + 1], small[0:n, 7, j:j + 1]))
                stt(yfin[j][0:n, 0:D], x_sb[0:n, j, :], small[0:n, 8, j:j + 1], gfb[0:n, :], ALU.mult,
                    ALU.mult).then_inc(out_ready, 1)

            for j in range(NT):
                n = TOK[j]
                dve.wait_ge(yfin_in[j], 16)
                link(stt(x_sb[0:n, j, :], yfin[j][0:n, 0:D], gates[0:n, j, 0:1], x_sb[0:n, j, :], ALU.mult, ALU.add))
                stt(x_sb[0:n, j, :], yfin[j][0:n, D:2 * D], gates[0:n, j, 1:2], x_sb[0:n, j, :], ALU.mult,
                    ALU.add).then_inc(acc_ready, 1)
                if j:
                    finish(j - 1)
            finish(NT - 1)

        @block.tensor
        def _(pe):
            mm = nc.tensor.matmul

            pe.wait_ge(consts_in, 16)

            def transpose_h(j):
                n = TOK[j]
                pe.wait_ge(h_ready, j + 1)
                if j >= 2:
                    pe.wait_ge(hT_ready, 2 * (j - 1))
                for h in range(2):
                    for k in range(4):
                        last = nc.tensor.transpose(ps[:, pair(j) + h, k * n:(k + 1) * n],
                                                   hstage[0:n, j % 2, (4 * h + k) * P:(4 * h + k + 1) * P],
                                                   ident[0:n, 0:n])
                    last.then_inc(hT_ps, 1)

            def product_v(j):
                n = TOK[j]
                pe.wait_ge(hT_ready, 2 * (j + 1))
                if j == 0:
                    pe.wait_ge(wi_in["v"], 16)
                if j >= 2:
                    pe.wait_ge(v_ready, j - 1)
                for k in range(KD):
                    last = mm(ps[0:n, 4 + j % 2, 0:D_SGU], hT[:, k, j * P:j * P + n], wi[:, k, COL_V:COL_V + D_SGU],
                              start=(k == 0), stop=(k == KD - 1))
                last.then_inc(v_ps, 1)

            transpose_h(0)
            pe.wait_ge(params_in, 80)
            nc.tensor.transpose(ps[:, 7, 0:R_ALL], prm[0:R_ALL, :], ident[0:R_ALL, 0:R_ALL]).then_inc(prm_ps, 1)
            transpose_h(1)
            pe.wait_ge(sguw_in, 16)
            for head in range(HEADS):
                last = nc.tensor.transpose(ps[:, 6, head * P:(head + 1) * P], sguw[:, head, :], ident)
            last.then_inc(wm_ps, 1)
            product_v(0)
            for j in range(2, NT):
                transpose_h(j)
                product_v(j - 1)
            product_v(NT - 1)

            def product(g, q):
                n = nth[g, q]
                if q == 0:
                    pe.wait_ge(wi_in[g], 16)
                if n >= 2:
                    evacuated(pe, n - 2)
                col = COLS[g] + q * P
                for k in range(KD):
                    for bank, a, b in halves:
                        last = mm(ps[:, pair(n) + bank, 0:b - a], wi[:, k, col:col + P], hT[:, k, a:b],
                                  start=(k == 0), stop=(k == KD - 1))
                last.then_inc(proj_ps, 1)

            def mix_positions(q):
                if q == 0:
                    pe.wait_ge(v_ready, NT)
                    pe.wait_ge(wm_ready, 1)
                    pe.wait_ge(prm_ready, 1)
                if q >= 2:
                    pe.wait_ge(sgu_read, q - 1)
                for t in range(NT):
                    n = TOK[t]
                    for qq, at, size, head, ch in pieces:
                        if qq != q:
                            continue
                        out = ps[at:at + size, 4 + q % 2, t * P:(t + 1) * P] if t < 4 else \
                            ps[at:at + size, 6 + q % 2, 0:DEC]
                        last = mm(out, v_sb[0:n, t, ch:ch + size], wmT[0:n, head, 0:n], start=True, stop=True)
                last.then_inc(sgu_ps, 1)

            def mix_pooled(r):
                pe.wait_ge(pooled_ready, r + 1)
                if r == 0:
                    pe.wait_ge(poolw_in, 64)
                    pe.wait_ge(sgu_read, 3)
                else:
                    pe.wait_ge(pool_ready, r)
                mm(ps[:, 6, 0:PO_A], pool_wbd[:, r, :], pooled[:, r, 0:PO_A], start=True, stop=True)
                mm(ps[:, 7, 0:PO - PO_A], pool_wbd[:, r, :], pooled[:, r, PO_A:PO], start=True,
                   stop=True).then_inc(pool_ps, 1)

            product("p", 0)
            product("p", 1)
            for q in range(3):
                product("u", q)
                mix_positions(q)
            product("c", 0)
            mix_pooled(0)
            product("h", 0)
            mix_pooled(1)
            product("b", 0)
            for q in (1, 2):
                for g in "chb":
                    product(g, q)
            pe.wait_ge(st_ready, 1)
            pe.wait_ge(pool_ready, 2)
            for q in range(3):
                nc.tensor.transpose(ps[0:4, 7, q * P:(q + 1) * P], convst[:, q, :], ident)
            for r in range(2):
                last = nc.tensor.transpose(ps[0:2 * POOL_HIST, 6, r * P:(r + 1) * P], poolst[:, r, :], ident)
            last.then_inc(st_ps, 1)

            def output(j):
                n = TOK[j]
                if j == 0:
                    pe.wait_ge(wo_in, 16)
                    pe.wait_ge(sgu_ready, 3)
                    pe.wait_ge(evac_dve, 6)
                if j >= 2:
                    pe.wait_ge(x2_ready, j - 1)
                for k in range(KD):
                    for half in range(2):
                        last = mm(ps[0:n, pair(j) + half, :], mixT[:, k, j * P:j * P + n],
                                  wo[:, k, half * 512:(half + 1) * 512], start=(k == 0), stop=(k == KD - 1))
                last.then_inc(wo_ps, 1)

            def transpose_hn2(j):
                n = TOK[j]
                pe.wait_ge(hn2_ready, j + 1)
                for h in range(2):
                    if j:
                        pe.wait_ge(hn2T_ready, 2 * (j - 1) + h + 1)
                    for k in range(4):
                        last = nc.tensor.transpose(ps[:, 4 + h, k * n:(k + 1) * n],
                                                   hn2p[0:n, j % 2, (4 * h + k) * P:(4 * h + k + 1) * P],
                                                   ident[0:n, 0:n])
                    last.then_inc(hn2T_ps, 1)

            def logits(j):
                n = TOK[j]
                pe.wait_ge(hn2T_ready, 2 * (j + 1))
                if j == 0:
                    pe.wait_ge(router_in, 64)
                    pe.wait_ge(st_rows, 2)
                if j >= 2:
                    pe.wait_ge(L_ready, j - 1)
                for k in range(KD):
                    last = mm(ps[0:n, 6 + j % 2, 0:NG + NE], hn2T[:, k, 0:n], rw[:, k, :], start=(k == 0),
                              stop=(k == KD - 1))
                last.then_inc(L_ps, 1)

            output(0)
            output(1)
            transpose_hn2(0)
            output(2)
            logits(0)
            transpose_hn2(1)
            output(3)
            logits(1)
            transpose_hn2(2)
            output(4)
            logits(2)
            transpose_hn2(3)
            logits(3)
            transpose_hn2(4)
            logits(4)

            pe.wait_ge(memb_ready, 1)
            pe.wait_ge(tri_ready, 1)
            mm(ps[:, 7, 0:(NT + 1) * NE], ones_b[:], Mc[:].rearrange("p t e -> p (t e)"), start=True, stop=False)
            mm(ps[:, 7, 0:NT * NE], tri_b[:], Mb[:].rearrange("p t e -> p (t e)"), start=False,
               stop=True).then_inc(pos_ps, 1)
            pe.wait_ge(onehot_ready, 1)
            for i in range(2 * NT):
                for h in range(2):
                    last = mm(ps[64 * h:64 * h + 64, 6, 0:3 * NCOL], onehot_s[:, i, :],
                              onehot_v[:, i, :, :].rearrange("p c n -> p (c n)"), start=(i == 0),
                              stop=(i == 2 * NT - 1))
            last.then_inc(idx_ps, 1)

            def transpose_x(s, uses):
                pe.wait_ge(xg_in[s], 16 * uses)
                for c in range(KD // 2):
                    last = nc.tensor.transpose(ps[:, 0, c * P:(c + 1) * P], xg[:, s, c * P:(c + 1) * P], ident)
                last.then_inc(xT_ps, 1)

            def gate_up(n, s, uses):
                pe.wait_ge(xT_ready, n + 1)
                pe.wait_ge(w1_in[s], 32 * uses)
                for k in range(KD):
                    lhs = xT[:, k % 4, 64 * (k // 4):64 * (k // 4) + 64]
                    for h in range(2):
                        last = mm(ps[64 * h:64 * h + 64, 1, :], lhs, w1[s][:, :, k, h * (F // 2):(h + 1) * (F // 2)],
                                  start=(k == 0), stop=(k == KD - 1))
                last.then_inc(gu_ps, 1)

            def transpose_act(n):
                pe.wait_ge(h_exp, n + 1)
                for c in range(2):
                    last = nc.tensor.transpose(ps[:, 2, c * P:(c + 1) * P], hexp[:, c * P:(c + 1) * P], ident)
                last.then_inc(hexT_ps, 1)

            def down(n, s, uses):
                pe.wait_ge(hexT_ready, n + 1)
                pe.wait_ge(wd_in[s], 16 * uses)
                if not (isinstance(n, int) and n == 0):
                    pe.wait_ge(y_ready, n)
                for c in range(F // P):
                    lhs = hexT[:, c % 2, 64 * (c // 2):64 * (c // 2) + 64]
                    for h in range(2):
                        last = mm(ps[64 * h:64 * h + 64, 3, :], lhs, wd[s][:, c, h * 512:(h + 1) * 512],
                                  start=(c == 0), stop=(c == F // P - 1))
                last.then_inc(dn_ps, 1)

            transpose_x(0, 1)

            def turn(i, s, more=True):
                n = NSLOT * i + s
                gate_up(n, s, i + 1)
                if more:
                    transpose_x((s + 1) % NSLOT, i + 1 + (s + 1) // NSLOT)
                transpose_act(n)
                down(n, s, i + 1)

            experts(pe, lambda i, s: turn(i, s, not (isinstance(i, int) and NSLOT * i + s == NE - 1)))

            def block_past(b):
                transpose_x(0, PRE[0] + b + 1)
                gate_up(NE + b, 0, PRE[0] + b + 1)
                transpose_act(NE + b)
                down(NE + b, 0, PRE[0] + b + 1)

            blocks_past(pe, block_past)


_INS = ["x_prompt", "x_sample", "state_conv", "state_pool", "norm1_g", "w_in", "conv_w", "pool_w", "pool_scale",
        "sgu_w", "sgu_b", "w_out", "norm2_g", "router_coarse_w", "router_coarse_b", "router_fine_w",
        "router_fine_b", "moe_w_gate", "moe_w_up", "moe_w_down", "final_norm_g"]
_OUTS = [(1, SEQ, D), (1, DEC, D), (1, 1, CONV_HIST, D_CONV), (1, 1, POOL_HIST, D_POOL),
         (1, 1, CONV_HIST, D_CONV), (1, 1, POOL_HIST, D_POOL), (1, 1, DEC, D_SGU)]


def kernel(**inputs):
    import numpy as np
    import concourse.bacc as bacc
    from concourse.bass_utils import run_bass_kernel_spmd

    nc = bacc.Bacc("TRN2", target_bir_lowering=False, num_devices=1)
    arrays, args = {}, []
    for name in _INS:
        a = np.ascontiguousarray(inputs[name])
        arrays[f"in_{name}"] = a
        args.append(nc.dram_tensor(f"in_{name}", a.shape, mybir.dt.from_np(a.dtype), kind="ExternalInput").ap())
    arrays["in_constants"] = constant_tile()
    args.append(nc.dram_tensor("in_constants", (P, NCONST), F32, kind="ExternalInput").ap())
    for i, shape in enumerate(_OUTS):
        args.append(nc.dram_tensor(f"out_{i}", shape, F32, kind="ExternalOutput").ap())
    build(nc, *args)
    r = run_bass_kernel_spmd(nc, [arrays], core_ids=[0])
    return tuple(r.results[0][f"out_{i}"] for i in range(len(_OUTS)))
```

```python
import concourse.bass as bass
from concourse import mybir
from concourse.alu_op_type import AluOpType as ALU

F32 = mybir.dt.float32
BF16 = mybir.dt.bfloat16
F32R = mybir.dt.float32r
I32 = mybir.dt.int32
ACT = mybir.ActivationFunctionType
AX = mybir.AxisListType

P = 128
D = 1024
KD = D // P
SEQ, DEC = 512, 64
T = SEQ + DEC
NT = 5
TOK = [P, P, P, P, DEC]
D_CONV, D_POOL, D_SGU = 384, 256, 384
CONV_HIST, POOL_HIST = 2, 15
D_PROJ = 3 * D_CONV + D_POOL + 2 * D_SGU
COL_B, COL_C, COL_H = 0, D_CONV, 2 * D_CONV
COL_P = 3 * D_CONV
COL_U = COL_P + D_POOL
COL_V = COL_U + D_SGU
HEADS, HEAD_DIM = 4, D_SGU // 4
NG, EPG, NE = 4, 8, 32
F = 512
EPS = 1e-6
HT = T // 2

ZC = CONV_HIST + SEQ + CONV_HIST + DEC
ZC_S = CONV_HIST + SEQ + CONV_HIST
YC = ZC - CONV_HIST
YC_S = SEQ + CONV_HIST
ZP = POOL_HIST + SEQ + POOL_HIST + DEC
ZP_S = POOL_HIST + SEQ + POOL_HIST
PO = ZP - POOL_HIST
PO_S = SEQ + POOL_HIST
PO_A = 296

R_CW, R_PS, R_SC, R_SP, R_ALL = 0, 9, 11, 17, 47

BLK = 64
MAX_J = T // BLK - 1
NOV = 2 * T // BLK
NCOL = NE + NOV
NSLOT = 3
PRE = [(NE - s + NSLOT - 1) // NSLOT for s in range(NSLOT)]
ROUNDS = NE // NSLOT
OUTSIDE = 4096

CONSTS = {}
_at = 0
for _name, _n in (("ident", P), ("causal", P), ("strict", P), ("iota_pos", BLK),
                  ("w4", NG), ("w8", EPG), ("vals", 4 * NT), ("two", NT), ("base", 1), ("invw", 2),
                  ("rc15", 2 * POOL_HIST), ("expert", NE), ("past", MAX_J), ("ovnum", NOV), ("eps", 1)):
    CONSTS[_name] = (_at, _at + _n)
    _at += _n
NCONST = _at


def constant_tile():
    import numpy as np
    c = np.zeros((P, NCONST), np.float32)
    p = np.arange(P)

    def put(name, value):
        a, b = CONSTS[name]
        c[:, a:b] = value

    put("ident", np.eye(P))
    put("causal", p[:, None] <= p[None, :])
    put("strict", p[:, None] < p[None, :])
    put("iota_pos", np.arange(BLK))
    put("w4", np.arange(NG, 0, -1))
    put("w8", np.arange(EPG, 0, -1))
    vals = np.zeros((P, NT, 2, 2))
    for t in range(NT):
        for k in range(2):
            vals[:TOK[t], t, k, 0] = 2 * (t * P + p[:TOK[t]]) - OUTSIDE
            vals[:TOK[t], t, k, 1] = 2 * (2 * (t * P + p[:TOK[t]]) + k) - OUTSIDE
    put("vals", vals.reshape(P, -1))
    put("two", np.array([[2.0 * (i < TOK[t]) for t in range(NT)] for i in range(P)]))
    put("base", OUTSIDE + (p >= 64)[:, None])
    win = np.array([[2, 8], [4, 16]])[(p >= 64).astype(int)]
    put("invw", 1.0 / win)
    put("rc15", (1.0 / np.minimum(win[:, :, None], np.arange(1, POOL_HIST + 1))).reshape(P, -1))
    put("expert", np.arange(NE))
    put("past", BLK * np.arange(1, MAX_J + 1))
    put("ovnum", np.arange(NOV))
    put("eps", EPS)
    return c


PIECE = 32


def build(nc, x_prompt, x_sample, state_conv, state_pool, norm1_g, w_in, conv_w, pool_w, pool_scale,
          sgu_w, sgu_b, w_out, norm2_g, rc_w, rc_b, rf_w, rf_b, w_gate, w_up, w_down, final_g, consts,
          y_prompt, y_sample, new_conv_prompt, new_pool_prompt, new_conv_sample, new_pool_sample,
          new_sgu_v):
    hn2_rows = nc.dram_tensor("hn2_rows", [2 * T, D // 2], F32, kind="Internal").ap()
    y_rows = nc.dram_tensor("y_rows", [4 * T, D // 2], F32, kind="Internal").ap()

    W1_BYTES, WD_BYTES = 2 * KD * F * 4, (F // P) * D * 4
    SLOT_BYTES = W1_BYTES + WD_BYTES
    first = (nc.sbuf_base + 31) // 32 * 32
    slot_at = [first + s * SLOT_BYTES for s in range(NSLOT + 1)]
    where = {}

    def region(start, end):
        at = [start]

        def place(name, shape, dt=F32):
            n = 2 if dt == BF16 else 4
            for x in shape[1:]:
                n *= x
            t = nc.alloc_sbuf_tensor_at(name, shape, dt, offset=at[0])
            where[name] = at[0]
            at[0] += (n + 31) // 32 * 32
            where["end"] = at[0]
            assert at[0] <= end, (name, at[0] - end)
            return t
        return place

    w1, wd = [], []
    for s in range(NSLOT):
        slot = region(slot_at[(s + 2) % 3], slot_at[(s + 2) % 3 + 1])
        w1.append(slot(f"w1_{s}", [P, 2, KD, F]))
        wd.append(slot(f"wd_{s}", [P, F // P, D]))

    early = region(slot_at[0], slot_at[3])
    wi, wi_lo = {}, {}
    WIDTH = {"v": D_SGU, "p": D_POOL, "u": D_SGU, "c": D_CONV, "h": D_CONV, "b": D_CONV}

    def columns(g):
        wi[g] = early(f"wi_{g}", [P, KD, WIDTH[g]])
        wi_lo[g] = nc.alloc_sbuf_tensor_at(f"wi_lo_{g}", [P, KD, WIDTH[g]], F32R, offset=where[f"wi_{g}"])

    for g in "vpuch":
        columns(g)
    v_hi_at = where["end"]
    early("gap", [P, 2, D])
    columns("b")
    hT_hi = early("hT_hi", [P, KD, T], F32R)
    wi_hi = early("wi_hi", [P, 3, KD, P], F32R)
    hT_lo = early("hT_lo", [P, KD, T], F32R)
    zc = early("zc", [P, 3, ZC])
    v_sb = early("v_sb", [P, NT, D_SGU])
    gated = early("gated", [P, T])
    pool_wbd = early("pool_wbd", [P, 2, P])
    wmT = early("wmT", [P, HEADS, P])
    convst = early("convst", [P, 3, 4])
    poolst = early("poolst", [P, 2, 2 * POOL_HIST])
    wi_hi_v = nc.alloc_sbuf_tensor_at("wi_hi_v", [P, KD, D_SGU], F32R, offset=v_hi_at)
    wo = nc.alloc_sbuf_tensor_at("wo", [P, KD, D], F32, offset=where["wi_v"])
    wo_lo = nc.alloc_sbuf_tensor_at("wo_lo", [P, KD, D], F32R, offset=where["wi_v"])
    wo_hi = nc.alloc_sbuf_tensor_at("wo_hi", [P, KD, D], F32R, offset=where["wi_c"])
    assert where["wi_c"] - where["wi_v"] == KD * D * 4 == where["wi_b"] - where["wi_c"]
    mix_hi = nc.alloc_sbuf_tensor_at("mix_hi", [P, KD, T], F32R, offset=where["hT_hi"])
    assert where["hT_hi"] + KD * T * 4 <= slot_at[2]
    late = region(where["v_sb"], where["gated"])
    conv_rows = late("conv_rows", [P, D_CONV])
    pool_rows = late("pool_rows", [P, D_POOL])

    rest = region(slot_at[3], nc.sbuf_usable_end)
    x_sb = rest("x_sb", [P, NT, D])
    mixT = rest("mixT", [P, KD, T])
    mixT_lo = nc.alloc_sbuf_tensor_at("mixT_lo", [P, KD, T], F32R, offset=where["mixT"])
    zp = rest("zp", [P, 2, ZP])
    win_a = rest("win_a", [P, ZP])
    win_b = rest("win_b", [P, ZP])
    pooled = rest("pooled", [P, 2, PO])
    pool_end = where["end"]
    cst = rest("cst", [P, NCONST])
    gain = rest("gain", [P, D])
    rw = rest("rw", [P, KD, NG + NE])
    rbias = rest("rbias", [P, NG + NE])
    bfull = rest("bfull", [P, 3, P])
    prmT = rest("prmT", [P, R_ALL])
    small = rest("small", [P, 30, NT])
    gates = rest("gates", [P, NT, 2])
    L = rest("L", [P, NT, NG + NE])
    idx = rest("idx", [P, 2, NCOL], I32)
    ovexp = rest("ovexp", [P, NOV], I32)
    nov = rest("nov", [P, 1], I32)
    idc_x = rest("idc_x", [P, NSLOT], I32)
    idc_y = rest("idc_y", [P, NSLOT], I32)
    pre = region(where["mixT"], where["zp"])
    hstage = pre("hstage", [P, 2, D])
    sguw = pre("sguw", [P, HEADS, P])
    prm = pre("prm", [P, P])
    post = region(where["mixT"], where["zp"])
    xT = post("xT", [P, KD // 2, P])
    silu_g = post("silu_g", [P, F // 2])
    hexp = post("hexp", [P, F // 2])
    hexT = post("hexT", [P, 2, P])
    t_g = post("t_g", [P, NT, NG])
    e_g = post("e_g", [P, NT, NG])
    oh_g = post("oh_g", [P, NT, NG])
    t_ge = post("t_ge", [P, NT, NG, EPG])
    sel = post("sel", [P, NT, EPG])
    t_e = post("t_e", [P, NT, EPG])
    oh_k = post("oh_k", [P, NT, 2, EPG])
    oh_both = post("oh_both", [P, NT, EPG])
    vals = post("vals", [P, NT, 2, 2])
    memb = post("memb", [P, NT, 2, NE])
    Mb = post("Mb", [P, NT + 1, NE], BF16)
    onehot_v = post("onehot_v", [P, NT * 2, 2, NE], F32R)
    t_m = post("t_m", [P, NT, 2, NE])
    t_j = post("t_j", [P, NE, MAX_J])
    nblk = post("nblk", [P, 3, NE])
    t_o = post("t_o", [P, NOV, NE])
    at_k = post("at_k", [P, 5, NT * 2])
    t_k = post("t_k", [P, NT * 2, MAX_J])
    p1 = region(where["zp"], pool_end)
    cbuf = p1("cbuf", [P, 3, T])
    junk = nc.alloc_sbuf_tensor_at("junk", [P, D], F32, offset=where["win_a"])
    yconv = p1("yconv", [P, 3, YC])
    p2 = region(where["zp"], pool_end)
    hn2p = p2("hn2p", [P, 2, D])
    hn2T = p2("hn2T", [P, KD, P])
    tri_b = p2("tri_b", [P, P], BF16)
    ones_b = p2("ones_b", [P, P], BF16)
    p3 = region(where["zp"], pool_end)
    xg = p3("xg", [P, NSLOT, D // 2])
    ybuf = p3("ybuf", [P, NSLOT, D // 2])
    p4 = region(where["ybuf"], pool_end)
    onehot_s = p4("onehot_s", [P, NT * 2, 2, BLK], F32R)
    onehot_c = p4("onehot_c", [P, NT * 2, NOV])
    onehot_p = p4("onehot_p", [P, NT * 2, 2, NOV], F32R)
    p5 = region(slot_at[1], slot_at[2])
    yfin = [p5(f"yfin{i}", [P, 2 * D]) for i in range(NT)]

    ps = nc.alloc_psum_tensor("ps", [P, 8, 512], F32)

    def con(name):
        a, b = CONSTS[name]
        return cst[:, a:b]

    ident = con("ident")

    sem = nc.alloc_semaphore
    consts_in, params_in, sguw_in, sgub_in = sem("consts_in"), sem("params_in"), sem("sguw_in"), sem("sgub_in")
    x_in = [sem(f"x_in{j}") for j in range(NT)]
    wi_in = {g: sem(f"wi_in_{g}") for g in "vpuchb"}
    v_hi, v_lo, wi_hi_ready, wi_lo_ready = sem("v_hi"), sem("v_lo"), sem("wi_hi_ready"), sem("wi_lo_ready")
    hT_hi_ready, hT_lo_ready = sem("hT_hi_ready"), sem("hT_lo_ready")
    wo_hi_ready, wo_lo_ready, mix_hi_ready, mix_lo_ready = (sem("wo_hi_ready"), sem("wo_lo_ready"),
                                                            sem("mix_hi_ready"), sem("mix_lo_ready"))
    g1_in = sem("g1_in")
    poolw_in, g2_in, router_in, wo_in, gf_in = (sem("poolw_in"), sem("g2_in"), sem("router_in"),
                                                sem("wo_in"), sem("gf_in"))
    zeroed, tri_ready = sem("zeroed"), sem("tri_ready")
    prm_ps, prm_ready, wm_ps, wm_ready = sem("prm_ps"), sem("prm_ready"), sem("wm_ps"), sem("wm_ready")
    hist_ready = sem("hist_ready")
    warm, std1, h_ready, hT_ps = sem("warm"), sem("std1"), sem("h_ready"), sem("hT_ps")
    v_ps, v_ready = sem("v_ps"), sem("v_ready")
    proj_ps, evac_act, evac_dve = sem("proj_ps"), sem("evac_act"), sem("evac_dve")
    sgu_ps, sgu_read, sgu_ready = sem("sgu_ps"), sem("sgu_read"), sem("sgu_ready")
    pooled_ready, pool_ps, pool_ready = sem("pooled_ready"), sem("pool_ps"), sem("pool_ready")
    st_ready, st_ps, st_rows, st_out = sem("st_ready"), sem("st_ps"), sem("st_rows"), sem("st_out")
    wo_ps, x2_ready, std2, hn2_ready = sem("wo_ps"), sem("x2_ready"), sem("std2"), sem("hn2_ready")
    hn2_out = [sem("hn2_out0"), sem("hn2_out1")]
    hn2T_ps, hn2T_ready, L_ps, L_ready = sem("hn2T_ps"), sem("hn2T_ready"), sem("L_ps"), sem("L_ready")
    gdiff_ready, gexp_ready, kdiff_ready, kexp_ready = (sem("gdiff_ready"), sem("gexp_ready"),
                                                        sem("kdiff_ready"), sem("kexp_ready"))
    memb_ready, pos_ps, onehot_ready, idx_ps, idx_ready, nov_ready = (
        sem("memb_ready"), sem("pos_ps"), sem("onehot_ready"), sem("idx_ps"), sem("idx_ready"),
        sem("nov_ready"))
    xg_zero = sem("xg_zero")
    w1_in = [[sem(f"w1_in{s}_{half}") for half in range(2)] for s in range(NSLOT)]
    wd_in = [sem(f"wd_in{s}") for s in range(NSLOT)]
    xg_in = [sem(f"xg_in{s}") for s in range(NSLOT)]
    y_out = [sem(f"y_out{s}") for s in range(NSLOT)]
    idc_ready = sem("idc_ready")
    idc_seen = sem("idc_seen")
    xT_ps, xT_ready, gu_ps, silu_ready, h_exp = (sem("xT_ps"), sem("xT_ready"), sem("gu_ps"),
                                                 sem("silu_ready"), sem("h_exp"))
    hexT_ps, hexT_ready, dn_ps, y_ready = sem("hexT_ps"), sem("hexT_ready"), sem("dn_ps"), sem("y_ready")
    yfin_in = [[sem(f"yfin_in{k}_{j}") for j in range(NT)] for k in range(2)]
    acc_ready, std3, rstd3, unit_ready, out_ready, y_done = (sem("acc_ready"), sem("std3"), sem("rstd3"),
                                                             sem("unit_ready"), [sem(f"out_ready{j}") for j in range(NT)],
                                                             sem("y_done"))
    dve_step, act_step = sem("dve_step"), sem("act_step")

    CHUNKS = [("p", 0), ("p", 1)] + [(g, q) for g in "uchb" for q in range(3)]
    NCH = len(CHUNKS)
    MIX_ORDER = (6, 7, 5, 3, 4, 0, 1, 2)
    WO_ORDER = ((6, 5), (7, 5), (0, 8), (1, 8), (2, 8), (3, 11), (4, 11), (5, 11))
    nth = {ch: n for n, ch in enumerate(CHUNKS)}
    ON_ACT = "puc"

    BY_POOL = (0, 1)

    def evacuated(eng, n):
        mine = CHUNKS[n][0] in ON_ACT
        count = sum((g in ON_ACT) == mine for g, _ in CHUNKS[:n + 1])
        eng.wait_ge(evac_act if mine else evac_dve, count)

    def pair(n):
        return 2 * (n % 2)

    halves = ((0, 0, HT), (1, HT, T))
    segs = ((0, 0, HT, 0, 0), (1, 0, SEQ - HT, HT, 0), (1, SEQ - HT, HT, SEQ, 1))

    def experts(eng, body, last=ROUNDS):
        for s in range(NSLOT):
            body(0, s)
        with eng.Fori(1, last) as i:
            for s in range(NSLOT):
                body(i, s)
        for n in range(NSLOT * last, NE):
            body(n // NSLOT, n % NSLOT)

    def blocks_past(eng, body):
        eng.wait_ge(nov_ready, 1)
        count = eng.value_load(nov[0:1, 0:1], min_val=0, max_val=NOV)
        with eng.If(count > 0):
            with eng.Fori(0, count) as b:
                body(b)
        return count

    with nc.Block() as block:

        @block.sync
        def _(sp):
            x_rows = [x_prompt[0, j * P:(j + 1) * P, :] for j in range(4)] + [x_sample[0]]
            wi_v = w_in[0].rearrange("(k p) n -> p k n", p=P)

            def load_wi(g, a, n):
                sp.dma_start(wi[g][:], wi_v[:, :, a:a + n]).then_inc(wi_in[g], 16)

            def load_x(j):
                sp.dma_start(x_sb[0:TOK[j], j, :], x_rows[j]).then_inc(x_in[j], 16)

            load_x(0)
            sp.dma_start(cst[:], consts).then_inc(consts_in, 16)
            sp.dma_start(gain[:], norm1_g[0:1, :].broadcast_to([P, D])).then_inc(g1_in, 16)
            load_x(1)
            load_wi("v", COL_V, D_SGU)
            for j in range(2, NT):
                load_x(j)
            sp.dma_start(sguw[:], sgu_w[0].rearrange("h i j -> i h j")).then_inc(sguw_in, 16)
            sp.dma_start(prm[R_CW:R_PS, :], conv_w[0].rearrange("k (q p) -> (k q) p", p=P)).then_inc(params_in, 16)
            sp.dma_start(prm[R_PS:R_SC, :], pool_scale[0].rearrange("(q p) -> q p", p=P)).then_inc(params_in, 16)
            sp.dma_start(prm[R_SC:R_SP, :], state_conv[0, 0].rearrange("r (q p) -> (r q) p", p=P)).then_inc(params_in, 16)
            sp.dma_start(prm[R_SP:R_ALL, :], state_pool[0, 0].rearrange("r (q p) -> (r q) p", p=P)).then_inc(params_in, 16)
            load_wi("p", COL_P, D_POOL)
            load_wi("u", COL_U, D_SGU)
            for head in range(HEADS):
                for q in range(3):
                    a, b = max(head * HEAD_DIM, q * P), min((head + 1) * HEAD_DIM, (q + 1) * P)
                    if a < b:
                        sp.dma_start(bfull[a - q * P:b - q * P, q, :],
                                     sgu_b[0, head:head + 1, :].broadcast_to([b - a, P])).then_inc(sgub_in, 16)
            sp.wait_ge(zeroed, 1)
            for g in range(4):
                r, a = g // 2, 64 * (g % 2)
                sp.dma_start(pool_wbd[a:a + 64, r, a:a + 64], pool_w[0, g]).then_inc(poolw_in, 16)
            load_wi("c", COL_C, D_CONV)
            load_wi("h", COL_H, D_CONV)
            sp.wait_ge(h_ready, NT)
            sp.dma_start(gain[:], norm2_g[0:1, :].broadcast_to([P, D])).then_inc(g2_in, 16)
            sp.dma_start(rw[:, :, 0:NG], rc_w[0].rearrange("(p k) e -> p k e", p=P)).then_inc(router_in, 16)
            sp.dma_start(rw[:, :, NG:NG + NE], rf_w[0].rearrange("(p k) e -> p k e", p=P)).then_inc(router_in, 16)
            sp.dma_start(rbias[:, 0:NG], rc_b[0:1, :].broadcast_to([P, NG])).then_inc(router_in, 16)
            sp.dma_start(rbias[:, NG:NG + NE], rf_b[0:1, :].broadcast_to([P, NE])).then_inc(router_in, 16)
            sp.wait_ge(v_ps, NT)
            load_wi("b", COL_B, D_CONV)
            sp.wait_ge(v_ready, NT)
            sp.dma_start(new_sgu_v[0, 0], v_sb[0:DEC, NT - 1, :]).then_inc(st_out, 16)

            gate_v = w_gate[0].rearrange("e (p k) f -> p e (k f)", p=P)
            up_v = w_up[0].rearrange("e (p k) f -> p e (k f)", p=P)
            down_v = w_down[0].rearrange("e (c p) d -> p e c d", p=P)

            def load_gate_up(e, s):
                for half in range(2):
                    for a, view in ((0, gate_v), (1, up_v)):
                        sp.dma_start(w1[s][:, a:a + 1, half * (KD // 2):(half + 1) * (KD // 2), :].rearrange(
                            "p a k f -> p a (k f)"), view[:, bass.ds(e, 1), half * (KD // 2) * F:(half + 1) * (KD // 2) * F]
                        ).then_inc(w1_in[s][half], 16)

            def load_down(e, s):
                sp.dma_start(wd[s][:].rearrange("p (o c) d -> p o c d", o=1),
                             down_v[:, bass.ds(e, 1), :, :]).then_inc(wd_in[s], 16)

            sp.wait_ge(proj_ps, nth["u", 2] + 1)
            sp.dma_start(wo[:], w_out[0].rearrange("(k p) n -> p k n", p=P)).then_inc(wo_in, 16)
            sp.wait_ge(st_rows, 2)
            sp.dma_start(new_conv_prompt[0, 0], conv_rows[0:2, :]).then_inc(st_out, 16)
            sp.dma_start(new_conv_sample[0, 0], conv_rows[2:4, :]).then_inc(st_out, 16)
            sp.dma_start(new_pool_prompt[0, 0], pool_rows[0:POOL_HIST, :]).then_inc(st_out, 16)
            sp.dma_start(new_pool_sample[0, 0], pool_rows[POOL_HIST:2 * POOL_HIST, :]).then_inc(st_out, 16)
            sp.wait_ge(st_out, 80)
            sp.wait_ge(proj_ps, NCH)
            sp.wait_ge(evac_dve, 6)
            load_gate_up(0, 0)
            load_down(0, 0)
            hn2_v = hn2_rows.rearrange("(t h) d -> t (h d)", h=2)
            for j in range(NT):
                sp.wait_ge(hn2_ready, j + 1)
                sp.dma_start(hn2_v[j * P:j * P + TOK[j], :], hn2p[0:TOK[j], j % 2, :]).then_inc(hn2_out[j % 2], 16)
                if j == NT - 1:
                    sp.dma_start(gain[:], final_g.rearrange("(o d) -> o d", o=1).broadcast_to([P, D])).then_inc(gf_in, 16)
            sp.wait_ge(wo_ps, NT)
            load_gate_up(1, 1)
            load_down(1, 1)
            sp.wait_ge(idc_seen, 2)
            load_gate_up(2, 2)
            load_down(2, 2)

            def refill(i, s):
                sp.wait_ge(gu_ps, NSLOT * (i - 1) + s + 1)
                load_gate_up(NSLOT * i + s, s)
                sp.wait_ge(dn_ps, NSLOT * (i - 1) + s + 1)
                load_down(NSLOT * i + s, s)

            with sp.Fori(1, ROUNDS) as i:
                for s in range(NSLOT):
                    refill(i, s)
            for n in range(NSLOT * ROUNDS, NE):
                refill(n // NSLOT, n % NSLOT)

            def block_past(b):
                sp.wait_ge(dn_ps, NE + b)
                e = sp.value_load(ovexp[0:1, bass.ds(b, 1)], min_val=0, max_val=NE - 1)
                load_gate_up(e, 0)
                load_down(e, 0)

            count = blocks_past(sp, block_past)
            y_v = y_rows.rearrange("(t r) d -> t (r d)", r=4)
            sp.wait_ge(y_out[0], 16 * (PRE[0] + count))
            sp.wait_ge(y_out[1], 16 * (PRE[1] - 1))
            sp.wait_ge(y_out[2], 16 * PRE[2])
            for k in range(2):
                if k == 1:
                    sp.wait_ge(y_out[(NE - 1) % NSLOT], 16 * PRE[(NE - 1) % NSLOT])
                for j in range(NT):
                    sp.dma_start(yfin[j][0:TOK[j], k * D:(k + 1) * D],
                                 y_v[j * P:j * P + TOK[j], k * D:(k + 1) * D]).then_inc(yfin_in[k][j], 16)
            y_tiles = [y_prompt[0, j * P:(j + 1) * P, :] for j in range(4)] + [y_sample[0]]
            for j in range(NT):
                sp.wait_ge(out_ready[j], 1)
                sp.dma_start(y_tiles[j], yfin[j][0:TOK[j], D:2 * D]).then_inc(y_done, 16)
            sp.wait_ge(y_done, 16 * NT)

        @block.gpsimd
        def _(pool):
            nc.gpsimd.memset(pool_wbd[:], 0.0).then_inc(zeroed, 1)
            nc.gpsimd.memset(zc[:], 0.0).then_inc(zeroed, 1)
            nc.gpsimd.memset(zp[:], 0.0).then_inc(zeroed, 1)
            evacuated(pool, nth["p", 1])
            nc.gpsimd.tensor_copy(poolst[:, :, 0:POOL_HIST], zp[:, :, SEQ:SEQ + POOL_HIST])
            nc.gpsimd.tensor_copy(poolst[:, :, POOL_HIST:], zp[:, :, ZP - POOL_HIST:ZP]).then_inc(st_ready, 1)
            evacuated(pool, nth["h", 2])
            nc.gpsimd.tensor_copy(convst[:, :, 0:2], zc[:, :, SEQ:SEQ + CONV_HIST])
            nc.gpsimd.tensor_copy(convst[:, :, 2:4], zc[:, :, ZC - CONV_HIST:ZC]).then_inc(st_ready, 1)

            pool.wait_ge(hn2T_ps, 2 * NT)
            for par in range(2):
                pool.wait_ge(hn2_out[par], 16 * len(range(par, NT, 2)))
            nc.gpsimd.memset(xg[:, 0:1, :], 0.0)
            pool.wait_ge(L_ps, NT)
            nc.gpsimd.memset(xg[:, 1:NSLOT, :], 0.0).then_inc(xg_zero, 1)
            pool.wait_ge(xg_zero, 1)
            pool.wait_ge(idx_ready, 1)

            def gather(col, s, done):
                nc.gpsimd.tensor_copy(idc_x[:, s:s + 1], idx[:, 0, bass.ds(col, 1)]).then_inc(idc_ready, 1)
                pool.wait_ge(idc_ready, done)
                pool.sem_inc(idc_seen, 1)
                nc.gpsimd.indirect_dma_start(
                    out=xg[:, s, :], out_offset=None, in_=hn2_rows,
                    in_offset=bass.IndirectOffsetOnAxis(ap=idc_x[:, s:s + 1], axis=0),
                    bounds_check=2 * T - 1, oob_is_err=False).then_inc(xg_in[s], 16)

            def scatter(col, s, n, done):
                pool.wait_ge(y_ready, n + 1)
                nc.gpsimd.tensor_copy(idc_y[:, s:s + 1], idx[:, 1, bass.ds(col, 1)]).then_inc(idc_ready, 1)
                pool.wait_ge(idc_ready, done)
                pool.sem_inc(idc_seen, 1)
                nc.gpsimd.indirect_dma_start(
                    out=y_rows, out_offset=bass.IndirectOffsetOnAxis(ap=idc_y[:, s:s + 1], axis=0),
                    in_=ybuf[:, s, :], in_offset=None,
                    bounds_check=4 * T - 1, oob_is_err=False).then_inc(y_out[s], 16)

            for s in range(NSLOT):
                gather(s, s, s + 1)

            def turn(i, s):
                n = NSLOT * i + s
                pool.wait_ge(xT_ps, n + 1)
                gather(n + NSLOT, s, NSLOT + 2 * n + 1)
                scatter(n, s, n, NSLOT + 2 * n + 2)

            for s in range(NSLOT):
                turn(0, s)
            with pool.Fori(1, ROUNDS - 1) as i:
                for s in range(NSLOT):
                    turn(i, s)
            for n in range(NSLOT * (ROUNDS - 1), NE - NSLOT):
                turn(n // NSLOT, n % NSLOT)
            copies = NSLOT + 2 * (NE - NSLOT)
            for n in range(NE - NSLOT, NE):
                copies += 1
                scatter(n, n % NSLOT, n, copies)

            pool.wait_ge(idx_ready, 2)

            def block_past(b):
                pool.wait_ge(y_ready, NE + b)
                gather(NE + b, 0, copies + 2 * b + 1)
                scatter(NE + b, 0, NE + b, copies + 2 * b + 2)

            blocks_past(pool, block_past)
            pool.wait_ge(gf_in, 16)
            for i, j in enumerate(BY_POOL):
                pool.wait_ge(unit_ready, i + 1)
                nc.gpsimd.tensor_tensor(yfin[j][:, D:2 * D], yfin[j][:, 0:D], gain[:], ALU.mult).then_inc(out_ready[j], 1)

        @block.scalar
        def _(act):
            steps = [0]

            def link(ins):
                steps[0] += 1
                ins.then_inc(act_step, 1)
                act.wait_ge(act_step, steps[0])

            def std(j, col, done):
                n = TOK[j]
                link(nc.scalar.activation(junk_of[col][0:n, :], x_sb[0:n, j, :], ACT.Square,
                                          accum_out=small[0:n, col, j:j + 1]))
                nc.scalar.activation(small[0:n, col + 1, j:j + 1], small[0:n, col, j:j + 1], ACT.Sqrt,
                                     bias=con("eps")[0:n, :], scale=1.0 / D).then_inc(done, 1)

            junk_of = {0: junk, 3: hn2T[:].rearrange("p k t -> p (k t)"), 6: xg[:].rearrange("p s d -> p (s d)")[:, 0:D]}

            def round_hT(j):
                n, t = TOK[j], slice(j * P, j * P + TOK[j])
                for h in range(2):
                    act.wait_ge(hT_ps, 2 * j + h + 1)
                    nc.scalar.copy(hT_hi[:, 4 * h:4 * h + 4, t],
                                   ps[:, pair(j) + h, 0:4 * n].rearrange("p (k t) -> p k t", k=4)).then_inc(hT_hi_ready, 1)

            def take_v(j):
                act.wait_ge(v_ps, j + 1)
                nc.scalar.copy(v_sb[0:TOK[j], j, :], ps[0:TOK[j], 4 + j % 2, 0:D_SGU]).then_inc(v_ready, 1)

            def round_wi(n):
                if n >= NCH:
                    return
                g, q = CHUNKS[n]
                if q == 0:
                    act.wait_ge(wi_in[g], 16)
                if n >= 3:
                    act.wait_ge(proj_ps, n - 2)
                nc.scalar.copy(wi_hi[:, n % 3, :, :], wi[g][:, :, q * P:(q + 1) * P]).then_inc(wi_hi_ready, 1)

            def first_std(j):
                act.wait_ge(x_in[j], 16)
                std(j, 0, std1)

            act.wait_ge(warm, 1)
            nc.scalar.activation(small[:, 22, :], small[:, 23, :], ACT.Sqrt)
            act.wait_ge(consts_in, 16)
            first_std(0)
            first_std(1)
            round_hT(0)
            first_std(2)
            act.wait_ge(wi_in["v"], 16)
            nc.scalar.copy(wi_hi_v[:], wi["v"][:]).then_inc(v_hi, 1)
            round_hT(1)
            first_std(3)
            round_hT(2)
            first_std(4)
            round_hT(3)
            take_v(0)
            round_hT(4)
            round_wi(0)
            take_v(1)
            round_wi(1)
            for j in range(2, NT):
                take_v(j)

            def take(g, q):
                n = nth[g, q]
                act.wait_ge(proj_ps, n + 1)
                b0 = pair(n)
                if g == "p":
                    for bank, a, b, t0, smp in segs:
                        at = POOL_HIST + t0 + smp * POOL_HIST
                        last = nc.scalar.copy(zp[:, q, at:at + b - a], ps[:, b0 + bank, a:b])
                elif g == "u":
                    for bank, a, b in halves:
                        last = nc.scalar.copy(mixT[:, 5 + q, a:b], ps[:, b0 + bank, 0:b - a])
                else:
                    for bank, a, b in halves:
                        last = nc.scalar.copy(cbuf[:, q, a:b], ps[:, b0 + bank, 0:b - a])
                last.then_inc(evac_act, 1)

            def take_pool(r):
                act.wait_ge(pool_ps, r + 1)
                scale = prmT[:, R_PS + r:R_PS + r + 1]
                nc.scalar.activation(mixT[:, 3 + r, 0:PO_A], ps[:, 6, 0:PO_A], ACT.Copy, scale=scale)
                nc.scalar.activation(mixT[:, 3 + r, PO_A:SEQ], ps[:, 7, 0:SEQ - PO_A], ACT.Copy, scale=scale)
                nc.scalar.activation(mixT[:, 3 + r, SEQ:T], ps[:, 7, PO_S - PO_A:PO - PO_A], ACT.Copy,
                                     scale=scale).then_inc(pool_ready, 1)

            act.wait_ge(hT_ps, 2 * NT)
            act.wait_ge(wm_ps, 1)
            act.wait_ge(prm_ready, 1)
            act.wait_ge(hist_ready, 1)
            wo_at = [0]

            def round_wo(n, most=2):
                while most and wo_at[0] < KD and WO_ORDER[wo_at[0]][1] <= n:
                    k, after = WO_ORDER[wo_at[0]]
                    act.wait_ge(wo_in, 16)
                    act.wait_ge(proj_ps, after)
                    nc.scalar.copy(wo_hi[:, k, :], wo[:, k, :]).then_inc(wo_hi_ready, 1)
                    wo_at[0] += 1
                    most -= 1

            for n, (g, q) in enumerate(CHUNKS):
                round_wi(n + 2)
                if n == nth["c", 0]:
                    take_pool(0)
                    take_pool(1)
                    act.wait_ge(st_ready, 1)
                if g in ON_ACT:
                    take(g, q)
                if n >= nth["h", 0]:
                    round_wo(n)
            round_wo(NCH, KD)
            for k in MIX_ORDER:
                if k == MIX_ORDER[0]:
                    act.wait_ge(proj_ps, NCH)
                    act.wait_ge(sgu_ready, 3)
                if k == 0:
                    act.wait_ge(evac_dve, 6)
                nc.scalar.copy(mix_hi[:, k, :], mixT[:, k, :]).then_inc(mix_hi_ready, 1)
            act.wait_ge(st_ps, 1)
            act.wait_ge(st_out, 16)
            nc.scalar.copy(conv_rows[0:4, :], ps[0:4, 7, 0:D_CONV]).then_inc(st_rows, 1)
            nc.scalar.copy(pool_rows[0:2 * POOL_HIST, :], ps[0:2 * POOL_HIST, 6, 0:D_POOL]).then_inc(st_rows, 1)

            def take_hn2T(j):
                n = TOK[j]
                if j:
                    act.wait_ge(L_ps, j)
                for h in range(2):
                    act.wait_ge(hn2T_ps, 2 * j + h + 1)
                    nc.scalar.copy(hn2T[:, 4 * h:4 * h + 4, 0:n],
                                   ps[:, 4 + h, 0:4 * n].rearrange("p (k t) -> p k t", k=4)).then_inc(hn2T_ready, 1)

            for j in range(NT):
                act.wait_ge(x2_ready, j + 1)
                if j >= 2:
                    act.wait_ge(L_ps, j - 1)
                std(j, 3, std2)
                if j >= 1:
                    take_hn2T(j - 1)
            take_hn2T(NT - 1)

            act.wait_ge(gdiff_ready, 1)
            nc.scalar.activation(e_g[:], t_g[:], ACT.Exp).then_inc(gexp_ready, 1)
            act.wait_ge(kdiff_ready, 1)
            nc.scalar.activation(small[:, 15, :], small[:, 14, :], ACT.Exp).then_inc(kexp_ready, 1)

            def work(n, s, i):
                act.wait_ge(gu_ps, n + 1)
                nc.scalar.activation(silu_g[:], ps[:, 1, 0:F // 2], ACT.Silu).then_inc(silu_ready, 1)
                act.wait_ge(dn_ps, n + 1)
                if not (isinstance(i, int) and i == 0):
                    act.wait_ge(y_out[s], 16 * i)
                nc.scalar.copy(ybuf[:, s, :], ps[:, 3, :]).then_inc(y_ready, 1)

            experts(act, lambda i, s: work(NSLOT * i + s, s, i))
            blocks_past(act, lambda b: work(NE + b, 0, PRE[0] + b))

            def unit(j):
                act.wait_ge(rstd3, BY_POOL.index(j) + 1)
                nc.scalar.activation(yfin[j][0:TOK[j], 0:D], x_sb[0:TOK[j], j, :], ACT.Copy,
                                     scale=small[0:TOK[j], 8, j:j + 1]).then_inc(unit_ready, 1)

            nc.scalar.activation(small[:, 22, :], small[:, 23, :], ACT.Sqrt)
            for j in range(NT):
                act.wait_ge(acc_ready, j + 1)
                std(j, 6, std3)
                if j - 1 in BY_POOL:
                    unit(j - 1)
            assert NT - 1 not in BY_POOL

        @block.vector
        def _(dve):
            steps = [0]

            def link(ins):
                steps[0] += 1
                ins.then_inc(dve_step, 1)
                dve.wait_ge(dve_step, steps[0])

            def tt(out, a, b, op):
                return nc.vector.tensor_tensor(out, a, b, op)

            def ts(out, a, s1, s2, op0, op1=ALU.bypass):
                return nc.vector.tensor_scalar(out, a, s1, s2, op0, op1)

            def stt(out, a, s, b, op0, op1):
                return nc.vector.scalar_tensor_tensor(out, a, s, b, op0, op1)

            def normalise(j):
                n = TOK[j]
                dve.wait_ge(std1, j + 1)
                link(nc.vector.reciprocal(small[0:n, 2, j:j + 1], small[0:n, 1, j:j + 1]))
                if j >= 2:
                    dve.wait_ge(hT_ps, 2 * (j - 1))
                stt(hstage[0:n, j % 2, :], x_sb[0:n, j, :], small[0:n, 2, j:j + 1], gain[0:n, :], ALU.mult,
                    ALU.mult).then_inc(h_ready, 1)

            def rest_hT(j):
                n, t = TOK[j], slice(j * P, j * P + TOK[j])
                for h in range(2):
                    dve.wait_ge(hT_hi_ready, 2 * j + h + 1)
                    k = slice(4 * h, 4 * h + 4)
                    tt(hT_lo[:, k, t], ps[:, pair(j) + h, 0:4 * n].rearrange("p (k t) -> p k t", k=4),
                       hT_hi[:, k, t].bitcast(F32), ALU.subtract).then_inc(hT_lo_ready, 1)

            def rest_wi(n):
                if n >= NCH:
                    return
                g, q = CHUNKS[n]
                dve.wait_ge(wi_hi_ready, n + 1)
                c = slice(q * P, (q + 1) * P)
                tt(wi_lo[g][:, :, c], wi[g][:, :, c], wi_hi[:, n % 3, :, :].bitcast(F32),
                   ALU.subtract).then_inc(wi_lo_ready, 1)

            nc.vector.memset(small[:, 22:24, :], 1.0).then_inc(warm, 1)
            dve.wait_ge(g1_in, 16)
            normalise(0)
            normalise(1)
            rest_hT(0)
            normalise(2)
            dve.wait_ge(v_hi, 1)
            tt(wi_lo["v"][:], wi["v"][:], wi_hi_v[:].bitcast(F32), ALU.subtract).then_inc(v_lo, 1)
            rest_hT(1)
            normalise(3)
            rest_hT(2)
            normalise(4)
            rest_hT(3)
            rest_hT(4)
            rest_wi(0)
            dve.wait_ge(prm_ps, 1)
            nc.vector.tensor_copy(prmT[:], ps[:, 7, 0:R_ALL]).then_inc(prm_ready, 1)
            dve.wait_ge(wm_ps, 1)
            dve.wait_ge(consts_in, 16)
            tt(wmT[:], ps[:, 6, :].rearrange("p (h i) -> p h i", h=HEADS),
               con("causal")[:, None, :].broadcast_to([P, HEADS, P]), ALU.mult).then_inc(wm_ready, 1)
            dve.wait_ge(prm_ready, 1)
            dve.wait_ge(zeroed, 3)
            nc.vector.tensor_copy(zc[:, :, ZC_S - CONV_HIST:ZC_S],
                                  prmT[:, R_SC:R_SP].rearrange("p (r q) -> p q r", q=3))
            nc.vector.tensor_copy(zp[:, :, ZP_S - POOL_HIST:ZP_S],
                                  prmT[:, R_SP:R_ALL].rearrange("p (r q) -> p q r", q=2)).then_inc(hist_ready, 1)
            rest_wi(1)
            dve.wait_ge(hist_ready, 1)

            def pool(r):
                evacuated(dve, nth["p", r])
                z = zp[:, r, :]
                link(tt(win_a[:, 1:ZP], z[:, 1:ZP], z[:, 0:ZP - 1], ALU.add))
                low, up = slice(0, 64), slice(64, P)
                if r == 0:
                    link(tt(win_b[up, 3:ZP], win_a[up, 3:ZP], win_a[up, 1:ZP - 2], ALU.add))
                else:
                    link(tt(win_b[:, 3:ZP], win_a[:, 3:ZP], win_a[:, 1:ZP - 2], ALU.add))
                    link(tt(win_a[:, 7:ZP], win_b[:, 7:ZP], win_b[:, 3:ZP - 4], ALU.add))
                    link(tt(win_b[up, 15:ZP], win_a[up, 15:ZP], win_a[up, 7:ZP - 8], ALU.add))
                rc = con("rc15").rearrange("p (r i) -> p r i", r=2)
                for part, win in ((low, win_a), (up, win_b)):
                    link(stt(pooled[part, r, :], win[part, POOL_HIST:ZP], con("invw")[part, r:r + 1],
                             z[part, POOL_HIST:ZP], ALU.mult, ALU.subtract))
                    link(tt(win[part, POOL_HIST:2 * POOL_HIST], win[part, POOL_HIST:2 * POOL_HIST],
                            rc[part, r, :], ALU.mult))
                    last = tt(pooled[part, r, 0:POOL_HIST], win[part, POOL_HIST:2 * POOL_HIST],
                              z[part, POOL_HIST:2 * POOL_HIST], ALU.subtract)
                    if part == low:
                        link(last)
                last.then_inc(pooled_ready, 1)

            def sgu(q):
                dve.wait_ge(sgu_ps, q + 1)
                if q == 0:
                    dve.wait_ge(sgub_in, 96)
                tt(gated[:, 0:SEQ].rearrange("p (n i) -> p n i", n=4),
                   ps[:, 4 + q % 2, :].rearrange("p (n i) -> p n i", n=4),
                   bfull[:, q, None, :].broadcast_to([P, 4, P]), ALU.add)
                tt(gated[:, SEQ:T], ps[:, 6 + q % 2, 0:DEC], bfull[:, q, 0:DEC], ALU.add).then_inc(sgu_read, 1)
                dve.wait_ge(sgu_read, q + 1)
                evacuated(dve, nth["u", q])
                tt(mixT[:, 5 + q, :], mixT[:, 5 + q, :], gated[:], ALU.mult).then_inc(sgu_ready, 1)
                dve.wait_ge(sgu_ready, q + 1)

            def take_h(q):
                n = nth["h", q]
                dve.wait_ge(proj_ps, n + 1)
                evacuated(dve, nth["c", q])
                for bank, a, b, t0, smp in segs:
                    at = CONV_HIST + t0 + smp * CONV_HIST
                    last = tt(zc[:, q, at:at + b - a], ps[:, pair(n) + bank, a:b], cbuf[:, q, t0:t0 + b - a], ALU.mult)
                last.then_inc(evac_dve, 1)
                dve.wait_ge(evac_dve, q + 1)
                z = zc[:, q, :]
                w = [prmT[:, R_CW + 3 * k + q:R_CW + 3 * k + q + 1] for k in range(3)]
                y = yconv[:, q, :]
                link(ts(y, z[:, 0:YC], w[0], None, ALU.mult))
                link(stt(y, z[:, 1:YC + 1], w[1], y, ALU.mult, ALU.add))
                link(stt(y, z[:, 2:YC + 2], w[2], y, ALU.mult, ALU.add))

            def take_b(q):
                n = nth["b", q]
                dve.wait_ge(proj_ps, n + 1)
                for bank, a, b, t0, smp in segs:
                    at = t0 + smp * CONV_HIST
                    last = tt(mixT[:, q, t0:t0 + b - a], ps[:, pair(n) + bank, a:b], yconv[:, q, at:at + b - a], ALU.mult)
                last.then_inc(evac_dve, 1)

            wo_at = [0]

            def rest_wo(upto):
                while wo_at[0] < upto:
                    k = WO_ORDER[wo_at[0]][0]
                    dve.wait_ge(wo_hi_ready, wo_at[0] + 1)
                    tt(wo_lo[:, k, :], wo[:, k, :], wo_hi[:, k, :].bitcast(F32), ALU.subtract).then_inc(wo_lo_ready, 1)
                    wo_at[0] += 1

            for n, (g, q) in enumerate(CHUNKS):
                rest_wi(n + 2)
                if g == "p":
                    pool(q)
                elif g == "u":
                    sgu(q)
                elif g == "h":
                    if q == 0:
                        dve.wait_ge(pool_ps, 2)
                    take_h(q)
                elif g == "b":
                    if q < 2:
                        take_b(q)
                if n >= nth["h", 1]:
                    rest_wo(min(KD - 1, 2 * (n - nth["h", 0])))
            rest_wo(KD)

            def rest_mix(i):
                dve.wait_ge(mix_hi_ready, i + 1)
                k = MIX_ORDER[i]
                tt(mixT_lo[:, k, :], mixT[:, k, :], mix_hi[:, k, :].bitcast(F32), ALU.subtract).then_inc(mix_lo_ready, 1)

            rest_mix(0)
            rest_mix(1)
            take_b(2)
            for i in range(2, KD):
                rest_mix(i)

            def take_L(j):
                n = TOK[j]
                dve.wait_ge(L_ps, j + 1)
                tt(L[0:n, j, :], ps[0:n, 6 + j % 2, 0:NG + NE], rbias[0:n, :], ALU.add).then_inc(L_ready, 1)

            link(nc.vector.memset(L[:], 0.0))
            dve.wait_ge(pool_ps, 2)
            nc.vector.memset(ones_b[:], 1.0)
            nc.vector.tensor_copy(tri_b[:], con("strict")).then_inc(tri_ready, 1)
            dve.wait_ge(g2_in, 16)
            dve.wait_ge(router_in, 64)
            for j in range(NT):
                n = TOK[j]
                dve.wait_ge(wo_ps, j + 1)
                tt(x_sb[0:n, j, :], ps[0:n, pair(j):pair(j) + 2, :].rearrange("p b n -> p (b n)"),
                   x_sb[0:n, j, :], ALU.add).then_inc(x2_ready, 1)
                dve.wait_ge(std2, j + 1)
                link(nc.vector.reciprocal(small[0:n, 5, j:j + 1], small[0:n, 4, j:j + 1]))
                if j >= 2:
                    dve.wait_ge(hn2_out[j % 2], 16 * (j // 2))
                    dve.wait_ge(hn2T_ps, 2 * (j - 1))
                stt(hn2p[0:n, j % 2, :].rearrange("t (k p) -> t k p", k=KD),
                    x_sb[0:n, j, :].rearrange("t (p k) -> t k p", k=KD), small[0:n, 5, j:j + 1],
                    gain[0:n, :].rearrange("t (p k) -> t k p", k=KD), ALU.mult, ALU.mult).then_inc(hn2_ready, 1)
                if j >= 2:
                    take_L(j - 2)
            take_L(NT - 2)
            take_L(NT - 1)
            dve.wait_ge(wo_ps, NT)
            nc.vector.memset(Mb[:, NT, :], 0.0)
            nc.vector.tensor_copy(vals[:].rearrange("p t k c -> p (t k c)"), con("vals"))
            dve.wait_ge(L_ready, NT)

            mx, v1, v2, mark, mark_1, mark_2 = (small[:, c, :] for c in (9, 10, 11, 12, 24, 25))
            second_first, swap = small[:, 26, :], small[:, 27, :]
            psel, kdiff, kexp, w_hi = (small[:, c, :] for c in (13, 14, 15, 16))

            def over(x, shape):
                return x.broadcast_to(shape)

            def first_greatest(out, x, top, weights, tmp, n, mark):
                link(tt(tmp, x, over(top[:, :, None], [P, NT, n]), ALU.is_equal))
                link(tt(tmp, tmp, over(weights[:, None, :], [P, NT, n]), ALU.mult))
                link(nc.vector.tensor_reduce(mark, tmp, AX.X, ALU.max))
                link(tt(out, tmp, over(mark[:, :, None], [P, NT, n]), ALU.is_equal))

            lc, lf = L[:, :, 0:NG], L[:, :, NG:].rearrange("p t (g e) -> p t g e", g=NG)
            link(nc.vector.tensor_reduce(mx, lc, AX.X, ALU.max))
            tt(t_g[:], lc, over(mx[:, :, None], [P, NT, NG]), ALU.subtract).then_inc(gdiff_ready, 1)
            dve.wait_ge(gdiff_ready, 1)
            link(stt(oh_g[:], t_g[:], 0.0, over(con("w4")[:, None, :], [P, NT, NG]), ALU.is_ge, ALU.mult))
            link(nc.vector.tensor_reduce(mark, oh_g[:], AX.X, ALU.max))
            link(tt(oh_g[:], oh_g[:], over(mark[:, :, None], [P, NT, NG]), ALU.is_equal))
            link(tt(t_ge[:], lf, over(oh_g[:, :, :, None], [P, NT, NG, EPG]), ALU.mult))
            link(nc.vector.tensor_reduce(sel[:], t_ge[:].rearrange("p t g e -> p t e g"), AX.X, ALU.add))
            link(nc.vector.tensor_reduce(v1, sel[:], AX.X, ALU.max))
            first_greatest(oh_k[:, :, 0, :], sel[:], v1, con("w8"), t_e[:], EPG, mark_1)
            link(stt(sel[:], oh_k[:, :, 0, :], -3.0e38, sel[:], ALU.mult, ALU.add))
            link(nc.vector.tensor_reduce(v2, sel[:], AX.X, ALU.max))
            tt(kdiff, v2, v1, ALU.subtract).then_inc(kdiff_ready, 1)
            first_greatest(oh_k[:, :, 1, :], sel[:], v2, con("w8"), t_e[:], EPG, mark_2)
            link(tt(oh_both[:], oh_k[:, :, 0, :], oh_k[:, :, 1, :], ALU.add))
            tt(Mb[:, 0:NT, :].rearrange("p t (g e) -> p t g e", g=NG), over(oh_g[:, :, :, None], [P, NT, NG, EPG]),
               over(oh_both[:, :, None, :], [P, NT, NG, EPG]), ALU.mult).then_inc(memb_ready, 1)
            nc.vector.tensor_tensor(second_first, mark_1, mark_2, ALU.is_lt).then_inc(dve_step, 1)
            steps[0] += 1
            for k in range(2):
                tt(memb[:, :, k, :].rearrange("p t (g e) -> p t g e", g=NG),
                   over(oh_g[:, :, :, None], [P, NT, NG, EPG]),
                   over(oh_k[:, :, k, None, :], [P, NT, NG, EPG]), ALU.mult)
            dve.wait_ge(dve_step, steps[0])
            link(tt(swap, second_first, con("two"), ALU.mult))
            tt(vals[:, :, 0, 1], vals[:, :, 0, 1], swap, ALU.add)
            link(tt(vals[:, :, 1, 1], vals[:, :, 1, 1], swap, ALU.subtract))
            choices = memb[:].rearrange("p t k e -> p (t k) e")
            rows = vals[:].rearrange("p t k c -> p (t k) c")
            tt(onehot_v[:], over(choices[:, :, None, :], [P, NT * 2, 2, NE]),
               over(rows[:, :, :, None], [P, NT * 2, 2, NE]), ALU.mult)
            place, past, j_k, col, dead = (at_k[:, c, :] for c in range(5))
            before = ps[:, 7, 0:NT * NE].rearrange("p (t e) -> p t e", e=NE)
            in_all = ps[:, 7, NT * NE:(NT + 1) * NE]
            t_c = t_m[:].rearrange("p t k e -> p (t k) e")
            dve.wait_ge(pos_ps, 1)
            link(tt(t_m[:], memb[:], over(before[:, :, None, :], [P, NT, 2, NE]), ALU.mult))
            link(nc.vector.tensor_reduce(place, t_c, AX.X, ALU.add))
            dve.wait_ge(hn2_out[0], 48)
            dve.wait_ge(hn2_out[1], 32)
            dve.wait_ge(L_ps, NT)
            positions = over(con("iota_pos")[:, None, None, :], [P, NT * 2, 2, BLK])
            tt(onehot_s[:], positions, over(place[:, :, None, None], [P, NT * 2, 2, BLK]), ALU.is_equal).then_inc(onehot_ready, 1)
            dve.wait_ge(idx_ps, 1)
            ts(idx[:, :, 0:NE], ps[:, 6, 0:2 * NE].rearrange("p (c n) -> p c n", c=2), con("base"), None,
               ALU.add).then_inc(idx_ready, 1)

            def blocks_past_first():
                link(tt(t_j[:], over(in_all[:, :, None], [P, NE, MAX_J]), over(con("past")[:, None, :], [P, NE, MAX_J]),
                        ALU.is_gt))
                link(nc.vector.tensor_reduce(nblk[:, 0, :], t_j[:], AX.X, ALU.add))
                link(nc.vector.tensor_tensor_scan(nblk[:, 1, :], nblk[:, 0, :], nblk[:, 0, :], 0.0, ALU.add, ALU.bypass))
                link(tt(nblk[:, 2, :], nblk[:, 1, :], nblk[:, 0, :], ALU.subtract))
                link(tt(t_m[:], memb[:], over(nblk[:, 2, None, None, :], [P, NT, 2, NE]), ALU.mult))
                nc.vector.tensor_reduce(past, t_c, AX.X, ALU.add)
                link(tt(t_k[:], over(place[:, :, None], [P, NT * 2, MAX_J]),
                        over(con("past")[:, None, :], [P, NT * 2, MAX_J]), ALU.is_ge))
                link(nc.vector.tensor_reduce(j_k, t_k[:], AX.X, ALU.add))
                ts(dead, j_k, 0.0, -1000.0, ALU.is_equal, ALU.mult)
                link(stt(col, j_k, -1.0, past, ALU.add, ALU.add))
                link(stt(place, j_k, -float(BLK), place, ALU.mult, ALU.add))
                link(tt(col, col, dead, ALU.add))
                tt(onehot_s[:], positions, over(place[:, :, None, None], [P, NT * 2, 2, BLK]), ALU.is_equal)
                link(tt(onehot_c[:], over(con("ovnum")[:, None, :], [P, NT * 2, NOV]),
                        over(col[:, :, None], [P, NT * 2, NOV]), ALU.is_equal))
                tt(onehot_p[:], over(onehot_c[:, :, None, :], [P, NT * 2, 2, NOV]),
                   over(rows[:, :, :, None], [P, NT * 2, 2, NOV]), ALU.mult).then_inc(onehot_ready, 1)
                link(tt(t_o[:], over(nblk[:, 1, None, :], [P, NOV, NE]), over(con("ovnum")[:, :, None], [P, NOV, NE]),
                        ALU.is_le))
                numbers = small[:, 17:21, :].rearrange("p a b -> p (a b)")[:, 0:NOV]
                link(nc.vector.tensor_reduce(numbers, t_o[:], AX.X, ALU.add))
                nc.vector.tensor_copy(ovexp[:], numbers)
                nc.vector.tensor_copy(nov[:], nblk[:, 1, NE - 1:NE]).then_inc(nov_ready, 1)
                dve.wait_ge(idx_ps, 2)
                ts(idx[:, :, NE:], ps[:, 5, 0:2 * NOV].rearrange("p (c n) -> p c n", c=2), con("base"), None,
                   ALU.add).then_inc(idx_ready, 1)

            def take_gates():
                dve.wait_ge(gexp_ready, 1)
                link(nc.vector.tensor_reduce(psel, e_g[:], AX.X, ALU.add))
                link(nc.vector.reciprocal(psel, psel))
                dve.wait_ge(kexp_ready, 1)
                link(ts(w_hi, kexp, 1.0, None, ALU.add))
                link(nc.vector.reciprocal(w_hi, w_hi))
                link(tt(w_hi, psel, w_hi, ALU.mult))
                link(tt(kexp, w_hi, kexp, ALU.mult))
                link(ts(swap, second_first, -1.0, 1.0, ALU.mult, ALU.add))
                for k, (a, b) in enumerate(((w_hi, kexp), (kexp, w_hi))):
                    link(tt(psel, swap, a, ALU.mult))
                    link(tt(gates[:, :, k], second_first, b, ALU.mult))
                    link(tt(gates[:, :, k], gates[:, :, k], psel, ALU.add))

            def work(n):
                dve.wait_ge(xT_ps, n + 1)
                nc.vector.tensor_copy(xT[:].rearrange("p c s -> p (c s)"), ps[:, 0, :]).then_inc(xT_ready, 1)

            def work_h(n):
                dve.wait_ge(silu_ready, n + 1)
                tt(hexp[:], silu_g[:], ps[:, 1, F // 2:F], ALU.mult).then_inc(h_exp, 1)

            def work_hT(n):
                dve.wait_ge(hexT_ps, n + 1)
                nc.vector.tensor_copy(hexT[:].rearrange("p c s -> p (c s)"), ps[:, 2, 0:2 * P]).then_inc(hexT_ready, 1)

            work(0)
            blocks_past_first()
            take_gates()

            def turn(i, s, more=True):
                n = NSLOT * i + s
                work_h(n)
                if more:
                    work(n + 1)
                work_hT(n)

            experts(dve, lambda i, s: turn(i, s, not (isinstance(i, int) and NSLOT * i + s == NE - 1)))

            def block_past(b):
                work(NE + b)
                work_h(NE + b)
                work_hT(NE + b)

            blocks_past(dve, block_past)

            def finish(j):
                n = TOK[j]
                dve.wait_ge(std3, j + 1)
                if j in BY_POOL:
                    nc.vector.reciprocal(small[0:n, 8, j:j + 1], small[0:n, 7, j:j + 1]).then_inc(rstd3, 1)
                else:
                    link(nc.vector.reciprocal(small[0:n, 8, j:j + 1], small[0:n, 7, j:j + 1]))
                    stt(yfin[j][0:n, D:2 * D], x_sb[0:n, j, :], small[0:n, 8, j:j + 1], gain[0:n, :], ALU.mult,
                        ALU.mult).then_inc(out_ready[j], 1)

            for j in range(NT):
                n = TOK[j]
                dve.wait_ge(yfin_in[0][j], 16)
                last = stt(x_sb[0:n, j, :], yfin[j][0:n, 0:D], gates[0:n, j, 0:1], x_sb[0:n, j, :], ALU.mult, ALU.add)
            link(last)
            dve.wait_ge(gf_in, 16)
            for j in range(NT):
                n = TOK[j]
                dve.wait_ge(yfin_in[1][j], 16)
                stt(x_sb[0:n, j, :], yfin[j][0:n, D:2 * D], gates[0:n, j, 1:2], x_sb[0:n, j, :], ALU.mult,
                    ALU.add).then_inc(acc_ready, 1)
                if j:
                    finish(j - 1)
            finish(NT - 1)

        @block.tensor
        def _(pe):
            mm = nc.tensor.matmul

            pe.wait_ge(consts_in, 16)

            def transpose_h(j):
                n = TOK[j]
                pe.wait_ge(h_ready, j + 1)
                if j >= 2:
                    pe.wait_ge(hT_lo_ready, 2 * (j - 1))
                for h in range(2):
                    for k in range(4):
                        last = nc.tensor.transpose(ps[:, pair(j) + h, k * n:(k + 1) * n],
                                                   hstage[0:n, j % 2, (4 * h + k) * P:(4 * h + k + 1) * P],
                                                   ident[0:n, 0:n])
                    last.then_inc(hT_ps, 1)

            def product_v(j):
                n = TOK[j]
                pe.wait_ge(hT_lo_ready, 2 * (j + 1))
                if j == 0:
                    pe.wait_ge(v_lo, 1)
                if j >= 2:
                    pe.wait_ge(v_ready, j - 1)
                out, t = ps[0:n, 4 + j % 2, 0:D_SGU], slice(j * P, j * P + n)
                for k in range(KD):
                    mm(out, hT_hi[:, k, t], wi_hi_v[:, k, :], start=(k == 0), stop=False)
                    mm(out, hT_hi[:, k, t], wi_lo["v"][:, k, :], start=False, stop=False)
                    last = mm(out, hT_lo[:, k, t], wi_hi_v[:, k, :], start=False, stop=(k == KD - 1))
                last.then_inc(v_ps, 1)

            transpose_h(0)
            transpose_h(1)
            transpose_h(2)
            product_v(0)
            transpose_h(3)
            product_v(1)
            transpose_h(4)
            pe.wait_ge(params_in, 64)
            nc.tensor.transpose(ps[:, 7, 0:R_ALL], prm[0:R_ALL, :], ident[0:R_ALL, 0:R_ALL]).then_inc(prm_ps, 1)
            pe.wait_ge(sguw_in, 16)
            for head in range(HEADS):
                last = nc.tensor.transpose(ps[:, 6, head * P:(head + 1) * P], sguw[:, head, :], ident)
            last.then_inc(wm_ps, 1)
            for j in range(2, NT):
                product_v(j)

            def product(g, q):
                n = nth[g, q]
                pe.wait_ge(wi_lo_ready, n + 1)
                if n == 0:
                    pe.wait_ge(hT_lo_ready, 2 * NT)
                if n >= 2:
                    evacuated(pe, n - 2)
                for k in range(KD):
                    w_hi, w_lo = wi_hi[:, n % 3, k, :], wi_lo[g][:, k, q * P:(q + 1) * P]
                    for part, (w, h) in enumerate(((w_hi, hT_hi), (w_hi, hT_lo), (w_lo, hT_hi))):
                        for bank, a, b in halves:
                            last = mm(ps[:, pair(n) + bank, 0:b - a], w, h[:, k, a:b], start=(k + part == 0),
                                      stop=(k == KD - 1 and part == 2))
                last.then_inc(proj_ps, 1)

            def mix_positions(q):
                if q == 0:
                    pe.wait_ge(v_ready, NT)
                    pe.wait_ge(wm_ready, 1)
                    pe.wait_ge(prm_ready, 1)
                if q >= 2:
                    pe.wait_ge(sgu_read, q - 1)
                for t in range(NT):
                    n = TOK[t]
                    for at in range(0, P, PIECE):
                        ch = q * P + at
                        out = ps[at:at + PIECE, 4 + q % 2, t * P:(t + 1) * P] if t < 4 else \
                            ps[at:at + PIECE, 6 + q % 2, 0:DEC]
                        last = mm(out, v_sb[0:n, t, ch:ch + PIECE], wmT[0:n, ch // HEAD_DIM, 0:n], start=True,
                                  stop=True)
                last.then_inc(sgu_ps, 1)

            def mix_pooled(r):
                pe.wait_ge(pooled_ready, r + 1)
                if r == 0:
                    pe.wait_ge(poolw_in, 64)
                    pe.wait_ge(sgu_read, 3)
                else:
                    pe.wait_ge(pool_ready, r)
                mm(ps[:, 6, 0:PO_A], pool_wbd[:, r, :], pooled[:, r, 0:PO_A], start=True, stop=True)
                mm(ps[:, 7, 0:PO - PO_A], pool_wbd[:, r, :], pooled[:, r, PO_A:PO], start=True,
                   stop=True).then_inc(pool_ps, 1)

            product("p", 0)
            product("p", 1)
            for q in range(3):
                product("u", q)
                mix_positions(q)
            for n in range(nth["c", 0], NCH):
                product(*CHUNKS[n])
                if n == nth["c", 0]:
                    mix_pooled(0)
                if n == nth["c", 1]:
                    mix_pooled(1)
            pe.wait_ge(st_ready, 2)
            pe.wait_ge(pool_ready, 2)
            for q in range(3):
                nc.tensor.transpose(ps[0:4, 7, q * P:(q + 1) * P], convst[:, q, :], ident)
            for r in range(2):
                last = nc.tensor.transpose(ps[0:2 * POOL_HIST, 6, r * P:(r + 1) * P], poolst[:, r, :], ident)
            last.then_inc(st_ps, 1)

            def output(j):
                n = TOK[j]
                if j == 0:
                    pe.wait_ge(wo_lo_ready, KD)
                if j >= 2:
                    pe.wait_ge(x2_ready, j - 1)
                t = slice(j * P, j * P + n)
                for i, k in enumerate(MIX_ORDER):
                    if j == 0:
                        pe.wait_ge(mix_lo_ready, i + 1)
                        if i == 0:
                            evacuated(pe, NCH - 2)
                    if j == 1 and i == 0:
                        evacuated(pe, NCH - 1)
                    for part, (m, w) in enumerate(((mix_hi, wo_hi), (mix_hi, wo_lo), (mixT_lo, wo_hi))):
                        for half in range(2):
                            last = mm(ps[0:n, pair(j) + half, :], m[:, k, t], w[:, k, half * 512:(half + 1) * 512],
                                      start=(i + part == 0), stop=(i == KD - 1 and part == 2))
                last.then_inc(wo_ps, 1)

            def transpose_hn2(j):
                n = TOK[j]
                pe.wait_ge(hn2_ready, j + 1)
                for h in range(2):
                    if j:
                        pe.wait_ge(hn2T_ready, 2 * (j - 1) + h + 1)
                    for k in range(4):
                        last = nc.tensor.transpose(ps[:, 4 + h, k * n:(k + 1) * n],
                                                   hn2p[0:n, j % 2, (4 * h + k) * P:(4 * h + k + 1) * P],
                                                   ident[0:n, 0:n])
                    last.then_inc(hn2T_ps, 1)

            def logits(j):
                n = TOK[j]
                pe.wait_ge(hn2T_ready, 2 * (j + 1))
                if j == 0:
                    pe.wait_ge(router_in, 64)
                    pe.wait_ge(st_rows, 2)
                if j >= 2:
                    pe.wait_ge(L_ready, j - 1)
                for k in range(KD):
                    last = mm(ps[0:n, 6 + j % 2, 0:NG + NE], hn2T[:, k, 0:n], rw[:, k, :], start=(k == 0),
                              stop=(k == KD - 1))
                last.then_inc(L_ps, 1)

            output(0)
            output(1)
            transpose_hn2(0)
            output(2)
            logits(0)
            transpose_hn2(1)
            output(3)
            logits(1)
            transpose_hn2(2)
            output(4)
            logits(2)
            transpose_hn2(3)
            logits(3)
            transpose_hn2(4)
            logits(4)

            pe.wait_ge(memb_ready, 1)
            pe.wait_ge(tri_ready, 1)
            mm(ps[:, 7, 0:(NT + 1) * NE], tri_b[:], Mb[:].rearrange("p t e -> p (t e)"), start=True, stop=False)
            for j in range(NT):
                n = TOK[j]
                last = mm(ps[:, 7, (j + 1) * NE:(NT + 1) * NE], ones_b[0:n, :],
                          Mb[0:n, j, None, :].broadcast_to([n, NT - j, NE]), start=False, stop=(j == NT - 1))
            last.then_inc(pos_ps, 1)

            def rows_of_places(bank, columns, done):
                pe.wait_ge(onehot_ready, done)
                for i in range(2 * NT):
                    last = mm(ps[:, bank, 0:columns.shape[2] * columns.shape[3]],
                              onehot_s[:, i, :, :].rearrange("p h b -> p (h b)"),
                              columns[:, i, :, :].rearrange("p c n -> p (c n)"), start=(i == 0), stop=(i == 2 * NT - 1))
                last.then_inc(idx_ps, 1)

            rows_of_places(6, onehot_v, 1)

            def transpose_x(s, uses):
                pe.wait_ge(xg_in[s], 16 * uses)
                for c in range(KD // 2):
                    last = nc.tensor.transpose(ps[:, 0, c * P:(c + 1) * P], xg[:, s, c * P:(c + 1) * P], ident)
                last.then_inc(xT_ps, 1)

            def gate_up(n, s, uses):
                pe.wait_ge(xT_ready, n + 1)
                for k in range(KD):
                    if k % (KD // 2) == 0:
                        pe.wait_ge(w1_in[s][k // (KD // 2)], 32 * uses)
                    lhs = xT[:, k % 4, 64 * (k // 4):64 * (k // 4) + 64]
                    for h in range(2):
                        last = mm(ps[64 * h:64 * h + 64, 1, :], lhs, w1[s][:, :, k, h * (F // 2):(h + 1) * (F // 2)],
                                  start=(k == 0), stop=(k == KD - 1))
                last.then_inc(gu_ps, 1)

            def transpose_act(n):
                pe.wait_ge(h_exp, n + 1)
                for c in range(2):
                    last = nc.tensor.transpose(ps[:, 2, c * P:(c + 1) * P], hexp[:, c * P:(c + 1) * P], ident)
                last.then_inc(hexT_ps, 1)

            def down(n, s, uses):
                pe.wait_ge(hexT_ready, n + 1)
                pe.wait_ge(wd_in[s], 16 * uses)
                if not (isinstance(n, int) and n == 0):
                    pe.wait_ge(y_ready, n)
                for c in range(F // P):
                    lhs = hexT[:, c % 2, 64 * (c // 2):64 * (c // 2) + 64]
                    for h in range(2):
                        last = mm(ps[64 * h:64 * h + 64, 3, :], lhs, wd[s][:, c, h * 512:(h + 1) * 512],
                                  start=(c == 0), stop=(c == F // P - 1))
                last.then_inc(dn_ps, 1)

            transpose_x(0, 1)

            def turn(i, s, more=True):
                n = NSLOT * i + s
                gate_up(n, s, i + 1)
                if isinstance(n, int) and n == 0:
                    rows_of_places(5, onehot_p, 2)
                if more:
                    transpose_x((s + 1) % NSLOT, i + 1 + (s + 1) // NSLOT)
                transpose_act(n)
                down(n, s, i + 1)

            experts(pe, lambda i, s: turn(i, s, not (isinstance(i, int) and NSLOT * i + s == NE - 1)))

            def block_past(b):
                transpose_x(0, PRE[0] + b + 1)
                gate_up(NE + b, 0, PRE[0] + b + 1)
                transpose_act(NE + b)
                down(NE + b, 0, PRE[0] + b + 1)

            blocks_past(pe, block_past)


_INS = ["x_prompt", "x_sample", "state_conv", "state_pool", "norm1_g", "w_in", "conv_w", "pool_w", "pool_scale",
        "sgu_w", "sgu_b", "w_out", "norm2_g", "router_coarse_w", "router_coarse_b", "router_fine_w",
        "router_fine_b", "moe_w_gate", "moe_w_up", "moe_w_down", "final_norm_g"]
_OUTS = [(1, SEQ, D), (1, DEC, D), (1, 1, CONV_HIST, D_CONV), (1, 1, POOL_HIST, D_POOL),
         (1, 1, CONV_HIST, D_CONV), (1, 1, POOL_HIST, D_POOL), (1, 1, DEC, D_SGU)]


def kernel(**inputs):
    import numpy as np
    import concourse.bacc as bacc
    from concourse.bass_utils import run_bass_kernel_spmd

    nc = bacc.Bacc("TRN2", target_bir_lowering=False, num_devices=1)
    arrays, args = {}, []
    for name in _INS:
        a = np.ascontiguousarray(inputs[name])
        arrays[f"in_{name}"] = a
        args.append(nc.dram_tensor(f"in_{name}", a.shape, mybir.dt.from_np(a.dtype), kind="ExternalInput").ap())
    arrays["in_constants"] = constant_tile()
    args.append(nc.dram_tensor("in_constants", (P, NCONST), F32, kind="ExternalInput").ap())
    for i, shape in enumerate(_OUTS):
        args.append(nc.dram_tensor(f"out_{i}", shape, F32, kind="ExternalOutput").ap())
    build(nc, *args)
    r = run_bass_kernel_spmd(nc, [arrays], core_ids=[0])
    return tuple(r.results[0][f"out_{i}"] for i in range(len(_OUTS)))
```

```python
import concourse.bass as bass
from concourse import mybir
from concourse.alu_op_type import AluOpType as ALU

F32 = mybir.dt.float32
BF16 = mybir.dt.bfloat16
F32R = mybir.dt.float32r
I32 = mybir.dt.int32
ACT = mybir.ActivationFunctionType
AX = mybir.AxisListType

P = 128
D = 1024
KD = D // P
SEQ, DEC = 512, 64
T = SEQ + DEC
NT = 5
TOK = [P, P, P, P, DEC]
D_CONV, D_POOL, D_SGU = 384, 256, 384
CONV_HIST, POOL_HIST = 2, 15
COL_B, COL_C, COL_H = 0, D_CONV, 2 * D_CONV
COL_P = 3 * D_CONV
COL_U = COL_P + D_POOL
COL_V = COL_U + D_SGU
HEADS, HEAD_DIM = 4, D_SGU // 4
NG, EPG, NE = 4, 8, 32
F = 512
EPS = 1e-6
HT = T // 2

ZC = CONV_HIST + SEQ + CONV_HIST + DEC
ZC_S = CONV_HIST + SEQ + CONV_HIST
YC = ZC - CONV_HIST
ZP = POOL_HIST + SEQ + POOL_HIST + DEC
ZP_S = POOL_HIST + SEQ + POOL_HIST
PO = ZP - POOL_HIST
PO_S = SEQ + POOL_HIST
PO_A = 296

R_CW, R_PS, R_SC, R_SP, R_ALL = 0, 9, 11, 17, 47

BLK = 64
MAX_J = T // BLK - 1
NOV = 2 * T // BLK
NCOL = NE + NOV
NSLOT = 3
PRE = [(NE - s + NSLOT - 1) // NSLOT for s in range(NSLOT)]
ROUNDS = NE // NSLOT
OUTSIDE = 4096

CONSTS = {}
_at = 0
for _name, _n in (("ident", P), ("causal", P), ("strict", P), ("iota_pos", BLK),
                  ("w4", NG), ("w8", EPG), ("vals", 4 * NT), ("two", NT), ("base", 1), ("invw", 2),
                  ("rc15", 2 * POOL_HIST), ("expert", NE), ("past", MAX_J), ("ovnum", NOV)):
    CONSTS[_name] = (_at, _at + _n)
    _at += _n
NCONST = _at


def constant_tile():
    import numpy as np
    c = np.zeros((P, NCONST), np.float32)
    p = np.arange(P)

    def put(name, value):
        a, b = CONSTS[name]
        c[:, a:b] = value

    put("ident", np.eye(P))
    put("causal", p[:, None] <= p[None, :])
    put("strict", p[:, None] < p[None, :])
    put("iota_pos", np.arange(BLK))
    put("w4", np.arange(NG, 0, -1))
    put("w8", np.arange(EPG, 0, -1))
    vals = np.zeros((P, NT, 2, 2))
    for t in range(NT):
        for k in range(2):
            vals[:TOK[t], t, k, 0] = 2 * (t * P + p[:TOK[t]]) - OUTSIDE
            vals[:TOK[t], t, k, 1] = 2 * (2 * (t * P + p[:TOK[t]]) + k) - OUTSIDE
    put("vals", vals.reshape(P, -1))
    put("two", np.array([[2.0 * (i < TOK[t]) for t in range(NT)] for i in range(P)]))
    put("base", OUTSIDE + (p >= 64)[:, None])
    win = np.array([[2, 8], [4, 16]])[(p >= 64).astype(int)]
    put("invw", 1.0 / win)
    put("rc15", (1.0 / np.minimum(win[:, :, None], np.arange(1, POOL_HIST + 1))).reshape(P, -1))
    put("expert", np.arange(NE))
    put("past", BLK * np.arange(1, MAX_J + 1))
    put("ovnum", np.arange(NOV))
    return c


PIECE = 32


def build(nc, x_prompt, x_sample, state_conv, state_pool, norm1_g, w_in, conv_w, pool_w, pool_scale,
          sgu_w, sgu_b, w_out, norm2_g, rc_w, rc_b, rf_w, rf_b, w_gate, w_up, w_down, final_g, consts,
          y_prompt, y_sample, new_conv_prompt, new_pool_prompt, new_conv_sample, new_pool_sample,
          new_sgu_v):
    hn2_rows = nc.dram_tensor("hn2_rows", [2 * T, D // 2], F32, kind="Internal").ap()
    y_rows = nc.dram_tensor("y_rows", [4 * T, D // 2], F32, kind="Internal").ap()

    W1_BYTES, WD_BYTES = 2 * KD * F * 4, (F // P) * D * 4
    SLOT_BYTES = W1_BYTES + WD_BYTES
    first = (nc.sbuf_base + 31) // 32 * 32
    slot_at = [first + s * SLOT_BYTES for s in range(NSLOT + 1)]
    where = {}

    def region(start, end):
        at = [start]

        def place(name, shape, dt=F32):
            n = 2 if dt == BF16 else 4
            for x in shape[1:]:
                n *= x
            t = nc.alloc_sbuf_tensor_at(name, shape, dt, offset=at[0])
            where[name] = at[0]
            at[0] += (n + 31) // 32 * 32
            where["end"] = at[0]
            assert at[0] <= end, (name, at[0] - end)
            return t
        return place

    w1, wd = [], []
    for s in range(NSLOT):
        slot = region(slot_at[(s + 2) % 3], slot_at[(s + 2) % 3 + 1])
        w1.append(slot(f"w1_{s}", [P, 2, KD, F]))
        wd.append(slot(f"wd_{s}", [P, F // P, D]))

    early = region(slot_at[0], slot_at[3])
    wi, wi_lo = {}, {}
    WIDTH = {"v": D_SGU, "p": D_POOL, "u": D_SGU, "c": D_CONV, "h": D_CONV, "b": D_CONV}

    def columns(g):
        wi[g] = early(f"wi_{g}", [P, KD, WIDTH[g]])
        wi_lo[g] = nc.alloc_sbuf_tensor_at(f"wi_lo_{g}", [P, KD, WIDTH[g]], F32R, offset=where[f"wi_{g}"])

    for g in "vpuch":
        columns(g)
    v_hi_at = where["end"]
    early("gap", [P, 2, D])
    columns("b")
    hT_hi = early("hT_hi", [P, KD, T], F32R)
    wi_hi = early("wi_hi", [P, 3, KD, P], F32R)
    hT_lo = early("hT_lo", [P, KD, T], F32R)
    zc = early("zc", [P, 3, ZC])
    v_sb = early("v_sb", [P, NT, D_SGU])
    gated = early("gated", [P, T])
    pool_wbd = early("pool_wbd", [P, 2, P])
    wmT = early("wmT", [P, HEADS, P])
    convst = early("convst", [P, 3, 4])
    poolst = early("poolst", [P, 2, 2 * POOL_HIST])
    wi_hi_v = nc.alloc_sbuf_tensor_at("wi_hi_v", [P, KD, D_SGU], F32R, offset=v_hi_at)
    wo = nc.alloc_sbuf_tensor_at("wo", [P, 2, KD, D // 2], F32, offset=where["wi_v"])
    wo_lo = nc.alloc_sbuf_tensor_at("wo_lo", [P, 2, KD, D // 2], F32R, offset=where["wi_v"])
    wo_hi = nc.alloc_sbuf_tensor_at("wo_hi", [P, 2, KD, D // 2], F32R, offset=where["wi_c"])
    assert where["wi_c"] - where["wi_v"] == KD * D * 4 == where["wi_b"] - where["wi_c"]
    assert where["wi_b"] == where["w1_2"] + KD * F * 4
    assert KD // 2 * F * 4 + KD * P * 4 <= where["hT_hi"] - where["wi_b"]
    assert where["wi_v"] == where["w1_1"] and where["wi_c"] == where["wd_1"]
    mix_hi = nc.alloc_sbuf_tensor_at("mix_hi", [P, KD, T], F32R, offset=where["hT_hi"])
    assert where["hT_hi"] + KD * T * 4 <= slot_at[2]
    late = region(where["v_sb"], where["gated"])
    conv_rows = late("conv_rows", [P, D_CONV])
    pool_rows = late("pool_rows", [P, D_POOL])

    rest = region(slot_at[3], nc.sbuf_usable_end)
    x_sb = rest("x_sb", [P, NT, D])
    mixT = rest("mixT", [P, KD, T])
    mixT_lo = nc.alloc_sbuf_tensor_at("mixT_lo", [P, KD, T], F32R, offset=where["mixT"])
    zp = rest("zp", [P, 2, ZP])
    win_a = rest("win_a", [P, ZP])
    win_b = rest("win_b", [P, ZP])
    pooled = rest("pooled", [P, 2, PO])
    pool_end = where["end"]
    cst = rest("cst", [P, NCONST])
    gain = rest("gain", [P, D])
    rw = rest("rw", [P, KD, NG + NE])
    rbias = rest("rbias", [P, NG + NE])
    bfull = rest("bfull", [P, 3, P])
    prmT = rest("prmT", [P, R_ALL])
    small = rest("small", [P, 30, NT])
    gates = rest("gates", [P, NT, 2])
    L = rest("L", [P, NT, NG + NE])
    idx = rest("idx", [P, 2, NCOL], I32)
    ovexp = rest("ovexp", [P, NOV], I32)
    nov = rest("nov", [P, 1], I32)
    idc_x = rest("idc_x", [P, NSLOT], I32)
    idc_y = rest("idc_y", [P, NSLOT], I32)
    pre = region(where["mixT"], where["zp"])
    hstage = pre("hstage", [P, 2, D])
    sguw = pre("sguw", [P, HEADS, P])
    prm = pre("prm", [P, P])
    post = region(where["mixT"], where["zp"])
    xT = post("xT", [P, KD // 2, P])
    silu_g = post("silu_g", [P, F // 2])
    hexp = post("hexp", [P, F // 2])
    hexT = post("hexT", [P, 2, P])
    t_g = post("t_g", [P, NT, NG])
    e_g = post("e_g", [P, NT, NG])
    oh_g = post("oh_g", [P, NT, NG])
    t_ge = post("t_ge", [P, NT, NG, EPG])
    sel = post("sel", [P, NT, EPG])
    t_e = post("t_e", [P, NT, EPG])
    oh_k = post("oh_k", [P, NT, 2, EPG])
    oh_both = post("oh_both", [P, NT, EPG])
    vals = post("vals", [P, NT, 2, 2])
    memb = post("memb", [P, NT, 2, NE])
    Mb = post("Mb", [P, NT + 1, NE], BF16)
    onehot_v = post("onehot_v", [P, NT * 2, 2, NE], F32R)
    t_m = post("t_m", [P, NT, 2, NE])
    t_j = post("t_j", [P, NE, MAX_J])
    nblk = post("nblk", [P, 3, NE])
    t_o = post("t_o", [P, NOV, NE])
    at_k = post("at_k", [P, 5, NT * 2])
    t_k = post("t_k", [P, NT * 2, MAX_J])
    p1 = region(where["zp"], pool_end)
    cbuf = p1("cbuf", [P, 3, T])
    junk = nc.alloc_sbuf_tensor_at("junk", [P, D], F32, offset=where["win_a"])
    yconv = p1("yconv", [P, 3, YC])
    p2 = region(where["zp"], pool_end)
    hn2p = p2("hn2p", [P, 2, D])
    hn2T = [p2("hn2T_0", [P, KD, P]),
            nc.alloc_sbuf_tensor_at("hn2T_1", [P, KD, P], F32, offset=where["hT_hi"] - KD * P * 4)]
    tri_b = p2("tri_b", [P, P], BF16)
    ones_b = p2("ones_b", [P, P], BF16)
    p3 = region(where["zp"], pool_end)
    xg = p3("xg", [P, NSLOT, D // 2])
    ybuf = p3("ybuf", [P, NSLOT, D // 2])
    p4 = region(where["ybuf"], pool_end)
    onehot_s = p4("onehot_s", [P, NT * 2, 2, BLK], F32R)
    onehot_c = p4("onehot_c", [P, NT * 2, NOV])
    onehot_p = p4("onehot_p", [P, NT * 2, 2, NOV], F32R)
    mark_1, mark_2, second_first, swap = (small[:, c, :] for c in range(24, 28))
    rows = vals[:].rearrange("p t k c -> p (t k) c")
    choices = memb[:].rearrange("p t k e -> p (t k) e")
    p5 = region(slot_at[1], slot_at[2])
    yfin = [p5(f"yfin{i}", [P, 2 * D]) for i in range(NT)]

    ps = nc.alloc_psum_tensor("ps", [P, 8, 512], F32)

    def con(name):
        a, b = CONSTS[name]
        return cst[:, a:b]

    ident = con("ident")

    sem = nc.alloc_semaphore
    consts_in, params_in, sguw_in, sgub_in = sem("consts_in"), sem("params_in"), sem("sguw_in"), sem("sgub_in")
    x_in = [sem(f"x_in{j}") for j in range(NT)]
    wi_in = {g: sem(f"wi_in_{g}") for g in "puchb"}
    wi_in_v = [sem(f"wi_in_v{i}") for i in range(4)]
    V_ROWS = [slice(i * KD // 4, (i + 1) * KD // 4) for i in range(4)]
    v_hi, v_lo, wi_hi_ready, wi_lo_ready = sem("v_hi"), sem("v_lo"), sem("wi_hi_ready"), sem("wi_lo_ready")
    hT_hi_ready, hT_lo_ready = sem("hT_hi_ready"), sem("hT_lo_ready")
    wo_hi_ready, wo_lo_ready, mix_hi_ready, mix_lo_ready = (sem("wo_hi_ready"), sem("wo_lo_ready"),
                                                            sem("mix_hi_ready"), sem("mix_lo_ready"))
    g1_in = sem("g1_in")
    poolw_in, g2_in, router_in, wo_in, gf_in = (sem("poolw_in"), sem("g2_in"), sem("router_in"),
                                                sem("wo_in"), sem("gf_in"))
    zeroed, tri_ready = sem("zeroed"), sem("tri_ready")
    prm_ps, prm_ready, wm_ps, wm_ready = sem("prm_ps"), sem("prm_ready"), sem("wm_ps"), sem("wm_ready")
    hist_ready = sem("hist_ready")
    warm, std1, h_ready, hT_ps = sem("warm"), sem("std1"), sem("h_ready"), sem("hT_ps")
    v_ps, v_ready = sem("v_ps"), sem("v_ready")
    proj_ps, evac_act, evac_dve = sem("proj_ps"), sem("evac_act"), sem("evac_dve")
    sgu_ps, sgu_read, sgu_ready = sem("sgu_ps"), sem("sgu_read"), sem("sgu_ready")
    pooled_ready, pool_ps, pool_ready = sem("pooled_ready"), sem("pool_ps"), sem("pool_ready")
    st_ready, st_ps, st_rows, st_out = sem("st_ready"), sem("st_ps"), sem("st_rows"), sem("st_out")
    wo_ps, x2_ready, std2, hn2_ready = sem("wo_ps"), sem("x2_ready"), sem("std2"), sem("hn2_ready")
    hn2_out = [sem("hn2_out0"), sem("hn2_out1")]
    hn2T_ps, hn2T_ready, L_ps, L_ready = sem("hn2T_ps"), sem("hn2T_ready"), sem("L_ps"), sem("L_ready")
    gdiff_ready, gexp_ready, kdiff_ready, kexp_ready = (sem("gdiff_ready"), sem("gexp_ready"),
                                                        sem("kdiff_ready"), sem("kexp_ready"))
    memb_ready, pos_ps, onehot_ready, idx_ps, idx_ready, nov_ready = (
        sem("memb_ready"), sem("pos_ps"), sem("onehot_ready"), sem("idx_ps"), sem("idx_ready"),
        sem("nov_ready"))
    xg_zero = sem("xg_zero")
    w1_in = [[sem(f"w1_in{s}_{half}") for half in range(2)] for s in range(NSLOT)]
    wd_in = [sem(f"wd_in{s}") for s in range(NSLOT)]
    xg_in = [sem(f"xg_in{s}") for s in range(NSLOT)]
    y_out = [sem(f"y_out{s}") for s in range(NSLOT)]
    idc_ready = sem("idc_ready")
    idc_seen = sem("idc_seen")
    xT_ps, xT_ready, gu_ps, silu_ready, h_exp = (sem("xT_ps"), sem("xT_ready"), sem("gu_ps"),
                                                 sem("silu_ready"), sem("h_exp"))
    order_ready = sem("order_ready")
    half_ps, picks_ready, rows_step, rows_ready = (sem("half_ps"), sem("picks_ready"), sem("rows_step"),
                                                   sem("rows_ready"))
    hexT_ps, hexT_ready, dn_ps, y_ready = sem("hexT_ps"), sem("hexT_ready"), sem("dn_ps"), sem("y_ready")
    yfin_in = [[sem(f"yfin_in{k}_{j}") for j in range(NT)] for k in range(2)]
    acc_ready, std3, out_ready, y_done = sem("acc_ready"), sem("std3"), sem("out_ready"), sem("y_done")
    dve_step, act_step = sem("dve_step"), sem("act_step")

    CHUNKS = [("p", 0), ("p", 1)] + [(g, q) for g in "uchb" for q in range(3)]
    NCH = len(CHUNKS)
    MIX_ORDER = (6, 7, 5, 3, 4, 0, 1, 2)
    WO_PIECES = ((1, 4, 6, 5), (1, 6, 8, 5), (0, 0, 2, 8), (0, 2, 4, 8), (0, 4, 6, 8), (0, 6, 8, 11), (1, 0, 2, 11),
                 (1, 2, 4, 11))
    WO_FIRST = 6
    nth = {ch: n for n, ch in enumerate(CHUNKS)}
    ON_ACT = "puc"

    WARM_START = (3, 1)
    WARM = (3, 2, 4, 1)

    def evacuated(eng, n):
        mine = CHUNKS[n][0] in ON_ACT
        count = sum((g in ON_ACT) == mine for g, _ in CHUNKS[:n + 1])
        eng.wait_ge(evac_act if mine else evac_dve, count)

    def pair(n):
        return 2 * (n % 2)

    halves = ((0, 0, HT), (1, HT, T))
    segs = ((0, 0, HT, 0, 0), (1, 0, SEQ - HT, HT, 0), (1, SEQ - HT, HT, SEQ, 1))

    def experts(eng, body, last=ROUNDS):
        for s in range(NSLOT):
            body(0, s)
        with eng.Fori(1, last) as i:
            for s in range(NSLOT):
                body(i, s)
        for n in range(NSLOT * last, NE):
            body(n // NSLOT, n % NSLOT)

    def blocks_past(eng, body):
        eng.wait_ge(nov_ready, 1)
        count = eng.value_load(nov[0:1, 0:1], min_val=0, max_val=NOV)
        with eng.If(count > 0):
            with eng.Fori(0, count) as b:
                body(b)
        return count

    with nc.Block() as block:

        @block.sync
        def _(sp):
            x_rows = [x_prompt[0, j * P:(j + 1) * P, :] for j in range(4)] + [x_sample[0]]
            wi_v = w_in[0].rearrange("(k p) n -> p k n", p=P)

            def load_wi_v(i):
                sp.dma_start(wi["v"][:, V_ROWS[i], :], wi_v[:, V_ROWS[i], COL_V:COL_V + D_SGU]).then_inc(wi_in_v[i], 16)

            def load_wi(g, a, n):
                sp.dma_start(wi[g][:], wi_v[:, :, a:a + n]).then_inc(wi_in[g], 16)

            def load_x(j):
                sp.dma_start(x_sb[0:TOK[j], j, :], x_rows[j]).then_inc(x_in[j], 16)

            load_x(0)
            sp.dma_start(gain[:], norm1_g[0:1, :].broadcast_to([P, D])).then_inc(g1_in, 16)
            sp.dma_start(cst[:], consts).then_inc(consts_in, 16)
            load_wi_v(0)
            load_wi_v(1)
            load_x(1)
            load_wi_v(2)
            load_wi_v(3)
            for j in range(2, NT):
                load_x(j)
            sp.dma_start(sguw[:], sgu_w[0].rearrange("h i j -> i h j")).then_inc(sguw_in, 16)
            sp.dma_start(prm[R_CW:R_PS, :], conv_w[0].rearrange("k (q p) -> (k q) p", p=P)).then_inc(params_in, 16)
            sp.dma_start(prm[R_PS:R_SC, :], pool_scale[0].rearrange("(q p) -> q p", p=P)).then_inc(params_in, 16)
            sp.dma_start(prm[R_SC:R_SP, :], state_conv[0, 0].rearrange("r (q p) -> (r q) p", p=P)).then_inc(params_in, 16)
            sp.dma_start(prm[R_SP:R_ALL, :], state_pool[0, 0].rearrange("r (q p) -> (r q) p", p=P)).then_inc(params_in, 16)
            load_wi("p", COL_P, D_POOL)
            load_wi("u", COL_U, D_SGU)
            for head in range(HEADS):
                for q in range(3):
                    a, b = max(head * HEAD_DIM, q * P), min((head + 1) * HEAD_DIM, (q + 1) * P)
                    if a < b:
                        sp.dma_start(bfull[a - q * P:b - q * P, q, :],
                                     sgu_b[0, head:head + 1, :].broadcast_to([b - a, P])).then_inc(sgub_in, 16)
            sp.wait_ge(zeroed, 2)
            for g in range(4):
                r, a = g // 2, 64 * (g % 2)
                sp.dma_start(pool_wbd[a:a + 64, r, a:a + 64], pool_w[0, g]).then_inc(poolw_in, 16)
            load_wi("c", COL_C, D_CONV)
            load_wi("h", COL_H, D_CONV)
            sp.wait_ge(h_ready, NT)
            sp.dma_start(gain[:], norm2_g[0:1, :].broadcast_to([P, D])).then_inc(g2_in, 16)
            sp.dma_start(rw[:, :, 0:NG], rc_w[0].rearrange("(p k) e -> p k e", p=P)).then_inc(router_in, 16)
            sp.dma_start(rw[:, :, NG:NG + NE], rf_w[0].rearrange("(p k) e -> p k e", p=P)).then_inc(router_in, 16)
            sp.dma_start(rbias[:, 0:NG], rc_b[0:1, :].broadcast_to([P, NG])).then_inc(router_in, 16)
            sp.dma_start(rbias[:, NG:NG + NE], rf_b[0:1, :].broadcast_to([P, NE])).then_inc(router_in, 16)
            sp.wait_ge(v_ps, NT)
            load_wi("b", COL_B, D_CONV)
            sp.wait_ge(v_ready, NT)
            sp.dma_start(new_sgu_v[0, 0], v_sb[0:DEC, NT - 1, :]).then_inc(st_out, 16)

            gate_v = w_gate[0].rearrange("e (p k) f -> p e (k f)", p=P)
            up_v = w_up[0].rearrange("e (p k) f -> p e (k f)", p=P)
            down_v = w_down[0].rearrange("e (c p) d -> p e c d", p=P)

            def load_gate_up(e, s, parts=(0, 1), halves=(0, 1)):
                for half in halves:
                    k = slice(half * (KD // 2), (half + 1) * (KD // 2))
                    for a in parts:
                        sp.dma_start(w1[s][:, a:a + 1, k, :].rearrange("p a k f -> p a (k f)"),
                                     (gate_v, up_v)[a][:, bass.ds(e, 1), k.start * F:k.stop * F]
                                     ).then_inc(w1_in[s][half], 16)

            def load_down(e, s, halves=(0, 1)):
                for half in halves:
                    c = slice(half * (F // P // 2), (half + 1) * (F // P // 2))
                    sp.dma_start(wd[s][:, c, :].rearrange("p (o c) d -> p o c d", o=1),
                                 down_v[:, bass.ds(e, 1), c, :]).then_inc(wd_in[s], 16)

            sp.wait_ge(proj_ps, nth["u", 2] + 1)
            for half in range(2):
                sp.dma_start(wo[:, half, :, :], w_out[0, :, half * (D // 2):(half + 1) * (D // 2)].rearrange(
                    "(k p) n -> p k n", p=P)).then_inc(wo_in, 16)
            sp.wait_ge(st_rows, 2)
            sp.dma_start(new_conv_prompt[0, 0], conv_rows[0:2, :]).then_inc(st_out, 16)
            sp.dma_start(new_conv_sample[0, 0], conv_rows[2:4, :]).then_inc(st_out, 16)
            sp.dma_start(new_pool_prompt[0, 0], pool_rows[0:POOL_HIST, :]).then_inc(st_out, 16)
            sp.dma_start(new_pool_sample[0, 0], pool_rows[POOL_HIST:2 * POOL_HIST, :]).then_inc(st_out, 16)
            sp.wait_ge(st_out, 80)
            sp.wait_ge(proj_ps, NCH)
            sp.wait_ge(evac_dve, 6)
            load_gate_up(0, 0)
            load_down(0, 0)
            load_gate_up(2, 2, parts=(1,), halves=(0,))
            sp.wait_ge(wo_ps, NT)
            load_gate_up(1, 1, parts=(0,))
            load_down(1, 1)
            hn2_v = hn2_rows.rearrange("(t h) d -> t (h d)", h=2)
            for j in range(NT):
                sp.wait_ge(hn2_ready, j + 1)
                sp.dma_start(hn2_v[j * P:j * P + TOK[j], :], hn2p[0:TOK[j], j % 2, :]).then_inc(hn2_out[j % 2], 16)
                if j == NT - 1:
                    sp.dma_start(gain[:], final_g.rearrange("(o d) -> o d", o=1).broadcast_to([P, D])).then_inc(gf_in, 16)
            sp.wait_ge(wo_ps, 2 * NT)
            load_gate_up(1, 1, parts=(1,))
            load_gate_up(2, 2, parts=(0,), halves=(0,))
            load_gate_up(2, 2, parts=(0,), halves=(1,))
            sp.wait_ge(L_ps, NT)
            load_gate_up(2, 2, parts=(1,), halves=(1,))
            sp.wait_ge(idc_seen, 2)
            load_down(2, 2)

            def refill(i, s):
                sp.wait_ge(half_ps, NSLOT * (i - 1) + s + 1)
                load_gate_up(NSLOT * i + s, s, halves=(0,))
                sp.wait_ge(gu_ps, NSLOT * (i - 1) + s + 1)
                load_gate_up(NSLOT * i + s, s, halves=(1,))
                sp.wait_ge(dn_ps, NSLOT * (i - 1) + s + 1)
                load_down(NSLOT * i + s, s)

            with sp.Fori(1, ROUNDS) as i:
                for s in range(NSLOT):
                    refill(i, s)
            for n in range(NSLOT * ROUNDS, NE):
                refill(n // NSLOT, n % NSLOT)

            def block_past(b):
                sp.wait_ge(dn_ps, NE + b)
                e = sp.value_load(ovexp[0:1, bass.ds(b, 1)], min_val=0, max_val=NE - 1)
                load_gate_up(e, 0)
                load_down(e, 0)

            count = blocks_past(sp, block_past)
            y_v = y_rows.rearrange("(t r) d -> t (r d)", r=4)
            sp.wait_ge(y_out[0], 16 * (PRE[0] + count))
            sp.wait_ge(y_out[1], 16 * (PRE[1] - 1))
            sp.wait_ge(y_out[2], 16 * PRE[2])
            for k in range(2):
                if k == 1:
                    sp.wait_ge(y_out[(NE - 1) % NSLOT], 16 * PRE[(NE - 1) % NSLOT])
                for j in range(NT):
                    if k == 0 and j == 2:
                        sp.wait_ge(idc_seen, 2 * NE)
                    sp.dma_start(yfin[j][0:TOK[j], k * D:(k + 1) * D],
                                 y_v[j * P:j * P + TOK[j], k * D:(k + 1) * D]).then_inc(yfin_in[k][j], 16)
            y_tiles = [y_prompt[0, j * P:(j + 1) * P, :] for j in range(4)] + [y_sample[0]]
            for j in range(NT):
                sp.wait_ge(out_ready, j + 1)
                sp.dma_start(y_tiles[j], yfin[j][0:TOK[j], D:2 * D]).then_inc(y_done, 16)
            sp.wait_ge(y_done, 16 * NT)

        @block.gpsimd
        def _(pool):
            nc.gpsimd.memset(gated[:], 0.0).then_inc(zeroed, 1)
            nc.gpsimd.memset(pool_wbd[:], 0.0).then_inc(zeroed, 1)
            nc.gpsimd.memset(zc[:], 0.0).then_inc(zeroed, 1)
            nc.gpsimd.memset(zp[:], 0.0).then_inc(zeroed, 1)
            evacuated(pool, nth["p", 1])
            nc.gpsimd.tensor_copy(poolst[:, :, 0:POOL_HIST], zp[:, :, SEQ:SEQ + POOL_HIST])
            nc.gpsimd.tensor_copy(poolst[:, :, POOL_HIST:], zp[:, :, ZP - POOL_HIST:ZP]).then_inc(st_ready, 1)
            evacuated(pool, nth["h", 2])
            nc.gpsimd.tensor_copy(convst[:, :, 0:2], zc[:, :, SEQ:SEQ + CONV_HIST])
            nc.gpsimd.tensor_copy(convst[:, :, 2:4], zc[:, :, ZC - CONV_HIST:ZC]).then_inc(st_ready, 1)

            pool.wait_ge(hn2T_ps, 2 * NT)
            for par in range(2):
                pool.wait_ge(hn2_out[par], 16 * len(range(par, NT, 2)))
            nc.gpsimd.memset(xg[:, 0:1, :], 0.0)
            pool.wait_ge(L_ps, NT)
            nc.gpsimd.memset(xg[:, 1:NSLOT, :], 0.0).then_inc(xg_zero, 1)
            pool.wait_ge(xg_zero, 1)

            pool.wait_ge(order_ready, 1)
            nc.gpsimd.tensor_tensor(swap, second_first, con("two"), ALU.mult).then_inc(rows_step, 1)
            pool.wait_ge(rows_step, 1)
            nc.gpsimd.tensor_tensor(vals[:, :, 0, 1], vals[:, :, 0, 1], swap, ALU.add)
            nc.gpsimd.tensor_tensor(vals[:, :, 1, 1], vals[:, :, 1, 1], swap, ALU.subtract).then_inc(rows_step, 1)
            pool.wait_ge(rows_step, 2)
            pool.wait_ge(picks_ready, 1)
            nc.gpsimd.tensor_tensor(onehot_v[:], choices[:, :, None, :].broadcast_to([P, NT * 2, 2, NE]),
                                    rows[:, :, :, None].broadcast_to([P, NT * 2, 2, NE]), ALU.mult).then_inc(rows_ready, 1)
            pool.wait_ge(idx_ready, 1)

            def gather(col, s, done):
                nc.gpsimd.tensor_copy(idc_x[:, s:s + 1], idx[:, 0, bass.ds(col, 1)]).then_inc(idc_ready, 1)
                pool.wait_ge(idc_ready, done)
                pool.sem_inc(idc_seen, 1)
                nc.gpsimd.indirect_dma_start(
                    out=xg[:, s, :], out_offset=None, in_=hn2_rows,
                    in_offset=bass.IndirectOffsetOnAxis(ap=idc_x[:, s:s + 1], axis=0),
                    bounds_check=2 * T - 1, oob_is_err=False).then_inc(xg_in[s], 16)

            def scatter(col, s, n, done, i):
                if not (isinstance(i, int) and i == 0):
                    pool.wait_ge(y_out[s], 16 * i)
                nc.gpsimd.tensor_copy(idc_y[:, s:s + 1], idx[:, 1, bass.ds(col, 1)]).then_inc(idc_ready, 1)
                pool.wait_ge(idc_ready, done)
                pool.wait_ge(y_ready, n + 1)
                pool.sem_inc(idc_seen, 1)
                nc.gpsimd.indirect_dma_start(
                    out=y_rows, out_offset=bass.IndirectOffsetOnAxis(ap=idc_y[:, s:s + 1], axis=0),
                    in_=ybuf[:, s, :], in_offset=None,
                    bounds_check=4 * T - 1, oob_is_err=False).then_inc(y_out[s], 16)

            for s in range(NSLOT):
                gather(s, s, s + 1)

            def turn(i, s):
                n = NSLOT * i + s
                pool.wait_ge(xT_ps, n + 1)
                gather(n + NSLOT, s, NSLOT + 2 * n + 1)
                scatter(n, s, n, NSLOT + 2 * n + 2, i)

            for s in range(NSLOT):
                turn(0, s)
            with pool.Fori(1, ROUNDS - 1) as i:
                for s in range(NSLOT):
                    turn(i, s)
            for n in range(NSLOT * (ROUNDS - 1), NE - NSLOT):
                turn(n // NSLOT, n % NSLOT)
            copies = NSLOT + 2 * (NE - NSLOT)
            for n in range(NE - NSLOT, NE):
                copies += 1
                scatter(n, n % NSLOT, n, copies, n // NSLOT)

            pool.wait_ge(idx_ready, 2)

            def block_past(b):
                pool.wait_ge(y_ready, NE + b)
                gather(NE + b, 0, copies + 2 * b + 1)
                scatter(NE + b, 0, NE + b, copies + 2 * b + 2, PRE[0] + b)

            blocks_past(pool, block_past)
        @block.scalar
        def _(act):
            steps = [0]

            def link(ins):
                steps[0] += 1
                ins.then_inc(act_step, 1)
                act.wait_ge(act_step, steps[0])

            def std(j, col, done):
                n = TOK[j]
                out = hn2p[:, j % 2, :] if col == 3 else junk_of[col]
                link(nc.scalar.activation(out[0:n, :], x_sb[0:n, j, :], ACT.Square,
                                          accum_out=small[0:n, col, j:j + 1]))
                nc.scalar.activation(small[0:n, col + 1, j:j + 1], small[0:n, col, j:j + 1], ACT.Sqrt,
                                     bias=small[0:n, 28, 0:1], scale=1.0 / D).then_inc(done, 1)

            junk_of = {0: junk, 6: xg[:].rearrange("p s d -> p (s d)")[:, 0:D]}

            def round_hT(j, halves=(0, 1)):
                n, t = TOK[j], slice(j * P, j * P + TOK[j])
                for h in halves:
                    act.wait_ge(hT_ps, 2 * j + h + 1)
                    nc.scalar.copy(hT_hi[:, 4 * h:4 * h + 4, t],
                                   ps[:, pair(j) + h, 0:4 * n].rearrange("p (k t) -> p k t", k=4)).then_inc(hT_hi_ready, 1)

            def take_v(j):
                act.wait_ge(v_ps, j + 1)
                nc.scalar.copy(v_sb[0:TOK[j], j, :], ps[0:TOK[j], 4 + j % 2, 0:D_SGU]).then_inc(v_ready, 1)

            def round_wi(n):
                if n >= NCH:
                    return
                g, q = CHUNKS[n]
                if q == 0:
                    act.wait_ge(wi_in[g], 16)
                if n >= 3:
                    act.wait_ge(proj_ps, n - 2)
                nc.scalar.copy(wi_hi[:, n % 3, :, :], wi[g][:, :, q * P:(q + 1) * P]).then_inc(wi_hi_ready, 1)

            def first_std(j):
                act.wait_ge(x_in[j], 16)
                std(j, 0, std1)

            act.wait_ge(warm, 1)
            nc.scalar.activation(small[:, 22, :], small[:, 23, :], ACT.Sqrt)
            first_std(0)

            def round_wi_v(i):
                act.wait_ge(wi_in_v[i], 16)
                nc.scalar.copy(wi_hi_v[:, V_ROWS[i], :], wi["v"][:, V_ROWS[i], :]).then_inc(v_hi, 1)

            round_hT(0, (0,))
            round_wi_v(0)
            round_hT(0, (1,))
            round_wi_v(1)
            first_std(1)
            round_wi_v(2)
            round_wi_v(3)
            first_std(2)
            round_hT(1)
            first_std(3)
            round_hT(2)
            first_std(4)
            round_hT(3)
            take_v(0)
            round_hT(4)
            round_wi(0)
            take_v(1)
            round_wi(1)
            for j in range(2, NT):
                take_v(j)

            def take(g, q):
                n = nth[g, q]
                act.wait_ge(proj_ps, n + 1)
                b0 = pair(n)
                if g == "p":
                    for bank, a, b, t0, smp in segs:
                        at = POOL_HIST + t0 + smp * POOL_HIST
                        last = nc.scalar.copy(zp[:, q, at:at + b - a], ps[:, b0 + bank, a:b])
                elif g == "u":
                    for bank, a, b in halves:
                        last = nc.scalar.copy(mixT[:, 5 + q, a:b], ps[:, b0 + bank, 0:b - a])
                else:
                    for bank, a, b in halves:
                        last = nc.scalar.copy(cbuf[:, q, a:b], ps[:, b0 + bank, 0:b - a])
                last.then_inc(evac_act, 1)

            def take_pool(r):
                act.wait_ge(pool_ps, r + 1)
                scale = prmT[:, R_PS + r:R_PS + r + 1]
                nc.scalar.activation(mixT[:, 3 + r, 0:PO_A], ps[:, 6, 0:PO_A], ACT.Copy, scale=scale)
                nc.scalar.activation(mixT[:, 3 + r, PO_A:SEQ], ps[:, 7, 0:SEQ - PO_A], ACT.Copy, scale=scale)
                nc.scalar.activation(mixT[:, 3 + r, SEQ:T], ps[:, 7, PO_S - PO_A:PO - PO_A], ACT.Copy,
                                     scale=scale).then_inc(pool_ready, 1)

            act.wait_ge(hT_ps, 2 * NT)
            act.wait_ge(wm_ps, 1)
            act.wait_ge(prm_ready, 1)
            act.wait_ge(hist_ready, 1)
            wo_at = [0]

            def round_wo(n, most=2):
                while most and wo_at[0] < len(WO_PIECES) and WO_PIECES[wo_at[0]][3] <= n:
                    half, a, b, after = WO_PIECES[wo_at[0]]
                    act.wait_ge(wo_in, 32)
                    act.wait_ge(proj_ps, after)
                    nc.scalar.copy(wo_hi[:, half, a:b, :], wo[:, half, a:b, :]).then_inc(wo_hi_ready, 1)
                    wo_at[0] += 1
                    most -= 1

            for n, (g, q) in enumerate(CHUNKS):
                round_wi(n + 2)
                if n == nth["c", 0]:
                    take_pool(0)
                    act.wait_ge(st_ready, 1)
                    act.wait_ge(pooled_ready, 2)
                if g in ON_ACT:
                    take(g, q)
                if n == nth["c", 1]:
                    take_pool(1)
                if n >= nth["h", 0]:
                    round_wo(n)
            round_wo(NCH, KD)
            for k in MIX_ORDER:
                if k == MIX_ORDER[0]:
                    act.wait_ge(proj_ps, NCH)
                    act.wait_ge(sgu_ready, 3)
                if k == 0:
                    act.wait_ge(evac_dve, 6)
                nc.scalar.copy(mix_hi[:, k, :], mixT[:, k, :]).then_inc(mix_hi_ready, 1)
            act.wait_ge(st_ps, 1)
            act.wait_ge(st_out, 16)
            nc.scalar.copy(conv_rows[0:4, :], ps[0:4, 7, 0:D_CONV]).then_inc(st_rows, 1)
            nc.scalar.copy(pool_rows[0:2 * POOL_HIST, :], ps[0:2 * POOL_HIST, 6, 0:D_POOL]).then_inc(st_rows, 1)

            def take_hn2T(j):
                n = TOK[j]
                if j >= 2:
                    act.wait_ge(L_ps, j - 1)
                for h in range(2):
                    act.wait_ge(hn2T_ps, 2 * j + h + 1)
                    nc.scalar.copy(hn2T[j % 2][:, 4 * h:4 * h + 4, 0:n],
                                   ps[:, 4 + h, 0:4 * n].rearrange("p (k t) -> p k t", k=4)).then_inc(hn2T_ready, 1)

            for j in range(NT):
                act.wait_ge(x2_ready, NT + j + 1)
                if j >= 2:
                    act.wait_ge(hn2_out[j % 2], 16 * (j // 2))
                    act.wait_ge(hn2T_ps, 2 * (j - 1))
                std(j, 3, std2)
                if j >= 1:
                    take_hn2T(j - 1)
            take_hn2T(NT - 1)

            act.wait_ge(gdiff_ready, 1)
            nc.scalar.activation(e_g[:], t_g[:], ACT.Exp).then_inc(gexp_ready, 1)
            act.wait_ge(kdiff_ready, 1)
            nc.scalar.activation(small[:, 15, :], small[:, 14, :], ACT.Exp).then_inc(kexp_ready, 1)

            def work(n, s, i):
                act.wait_ge(gu_ps, n + 1)
                nc.scalar.activation(silu_g[:], ps[:, 1, 0:F // 2], ACT.Silu).then_inc(silu_ready, 1)
                act.wait_ge(dn_ps, n + 1)
                if not (isinstance(i, int) and i == 0):
                    act.wait_ge(y_out[s], 16 * i)
                nc.scalar.copy(ybuf[:, s, :], ps[:, 3, :]).then_inc(y_ready, 1)

            experts(act, lambda i, s: work(NSLOT * i + s, s, i))
            blocks_past(act, lambda b: work(NE + b, 0, PRE[0] + b))

            nc.scalar.activation(small[:, 22, :], small[:, 23, :], ACT.Sqrt)
            for j in range(NT):
                act.wait_ge(acc_ready, j + 1)
                std(j, 6, std3)

        @block.vector
        def _(dve):
            steps = [0]

            def link(ins):
                steps[0] += 1
                ins.then_inc(dve_step, 1)
                dve.wait_ge(dve_step, steps[0])

            def tt(out, a, b, op):
                return nc.vector.tensor_tensor(out, a, b, op)

            def ts(out, a, s1, s2, op0, op1=ALU.bypass):
                return nc.vector.tensor_scalar(out, a, s1, s2, op0, op1)

            def stt(out, a, s, b, op0, op1):
                return nc.vector.scalar_tensor_tensor(out, a, s, b, op0, op1)

            def normalise(j):
                n = TOK[j]
                dve.wait_ge(std1, j + 1)
                link(nc.vector.reciprocal(small[0:n, 2, j:j + 1], small[0:n, 1, j:j + 1]))
                if j >= 2:
                    dve.wait_ge(hT_ps, 2 * (j - 1))
                stt(hstage[0:n, j % 2, :], x_sb[0:n, j, :], small[0:n, 2, j:j + 1], gain[0:n, :], ALU.mult,
                    ALU.mult).then_inc(h_ready, 1)

            def rest_hT(j, halves=(0, 1)):
                n, t = TOK[j], slice(j * P, j * P + TOK[j])
                for h in halves:
                    dve.wait_ge(hT_hi_ready, 2 * j + h + 1)
                    k = slice(4 * h, 4 * h + 4)
                    tt(hT_lo[:, k, t], ps[:, pair(j) + h, 0:4 * n].rearrange("p (k t) -> p k t", k=4),
                       hT_hi[:, k, t].bitcast(F32), ALU.subtract).then_inc(hT_lo_ready, 1)

            def rest_wi(n):
                if n >= NCH:
                    return
                g, q = CHUNKS[n]
                dve.wait_ge(wi_hi_ready, n + 1)
                c = slice(q * P, (q + 1) * P)
                tt(wi_lo[g][:, :, c], wi[g][:, :, c], wi_hi[:, n % 3, :, :].bitcast(F32),
                   ALU.subtract).then_inc(wi_lo_ready, 1)

            nc.vector.memset(small[:, 28, :], EPS)
            nc.vector.memset(small[:, 22:24, :], 1.0).then_inc(warm, 1)
            dve.wait_ge(g1_in, 16)
            normalise(0)

            def rest_wi_v(i):
                dve.wait_ge(v_hi, i + 1)
                tt(wi_lo["v"][:, V_ROWS[i], :], wi["v"][:, V_ROWS[i], :], wi_hi_v[:, V_ROWS[i], :].bitcast(F32),
                   ALU.subtract).then_inc(v_lo, 1)

            rest_hT(0, (0,))
            rest_wi_v(0)
            rest_hT(0, (1,))
            rest_wi_v(1)
            normalise(1)
            rest_wi_v(2)
            rest_wi_v(3)
            normalise(2)
            rest_hT(1)
            normalise(3)
            rest_hT(2)
            normalise(4)
            rest_hT(3)
            rest_hT(4)
            rest_wi(0)
            dve.wait_ge(prm_ps, 1)
            nc.vector.tensor_copy(prmT[:], ps[:, 7, 0:R_ALL]).then_inc(prm_ready, 1)
            dve.wait_ge(wm_ps, 1)
            dve.wait_ge(consts_in, 16)
            tt(wmT[:], ps[:, 6, :].rearrange("p (h i) -> p h i", h=HEADS),
               con("causal")[:, None, :].broadcast_to([P, HEADS, P]), ALU.mult).then_inc(wm_ready, 1)
            dve.wait_ge(prm_ready, 1)
            dve.wait_ge(zeroed, 4)
            nc.vector.tensor_copy(zc[:, :, ZC_S - CONV_HIST:ZC_S],
                                  prmT[:, R_SC:R_SP].rearrange("p (r q) -> p q r", q=3))
            nc.vector.tensor_copy(zp[:, :, ZP_S - POOL_HIST:ZP_S],
                                  prmT[:, R_SP:R_ALL].rearrange("p (r q) -> p q r", q=2)).then_inc(hist_ready, 1)
            rest_wi(1)
            dve.wait_ge(hist_ready, 1)

            def pool(r):
                evacuated(dve, nth["p", r])
                z = zp[:, r, :]
                link(tt(win_a[:, 1:ZP], z[:, 1:ZP], z[:, 0:ZP - 1], ALU.add))
                low, up = slice(0, 64), slice(64, P)
                if r == 0:
                    link(tt(win_b[up, 3:ZP], win_a[up, 3:ZP], win_a[up, 1:ZP - 2], ALU.add))
                else:
                    link(tt(win_b[:, 3:ZP], win_a[:, 3:ZP], win_a[:, 1:ZP - 2], ALU.add))
                    link(tt(win_a[:, 7:ZP], win_b[:, 7:ZP], win_b[:, 3:ZP - 4], ALU.add))
                    link(tt(win_b[up, 15:ZP], win_a[up, 15:ZP], win_a[up, 7:ZP - 8], ALU.add))
                rc = con("rc15").rearrange("p (r i) -> p r i", r=2)
                for part, win in ((low, win_a), (up, win_b)):
                    link(stt(pooled[part, r, :], win[part, POOL_HIST:ZP], con("invw")[part, r:r + 1],
                             z[part, POOL_HIST:ZP], ALU.mult, ALU.subtract))
                    link(tt(win[part, POOL_HIST:2 * POOL_HIST], win[part, POOL_HIST:2 * POOL_HIST],
                            rc[part, r, :], ALU.mult))
                    last = tt(pooled[part, r, 0:POOL_HIST], win[part, POOL_HIST:2 * POOL_HIST],
                              z[part, POOL_HIST:2 * POOL_HIST], ALU.subtract)
                    if part == low:
                        link(last)
                last.then_inc(pooled_ready, 1)

            def sgu(q):
                dve.wait_ge(sgu_ps, q + 1)
                if q == 0:
                    dve.wait_ge(sgub_in, 96)
                tt(gated[:, 0:SEQ].rearrange("p (n i) -> p n i", n=4),
                   ps[:, 4 + q % 2, :].rearrange("p (n i) -> p n i", n=4),
                   bfull[:, q, None, :].broadcast_to([P, 4, P]), ALU.add)
                tt(gated[:, SEQ:T], ps[:, 6 + q % 2, 0:DEC], bfull[:, q, 0:DEC], ALU.add).then_inc(sgu_read, 1)
                dve.wait_ge(sgu_read, q + 1)
                evacuated(dve, nth["u", q])
                tt(mixT[:, 5 + q, :], mixT[:, 5 + q, :], gated[:], ALU.mult).then_inc(sgu_ready, 1)
                dve.wait_ge(sgu_ready, q + 1)

            def take_h(q):
                n = nth["h", q]
                dve.wait_ge(proj_ps, n + 1)
                evacuated(dve, nth["c", q])
                for bank, a, b, t0, smp in segs:
                    at = CONV_HIST + t0 + smp * CONV_HIST
                    last = tt(zc[:, q, at:at + b - a], ps[:, pair(n) + bank, a:b], cbuf[:, q, t0:t0 + b - a], ALU.mult)
                last.then_inc(evac_dve, 1)
                dve.wait_ge(evac_dve, q + 1)
                z = zc[:, q, :]
                w = [prmT[:, R_CW + 3 * k + q:R_CW + 3 * k + q + 1] for k in range(3)]
                y = yconv[:, q, :]
                link(ts(y, z[:, 0:YC], w[0], None, ALU.mult))
                link(stt(y, z[:, 1:YC + 1], w[1], y, ALU.mult, ALU.add))
                link(stt(y, z[:, 2:YC + 2], w[2], y, ALU.mult, ALU.add))

            def take_b(q):
                n = nth["b", q]
                dve.wait_ge(proj_ps, n + 1)
                for bank, a, b, t0, smp in segs:
                    at = t0 + smp * CONV_HIST
                    last = tt(mixT[:, q, t0:t0 + b - a], ps[:, pair(n) + bank, a:b], yconv[:, q, at:at + b - a], ALU.mult)
                last.then_inc(evac_dve, 1)

            wo_at = [0]

            def rest_wo(upto):
                while wo_at[0] < upto:
                    half, a, b, _ = WO_PIECES[wo_at[0]]
                    dve.wait_ge(wo_hi_ready, wo_at[0] + 1)
                    tt(wo_lo[:, half, a:b, :], wo[:, half, a:b, :], wo_hi[:, half, a:b, :].bitcast(F32),
                       ALU.subtract).then_inc(wo_lo_ready, 1)
                    wo_at[0] += 1

            for n, (g, q) in enumerate(CHUNKS):
                rest_wi(n + 2)
                if g == "p":
                    pool(q)
                elif g == "u":
                    sgu(q)
                elif g == "h":
                    if q == 0:
                        dve.wait_ge(pool_ps, 2)
                    take_h(q)
                elif g == "b":
                    if q < 2:
                        take_b(q)
                if n >= nth["h", 1]:
                    rest_wo(min(KD - 1, 2 * (n - nth["h", 0])))
            rest_wo(KD)

            def rest_mix(i):
                dve.wait_ge(mix_hi_ready, i + 1)
                k = MIX_ORDER[i]
                tt(mixT_lo[:, k, :], mixT[:, k, :], mix_hi[:, k, :].bitcast(F32), ALU.subtract).then_inc(mix_lo_ready, 1)

            rest_mix(0)
            rest_mix(1)
            take_b(2)
            for i in range(2, KD):
                rest_mix(i)

            def take_L(j):
                n = TOK[j]
                dve.wait_ge(L_ps, j + 1)
                tt(L[0:n, j, :], ps[0:n, 6 + j % 2, 0:NG + NE], rbias[0:n, :], ALU.add).then_inc(L_ready, 1)

            link(nc.vector.memset(L[:], 0.0))
            dve.wait_ge(pool_ps, 2)
            nc.vector.memset(ones_b[:], 1.0)
            nc.vector.tensor_copy(tri_b[:], con("strict")).then_inc(tri_ready, 1)
            dve.wait_ge(g2_in, 16)
            dve.wait_ge(router_in, 64)

            def add_mix(half, j):
                n, c = TOK[j], slice(half * (D // 2), (half + 1) * (D // 2))
                turn = half * NT + j
                dve.wait_ge(wo_ps, turn + 1)
                tt(x_sb[0:n, j, c], ps[0:n, turn % 4, :], x_sb[0:n, j, c], ALU.add).then_inc(x2_ready, 1)

            for j in range(NT):
                add_mix(0, j)
            for j in range(NT):
                n = TOK[j]
                add_mix(1, j)
                dve.wait_ge(std2, j + 1)
                link(nc.vector.reciprocal(small[0:n, 5, j:j + 1], small[0:n, 4, j:j + 1]))
                if j >= 2:
                    dve.wait_ge(hn2_out[j % 2], 16 * (j // 2))
                    dve.wait_ge(hn2T_ps, 2 * (j - 1))
                stt(hn2p[0:n, j % 2, :].rearrange("t (k p) -> t k p", k=KD),
                    x_sb[0:n, j, :].rearrange("t (p k) -> t k p", k=KD), small[0:n, 5, j:j + 1],
                    gain[0:n, :].rearrange("t (p k) -> t k p", k=KD), ALU.mult, ALU.mult).then_inc(hn2_ready, 1)
                if j >= 2:
                    take_L(j - 2)
            take_L(NT - 2)
            take_L(NT - 1)
            dve.wait_ge(wo_ps, 2 * NT)
            nc.vector.memset(Mb[:, NT, :], 0.0)
            nc.vector.tensor_copy(vals[:].rearrange("p t k c -> p (t k c)"), con("vals"))
            dve.wait_ge(L_ready, NT)

            mx, v1, v2, mark = (small[:, c, :] for c in (9, 10, 11, 12))
            psel, kdiff, kexp, w_hi = (small[:, c, :] for c in (13, 14, 15, 16))

            def over(x, shape):
                return x.broadcast_to(shape)

            def first_greatest(out, x, top, weights, tmp, n, mark):
                link(tt(tmp, x, over(top[:, :, None], [P, NT, n]), ALU.is_equal))
                link(tt(tmp, tmp, over(weights[:, None, :], [P, NT, n]), ALU.mult))
                link(nc.vector.tensor_reduce(mark, tmp, AX.X, ALU.max))
                link(tt(out, tmp, over(mark[:, :, None], [P, NT, n]), ALU.is_equal))

            lc, lf = L[:, :, 0:NG], L[:, :, NG:].rearrange("p t (g e) -> p t g e", g=NG)
            link(nc.vector.tensor_reduce(mx, lc, AX.X, ALU.max))
            tt(t_g[:], lc, over(mx[:, :, None], [P, NT, NG]), ALU.subtract).then_inc(gdiff_ready, 1)
            dve.wait_ge(gdiff_ready, 1)
            link(stt(oh_g[:], t_g[:], 0.0, over(con("w4")[:, None, :], [P, NT, NG]), ALU.is_ge, ALU.mult))
            link(nc.vector.tensor_reduce(mark, oh_g[:], AX.X, ALU.max))
            link(tt(oh_g[:], oh_g[:], over(mark[:, :, None], [P, NT, NG]), ALU.is_equal))
            link(tt(t_ge[:], lf, over(oh_g[:, :, :, None], [P, NT, NG, EPG]), ALU.mult))
            link(nc.vector.tensor_reduce(sel[:], t_ge[:].rearrange("p t g e -> p t e g"), AX.X, ALU.add))
            link(nc.vector.tensor_reduce(v1, sel[:], AX.X, ALU.max))
            first_greatest(oh_k[:, :, 0, :], sel[:], v1, con("w8"), t_e[:], EPG, mark_1)
            link(stt(sel[:], oh_k[:, :, 0, :], -3.0e38, sel[:], ALU.mult, ALU.add))
            link(nc.vector.tensor_reduce(v2, sel[:], AX.X, ALU.max))
            tt(kdiff, v2, v1, ALU.subtract).then_inc(kdiff_ready, 1)
            first_greatest(oh_k[:, :, 1, :], sel[:], v2, con("w8"), t_e[:], EPG, mark_2)
            link(tt(oh_both[:], oh_k[:, :, 0, :], oh_k[:, :, 1, :], ALU.add))
            tt(Mb[:, 0:NT, :].rearrange("p t (g e) -> p t g e", g=NG), over(oh_g[:, :, :, None], [P, NT, NG, EPG]),
               over(oh_both[:, :, None, :], [P, NT, NG, EPG]), ALU.mult).then_inc(memb_ready, 1)
            tt(second_first, mark_1, mark_2, ALU.is_lt).then_inc(order_ready, 1)
            for k in range(2):
                last = tt(memb[:, :, k, :].rearrange("p t (g e) -> p t g e", g=NG),
                          over(oh_g[:, :, :, None], [P, NT, NG, EPG]),
                          over(oh_k[:, :, k, None, :], [P, NT, NG, EPG]), ALU.mult)
            last.then_inc(picks_ready, 1)
            place, past, j_k, col, dead = (at_k[:, c, :] for c in range(5))
            before = ps[:, 7, 0:NT * NE].rearrange("p (t e) -> p t e", e=NE)
            in_all = ps[:, 7, NT * NE:(NT + 1) * NE]
            t_c = t_m[:].rearrange("p t k e -> p (t k) e")
            dve.wait_ge(pos_ps, 1)
            dve.wait_ge(picks_ready, 1)
            link(tt(t_m[:], memb[:], over(before[:, :, None, :], [P, NT, 2, NE]), ALU.mult))
            link(nc.vector.tensor_reduce(place, t_c, AX.X, ALU.add))
            dve.wait_ge(hn2_out[0], 48)
            dve.wait_ge(hn2_out[1], 32)
            dve.wait_ge(L_ps, NT)
            positions = over(con("iota_pos")[:, None, None, :], [P, NT * 2, 2, BLK])
            for i in range(2):
                c = slice(i * NT, (i + 1) * NT)
                tt(onehot_s[:, c], positions[:, c], over(place[:, c, None, None], [P, NT, 2, BLK]),
                   ALU.is_equal).then_inc(onehot_ready, 1)
            dve.wait_ge(idx_ps, 1)
            ts(idx[:, :, 0:NE], ps[:, 6, 0:2 * NE].rearrange("p (c n) -> p c n", c=2), con("base"), None,
               ALU.add).then_inc(idx_ready, 1)

            def blocks_past_first():
                link(tt(t_j[:], over(in_all[:, :, None], [P, NE, MAX_J]), over(con("past")[:, None, :], [P, NE, MAX_J]),
                        ALU.is_gt))
                link(nc.vector.tensor_reduce(nblk[:, 0, :], t_j[:], AX.X, ALU.add))
                link(nc.vector.tensor_tensor_scan(nblk[:, 1, :], nblk[:, 0, :], nblk[:, 0, :], 0.0, ALU.add, ALU.bypass))
                link(tt(nblk[:, 2, :], nblk[:, 1, :], nblk[:, 0, :], ALU.subtract))
                link(tt(t_m[:], memb[:], over(nblk[:, 2, None, None, :], [P, NT, 2, NE]), ALU.mult))
                nc.vector.tensor_reduce(past, t_c, AX.X, ALU.add)
                link(tt(t_k[:], over(place[:, :, None], [P, NT * 2, MAX_J]),
                        over(con("past")[:, None, :], [P, NT * 2, MAX_J]), ALU.is_ge))
                link(nc.vector.tensor_reduce(j_k, t_k[:], AX.X, ALU.add))
                ts(dead, j_k, 0.0, -1000.0, ALU.is_equal, ALU.mult)
                link(stt(col, j_k, -1.0, past, ALU.add, ALU.add))
                link(stt(place, j_k, -float(BLK), place, ALU.mult, ALU.add))
                link(tt(col, col, dead, ALU.add))
                tt(onehot_s[:], positions, over(place[:, :, None, None], [P, NT * 2, 2, BLK]), ALU.is_equal)
                link(tt(onehot_c[:], over(con("ovnum")[:, None, :], [P, NT * 2, NOV]),
                        over(col[:, :, None], [P, NT * 2, NOV]), ALU.is_equal))
                tt(onehot_p[:], over(onehot_c[:, :, None, :], [P, NT * 2, 2, NOV]),
                   over(rows[:, :, :, None], [P, NT * 2, 2, NOV]), ALU.mult).then_inc(onehot_ready, 2)
                link(tt(t_o[:], over(nblk[:, 1, None, :], [P, NOV, NE]), over(con("ovnum")[:, :, None], [P, NOV, NE]),
                        ALU.is_le))
                numbers = small[:, 17:21, :].rearrange("p a b -> p (a b)")[:, 0:NOV]
                link(nc.vector.tensor_reduce(numbers, t_o[:], AX.X, ALU.add))
                nc.vector.tensor_copy(ovexp[:], numbers)
                nc.vector.tensor_copy(nov[:], nblk[:, 1, NE - 1:NE]).then_inc(nov_ready, 1)

            def rows_past_first():
                dve.wait_ge(idx_ps, 2)
                ts(idx[:, :, NE:], ps[:, 5, 0:2 * NOV].rearrange("p (c n) -> p c n", c=2), con("base"), None,
                   ALU.add).then_inc(idx_ready, 1)

            def take_gates():
                dve.wait_ge(gexp_ready, 1)
                link(nc.vector.tensor_reduce(psel, e_g[:], AX.X, ALU.add))
                link(nc.vector.reciprocal(psel, psel))
                dve.wait_ge(kexp_ready, 1)
                link(ts(w_hi, kexp, 1.0, None, ALU.add))
                link(nc.vector.reciprocal(w_hi, w_hi))
                link(tt(w_hi, psel, w_hi, ALU.mult))
                link(tt(kexp, w_hi, kexp, ALU.mult))
                link(ts(swap, second_first, -1.0, 1.0, ALU.mult, ALU.add))
                for k, (a, b) in enumerate(((w_hi, kexp), (kexp, w_hi))):
                    link(tt(psel, swap, a, ALU.mult))
                    link(tt(gates[:, :, k], second_first, b, ALU.mult))
                    link(tt(gates[:, :, k], gates[:, :, k], psel, ALU.add))

            def work(n):
                dve.wait_ge(xT_ps, n + 1)
                nc.vector.tensor_copy(xT[:].rearrange("p c s -> p (c s)"), ps[:, 0, :]).then_inc(xT_ready, 1)

            def work_h(n):
                dve.wait_ge(silu_ready, n + 1)
                tt(hexp[:], silu_g[:], ps[:, 1, F // 2:F], ALU.mult).then_inc(h_exp, 1)

            def work_hT(n):
                dve.wait_ge(hexT_ps, n + 1)
                nc.vector.tensor_copy(hexT[:].rearrange("p c s -> p (c s)"), ps[:, 2, 0:2 * P]).then_inc(hexT_ready, 1)

            work(0)
            blocks_past_first()

            def turn(i, s, more=True):
                n = NSLOT * i + s
                work_h(n)
                if more:
                    work(n + 1)
                work_hT(n)
                if isinstance(n, int) and n == 0:
                    rows_past_first()
                    take_gates()

            experts(dve, lambda i, s: turn(i, s, not (isinstance(i, int) and NSLOT * i + s == NE - 1)))

            def block_past(b):
                work(NE + b)
                work_h(NE + b)
                work_hT(NE + b)

            blocks_past(dve, block_past)

            def finish(j):
                n = TOK[j]
                dve.wait_ge(std3, j + 1)
                link(nc.vector.reciprocal(small[0:n, 8, j:j + 1], small[0:n, 7, j:j + 1]))
                stt(yfin[j][0:n, D:2 * D], x_sb[0:n, j, :], small[0:n, 8, j:j + 1], gain[0:n, :], ALU.mult,
                    ALU.mult).then_inc(out_ready, 1)

            for j in range(NT):
                n = TOK[j]
                dve.wait_ge(yfin_in[0][j], 16)
                last = stt(x_sb[0:n, j, :], yfin[j][0:n, 0:D], gates[0:n, j, 0:1], x_sb[0:n, j, :], ALU.mult, ALU.add)
            link(last)
            dve.wait_ge(gf_in, 16)
            for j in range(NT):
                n = TOK[j]
                dve.wait_ge(yfin_in[1][j], 16)
                stt(x_sb[0:n, j, :], yfin[j][0:n, D:2 * D], gates[0:n, j, 1:2], x_sb[0:n, j, :], ALU.mult,
                    ALU.add).then_inc(acc_ready, 1)
                if j:
                    finish(j - 1)
            finish(NT - 1)

        @block.tensor
        def _(pe):
            mm = nc.tensor.matmul

            def stay_warm(count, x):
                for _ in range(count):
                    mm(ps[:, 4, :], x[:, 0:P], x[:, 0:512], start=True, stop=True)

            pe.wait_ge(zeroed, 1)
            stay_warm(WARM_START[0], gated)
            pe.wait_ge(consts_in, 16)

            def transpose_h(j):
                n = TOK[j]
                pe.wait_ge(h_ready, j + 1)
                if j >= 2:
                    pe.wait_ge(hT_lo_ready, 2 * (j - 1))
                for h in range(2):
                    for k in range(4):
                        last = nc.tensor.transpose(ps[:, pair(j) + h, k * n:(k + 1) * n],
                                                   hstage[0:n, j % 2, (4 * h + k) * P:(4 * h + k + 1) * P],
                                                   ident[0:n, 0:n])
                    last.then_inc(hT_ps, 1)

            def product_v(j, halves=(0, 1)):
                n = TOK[j]
                if j >= 2:
                    pe.wait_ge(v_ready, j - 1)
                out, t = ps[0:n, 4 + j % 2, 0:D_SGU], slice(j * P, j * P + n)
                for half in halves:
                    pe.wait_ge(hT_lo_ready, 2 * j + half + 1)
                    for k in range(half * (KD // 2), (half + 1) * (KD // 2)):
                        if j == 0 and k % 2 == 0:
                            pe.wait_ge(v_lo, k // 2 + 1)
                        mm(out, hT_hi[:, k, t], wi_hi_v[:, k, :], start=(k == 0), stop=False)
                        mm(out, hT_hi[:, k, t], wi_lo["v"][:, k, :], start=False, stop=False)
                        last = mm(out, hT_lo[:, k, t], wi_hi_v[:, k, :], start=False, stop=(k == KD - 1))
                if 1 in halves:
                    last.then_inc(v_ps, 1)

            transpose_h(0)
            stay_warm(WARM_START[1], gated)
            product_v(0, (0,))
            transpose_h(1)
            product_v(0, (1,))
            transpose_h(2)
            product_v(1)
            transpose_h(3)
            transpose_h(4)
            pe.wait_ge(params_in, 64)
            nc.tensor.transpose(ps[:, 7, 0:R_ALL], prm[0:R_ALL, :], ident[0:R_ALL, 0:R_ALL]).then_inc(prm_ps, 1)
            pe.wait_ge(sguw_in, 16)
            for head in range(HEADS):
                last = nc.tensor.transpose(ps[:, 6, head * P:(head + 1) * P], sguw[:, head, :], ident)
            last.then_inc(wm_ps, 1)
            for j in range(2, NT):
                product_v(j)

            def product(g, q):
                n = nth[g, q]
                pe.wait_ge(wi_lo_ready, n + 1)
                if n == 0:
                    pe.wait_ge(hT_lo_ready, 2 * NT)
                if n >= 2:
                    evacuated(pe, n - 2)
                for k in range(KD):
                    w_hi, w_lo = wi_hi[:, n % 3, k, :], wi_lo[g][:, k, q * P:(q + 1) * P]
                    for part, (w, h) in enumerate(((w_hi, hT_hi), (w_hi, hT_lo), (w_lo, hT_hi))):
                        for bank, a, b in halves:
                            last = mm(ps[:, pair(n) + bank, 0:b - a], w, h[:, k, a:b], start=(k + part == 0),
                                      stop=(k == KD - 1 and part == 2))
                last.then_inc(proj_ps, 1)

            def mix_positions(q):
                if q == 0:
                    pe.wait_ge(v_ready, NT)
                    pe.wait_ge(wm_ready, 1)
                    pe.wait_ge(prm_ready, 1)
                if q >= 2:
                    pe.wait_ge(sgu_read, q - 1)
                for t in range(NT):
                    n = TOK[t]
                    for at in range(0, P, PIECE):
                        ch = q * P + at
                        out = ps[at:at + PIECE, 4 + q % 2, t * P:(t + 1) * P] if t < 4 else \
                            ps[at:at + PIECE, 6 + q % 2, 0:DEC]
                        last = mm(out, v_sb[0:n, t, ch:ch + PIECE], wmT[0:n, ch // HEAD_DIM, 0:n], start=True,
                                  stop=True)
                last.then_inc(sgu_ps, 1)

            def mix_pooled(r):
                pe.wait_ge(pooled_ready, r + 1)
                if r == 0:
                    pe.wait_ge(poolw_in, 64)
                    pe.wait_ge(sgu_read, 3)
                else:
                    pe.wait_ge(pool_ready, r)
                mm(ps[:, 6, 0:PO_A], pool_wbd[:, r, :], pooled[:, r, 0:PO_A], start=True, stop=True)
                mm(ps[:, 7, 0:PO - PO_A], pool_wbd[:, r, :], pooled[:, r, PO_A:PO], start=True,
                   stop=True).then_inc(pool_ps, 1)

            product("p", 0)
            product("p", 1)
            for q in range(3):
                product("u", q)
                mix_positions(q)
            for n in range(nth["c", 0], NCH):
                product(*CHUNKS[n])
                if n == nth["c", 0]:
                    mix_pooled(0)
                if n == nth["c", 1]:
                    mix_pooled(1)
            pe.wait_ge(st_ready, 2)
            pe.wait_ge(pool_ready, 2)
            for q in range(3):
                nc.tensor.transpose(ps[0:4, 7, q * P:(q + 1) * P], convst[:, q, :], ident)
            for r in range(2):
                last = nc.tensor.transpose(ps[0:2 * POOL_HIST, 6, r * P:(r + 1) * P], poolst[:, r, :], ident)
            last.then_inc(st_ps, 1)

            def output(half, *tiles):
                turns = [half * NT + j for j in tiles]
                if tiles[0] == 0:
                    pe.wait_ge(wo_lo_ready, len(WO_PIECES) if half else WO_FIRST)
                if turns[0] == 2:
                    evacuated(pe, NCH - 1)
                if turns[-1] >= 4:
                    pe.wait_ge(x2_ready, turns[-1] - 3)
                for i, k in enumerate(MIX_ORDER):
                    if turns[0] == 0:
                        pe.wait_ge(mix_lo_ready, i + 1)
                        if i == 0:
                            evacuated(pe, NCH - 2)
                    for turn, j in zip(turns, tiles):
                        n, t = TOK[j], slice(j * P, j * P + TOK[j])
                        for part, (m, w) in enumerate(((mix_hi, wo_hi), (mix_hi, wo_lo), (mixT_lo, wo_hi))):
                            last = mm(ps[0:n, turn % 4, :], m[:, k, t], w[:, half, k, :], start=(i + part == 0),
                                      stop=(i == KD - 1 and part == 2))
                        if i == KD - 1:
                            last.then_inc(wo_ps, 1)

            def transpose_hn2(j):
                n = TOK[j]
                pe.wait_ge(hn2_ready, j + 1)
                for h in range(2):
                    if j:
                        pe.wait_ge(hn2T_ready, 2 * (j - 1) + h + 1)
                    for k in range(4):
                        last = nc.tensor.transpose(ps[:, 4 + h, k * n:(k + 1) * n],
                                                   hn2p[0:n, j % 2, (4 * h + k) * P:(4 * h + k + 1) * P],
                                                   ident[0:n, 0:n])
                    last.then_inc(hn2T_ps, 1)

            def logits(j):
                n = TOK[j]
                pe.wait_ge(hn2T_ready, 2 * (j + 1))
                if j == 0:
                    pe.wait_ge(router_in, 64)
                    pe.wait_ge(st_rows, 2)
                if j >= 2:
                    pe.wait_ge(L_ready, j - 1)
                for k in range(KD):
                    last = mm(ps[0:n, 6 + j % 2, 0:NG + NE], hn2T[j % 2][:, k, 0:n], rw[:, k, :], start=(k == 0),
                              stop=(k == KD - 1))
                last.then_inc(L_ps, 1)

            output(0, 0, 1)
            for j in range(2, NT):
                output(0, j)
            output(1, 0)
            output(1, 1)
            transpose_hn2(0)
            output(1, 2)
            logits(0)
            transpose_hn2(1)
            output(1, 3)
            logits(1)
            transpose_hn2(2)
            output(1, 4)
            transpose_hn2(3)
            logits(2)
            transpose_hn2(4)
            logits(3)
            logits(4)

            stay_warm(WARM[0], x_sb[:, 0, :])
            pe.wait_ge(memb_ready, 1)
            pe.wait_ge(tri_ready, 1)
            mm(ps[:, 7, 0:(NT + 1) * NE], tri_b[:], Mb[:].rearrange("p t e -> p (t e)"), start=True, stop=False)
            for j in range(NT):
                n = TOK[j]
                last = mm(ps[:, 7, (j + 1) * NE:(NT + 1) * NE], ones_b[0:n, :],
                          Mb[0:n, j, None, :].broadcast_to([n, NT - j, NE]), start=False, stop=(j == NT - 1))
            last.then_inc(pos_ps, 1)

            def rows_of_places(bank, columns, done):
                for i in range(2 * NT):
                    if i % NT == 0:
                        pe.wait_ge(onehot_ready, 2 * (done - 1) + i // NT + 1)
                    last = mm(ps[:, bank, 0:columns.shape[2] * columns.shape[3]],
                              onehot_s[:, i, :, :].rearrange("p h b -> p (h b)"),
                              columns[:, i, :, :].rearrange("p c n -> p (c n)"), start=(i == 0), stop=(i == 2 * NT - 1))
                last.then_inc(idx_ps, 1)

            stay_warm(WARM[1], x_sb[:, 0, :])
            pe.wait_ge(rows_ready, 1)
            rows_of_places(6, onehot_v, 1)
            stay_warm(WARM[2], x_sb[:, 0, :])

            def transpose_x(s, uses):
                pe.wait_ge(xg_in[s], 16 * uses)
                for c in range(KD // 2):
                    last = nc.tensor.transpose(ps[:, 0, c * P:(c + 1) * P], xg[:, s, c * P:(c + 1) * P], ident)
                last.then_inc(xT_ps, 1)

            def gate_up(n, s, uses):
                pe.wait_ge(xT_ready, n + 1)
                for k in range(KD):
                    if k % (KD // 2) == 0:
                        pe.wait_ge(w1_in[s][k // (KD // 2)], 32 * uses)
                    lhs = xT[:, k % 4, 64 * (k // 4):64 * (k // 4) + 64]
                    for h in range(2):
                        last = mm(ps[64 * h:64 * h + 64, 1, :], lhs, w1[s][:, :, k, h * (F // 2):(h + 1) * (F // 2)],
                                  start=(k == 0), stop=(k == KD - 1))
                    if k == KD // 2 - 1:
                        last.then_inc(half_ps, 1)
                last.then_inc(gu_ps, 1)

            def transpose_act(n):
                pe.wait_ge(h_exp, n + 1)
                for c in range(2):
                    last = nc.tensor.transpose(ps[:, 2, c * P:(c + 1) * P], hexp[:, c * P:(c + 1) * P], ident)
                last.then_inc(hexT_ps, 1)

            def down(n, s, uses):
                pe.wait_ge(hexT_ready, n + 1)
                pe.wait_ge(wd_in[s], 32 * uses)
                if not (isinstance(n, int) and n == 0):
                    pe.wait_ge(y_ready, n)
                for c in range(F // P):
                    lhs = hexT[:, c % 2, 64 * (c // 2):64 * (c // 2) + 64]
                    for h in range(2):
                        last = mm(ps[64 * h:64 * h + 64, 3, :], lhs, wd[s][:, c, h * 512:(h + 1) * 512],
                                  start=(c == 0), stop=(c == F // P - 1))
                last.then_inc(dn_ps, 1)

            transpose_x(0, 1)
            stay_warm(WARM[3], x_sb[:, 0, :])

            def turn(i, s, more=True):
                n = NSLOT * i + s
                gate_up(n, s, i + 1)
                if more:
                    transpose_x((s + 1) % NSLOT, i + 1 + (s + 1) // NSLOT)
                transpose_act(n)
                if isinstance(n, int) and n == 0:
                    rows_of_places(5, onehot_p, 2)
                down(n, s, i + 1)

            experts(pe, lambda i, s: turn(i, s, not (isinstance(i, int) and NSLOT * i + s == NE - 1)))

            def block_past(b):
                transpose_x(0, PRE[0] + b + 1)
                gate_up(NE + b, 0, PRE[0] + b + 1)
                transpose_act(NE + b)
                down(NE + b, 0, PRE[0] + b + 1)

            blocks_past(pe, block_past)


_INS = ["x_prompt", "x_sample", "state_conv", "state_pool", "norm1_g", "w_in", "conv_w", "pool_w", "pool_scale",
        "sgu_w", "sgu_b", "w_out", "norm2_g", "router_coarse_w", "router_coarse_b", "router_fine_w",
        "router_fine_b", "moe_w_gate", "moe_w_up", "moe_w_down", "final_norm_g"]
_OUTS = [(1, SEQ, D), (1, DEC, D), (1, 1, CONV_HIST, D_CONV), (1, 1, POOL_HIST, D_POOL),
         (1, 1, CONV_HIST, D_CONV), (1, 1, POOL_HIST, D_POOL), (1, 1, DEC, D_SGU)]


def kernel(**inputs):
    import numpy as np
    import concourse.bacc as bacc
    from concourse.bass_utils import run_bass_kernel_spmd

    nc = bacc.Bacc("TRN2", target_bir_lowering=False, num_devices=1)
    arrays, args = {}, []
    for name in _INS:
        a = np.ascontiguousarray(inputs[name])
        arrays[f"in_{name}"] = a
        args.append(nc.dram_tensor(f"in_{name}", a.shape, mybir.dt.from_np(a.dtype), kind="ExternalInput").ap())
    arrays["in_constants"] = constant_tile()
    args.append(nc.dram_tensor("in_constants", (P, NCONST), F32, kind="ExternalInput").ap())
    for i, shape in enumerate(_OUTS):
        args.append(nc.dram_tensor(f"out_{i}", shape, F32, kind="ExternalOutput").ap())
    build(nc, *args)
    r = run_bass_kernel_spmd(nc, [arrays], core_ids=[0])
    return tuple(r.results[0][f"out_{i}"] for i in range(len(_OUTS)))
```
